# Optimizing a Trainium2 kernel written in Bass

```python
import jax, jax.numpy as jnp
from jax import lax
import numpy as np

D_MODEL = 1024
BATCH = 1
SEQ = 2048
DEPTH = 1
DEC_BATCH = 8
DEC_SEQ = 16
PAST_LEN = 1024

CHUNK = 64
HG_HEADS = 4
HG_DK = 128
HG_DV = 128
HG_WIDTH = HG_HEADS * HG_DV
RW_HEADS = 8
RW_HEAD = 64
RW_WIDTH = RW_HEADS * RW_HEAD
MIX_WIDTH = HG_WIDTH + RW_WIDTH
HG_PROJ = 2 * HG_HEADS * HG_DK + 2 * HG_WIDTH
RW_PROJ = 3 * RW_WIDTH
IN_WIDTH = HG_PROJ + RW_PROJ
RW_DECAY_LORA = 64
RW_ICLR_LORA = 64
RW_VRES_LORA = 32
RW_GATE_LORA = 128
N_GROUPS = 4
EXPERTS_PER_GROUP = 8
N_EXPERTS = N_GROUPS * EXPERTS_PER_GROUP
TOP_K = 2
D_EXPERT = 512
MOE_BLOCK = 128
NORM_EPS = 1e-6
RW_GN_EPS = 64e-5

kernel_name = 'hybrid_hgrn2_rwkv7_hmoe_stream_step'

def rmsnorm(x, w):
    xf = x.astype(jnp.float32)
    y = xf * lax.rsqrt(jnp.mean(xf * xf, axis=-1, keepdims=True) + NORM_EPS)
    return (y * w.astype(jnp.float32)).astype(x.dtype)

def shift_right(seq, first):
    return jnp.concatenate([first[:, None, :], seq[:, :-1, :]], axis=1)

def hgrn2_chunked(q, k, v, logf, S0):
    B, L, H, DK = q.shape
    DV = v.shape[-1]
    C = min(L, CHUNK)
    n = L // C

    def blocks(t):
        return t.reshape(B, n, C, H, t.shape[-1]).transpose(1, 0, 3, 2, 4)

    causal = jnp.tril(jnp.ones((C, C), dtype=bool))[:, :, None]

    def step(S, blk):
        qc, kc, vc, gc = blk
        b = jnp.cumsum(gc, axis=2)
        diff = b[:, :, :, None, :] - b[:, :, None, :, :]
        decay = jnp.exp(jnp.where(causal, diff, -jnp.inf))
        scores = jnp.einsum('bhtd,bhsd,bhtsd->bhts', qc, kc, decay)
        o = (jnp.einsum('bhts,bhsv->bhtv', scores, vc)
             + jnp.einsum('bhtd,bhdv->bhtv', qc * jnp.exp(b), S))
        b_last = b[:, :, -1:, :]
        S_new = (jnp.exp(b_last[:, :, 0, :])[..., None] * S
                 + jnp.einsum('bhsd,bhsv->bhdv', kc * jnp.exp(b_last - b), vc))
        return S_new, o

    S_fin, o = lax.scan(step, S0, (blocks(q), blocks(k), blocks(v), blocks(logf)))
    o = o.transpose(1, 0, 3, 2, 4).reshape(B, L, H, DV)
    return o, S_fin

def rwkv7_scan(r, logw, k, v, kk, a, S0):
    def step(S, inp):
        r_t, lw_t, k_t, v_t, kk_t, a_t = inp
        sa = jnp.einsum('bhij,bhj->bhi', S, -kk_t)
        S = (S * jnp.exp(lw_t)[:, :, None, :]
             + sa[..., None] * (kk_t * a_t)[:, :, None, :]
             + v_t[..., None] * k_t[:, :, None, :])
        y = jnp.einsum('bhij,bhj->bhi', S, r_t)
        return S, y

    xs = tuple(t.transpose(1, 0, 2, 3) for t in (r, logw, k, v, kk, a))
    S_fin, y = lax.scan(step, S0, xs)
    return y.transpose(1, 0, 2, 3), S_fin

def token_mixers(h, h_prev, S_hg0, S_rw0, v_first, l, lb, p):
    B, L, _ = h.shape
    f32 = jnp.float32
    w_in = p['w_in'][l]
    proj = h @ w_in

    qk_w = HG_HEADS * HG_DK
    hq, hf, hi, hgate = jnp.split(proj[..., :HG_PROJ], [qk_w, 2 * qk_w, 2 * qk_w + HG_WIDTH], axis=-1)
    q = jax.nn.silu(hq.astype(f32)).reshape(B, L, HG_HEADS, HG_DK)
    lb_l = lb[l]
    logf = jnp.logaddexp(jnp.log(lb_l), jnp.log1p(-lb_l) + jax.nn.log_sigmoid(hf.astype(f32)))
    logf = logf.reshape(B, L, HG_HEADS, HG_DK)
    k_hg = -jnp.expm1(logf)
    i_hg = hi.astype(f32).reshape(B, L, HG_HEADS, HG_DV)
    o_hg, S_hg = hgrn2_chunked(q, k_hg, i_hg, logf, S_hg0.astype(f32))
    o_hg = rmsnorm(o_hg, p['hg_norm_w'][l].reshape(HG_HEADS, HG_DV)).reshape(B, L, HG_WIDTH)
    o_hg = (o_hg * jax.nn.silu(hgate.astype(f32))).astype(h.dtype)

    P = proj[..., HG_PROJ:]
    P_prev = shift_right(P, h_prev @ w_in[:, HG_PROJ:])
    P = P + (P_prev - P) * p['rw_mu_proj'][l]
    r, k, v = jnp.split(P, 3, axis=-1)
    dh = shift_right(h, h_prev) - h
    mu = p['rw_mu_lora'][l]
    xw = h + dh * mu[0]
    xa = h + dh * mu[1]
    xg = h + dh * mu[2]
    w_pre = p['rw_w0'][l] + jnp.tanh(xw @ p['rw_w1'][l]) @ p['rw_w2'][l]
    logw = -jnp.exp(-jax.nn.softplus(-w_pre.astype(f32)) - 0.5)
    a = jax.nn.sigmoid((p['rw_a0'][l] + (xa @ p['rw_a1'][l]) @ p['rw_a2'][l]).astype(f32))
    g = jax.nn.sigmoid(xg @ p['rw_g1'][l]) @ p['rw_g2'][l]
    if l == 0:
        v_first = v
    else:
        xv = h + dh * p['rw_mu_vres'][l - 1]
        nu = jax.nn.sigmoid(p['rw_v0'][l - 1] + (xv @ p['rw_v1'][l - 1]) @ p['rw_v2'][l - 1])
        v = v + (v_first - v) * nu

    def heads(t):
        return t.astype(f32).reshape(B, L, RW_HEADS, RW_HEAD)

    r_h, k_h, v_h, a_h, lw_h = heads(r), heads(k), heads(v), heads(a), heads(logw)
    kk = k_h * p['rw_kk'][l].reshape(RW_HEADS, RW_HEAD)
    kk = kk / jnp.maximum(jnp.sqrt(jnp.sum(kk * kk, axis=-1, keepdims=True)), 1e-12)
    k_h = k_h * (1.0 + (a_h - 1.0) * p['rw_ka'][l].reshape(RW_HEADS, RW_HEAD))
    y, S_rw = rwkv7_scan(r_h, lw_h, k_h, v_h, kk, a_h, S_rw0.astype(f32))
    mean = jnp.mean(y, axis=-1, keepdims=True)
    var = jnp.mean(jnp.square(y - mean), axis=-1, keepdims=True)
    y = ((y - mean) * lax.rsqrt(var + RW_GN_EPS) * p['rw_ln_w'][l].reshape(RW_HEADS, RW_HEAD)
         + p['rw_ln_b'][l].reshape(RW_HEADS, RW_HEAD))
    y = y + jnp.sum(r_h * k_h * p['rw_rk'][l], axis=-1, keepdims=True) * v_h
    y = (y.reshape(B, L, RW_WIDTH) * g.astype(f32)).astype(h.dtype)

    out = jnp.concatenate([o_hg, y], axis=-1) @ p['w_out'][l]
    return out, S_hg, S_rw, v_first, h[:, -1, :]

def routed_experts(x, expert_ids, gates, wg, wu, wd):
    T, D = x.shape
    N = T * TOP_K
    flat_e = expert_ids.reshape(N)
    flat_tok = jnp.arange(N, dtype=jnp.int32) // TOP_K
    flat_g = gates.reshape(N)
    order = jnp.argsort(flat_e)
    sorted_e = flat_e[order]
    counts = jnp.bincount(flat_e, length=N_EXPERTS)
    padded = ((counts + MOE_BLOCK - 1) // MOE_BLOCK) * MOE_BLOCK
    start = jnp.cumsum(counts) - counts
    pstart = jnp.cumsum(padded) - padded
    dest = pstart[sorted_e] + jnp.arange(N, dtype=jnp.int32) - start[sorted_e]
    n_blocks = -(-(N + N_EXPERTS * (MOE_BLOCK - 1)) // MOE_BLOCK)
    P = n_blocks * MOE_BLOCK
    buf_tok = jnp.full((P,), T, jnp.int32).at[dest].set(flat_tok[order])
    buf_gate = jnp.zeros((P,), x.dtype).at[dest].set(flat_g[order].astype(x.dtype))
    block_end = jnp.cumsum(padded) // MOE_BLOCK
    block_e = jnp.minimum(jnp.searchsorted(block_end, jnp.arange(n_blocks), side='right'), N_EXPERTS - 1)
    x_pad = jnp.concatenate([x, jnp.zeros((1, D), x.dtype)], axis=0)

    def run_block(args):
        tok, gate, e = args
        xb = x_pad[tok]
        hdn = jax.nn.silu(xb @ wg[e]) * (xb @ wu[e])
        return (hdn @ wd[e]) * gate[:, None]

    yb = lax.map(run_block, (buf_tok.reshape(n_blocks, MOE_BLOCK),
                             buf_gate.reshape(n_blocks, MOE_BLOCK), block_e))
    y = jnp.zeros((T + 1, D), yb.dtype).at[buf_tok].add(yb.reshape(P, D))[:T]
    return y.astype(x.dtype)

def hier_moe(h, l, p):
    B, L, D = h.shape
    T = B * L
    x = h.reshape(T, D)
    f32 = jnp.float32
    g_logits = (x @ p['router_g_w'][l] + p['router_g_b'][l]).astype(f32)
    grp = jnp.argmax(g_logits, axis=-1).astype(jnp.int32)
    p_grp = jnp.take_along_axis(jax.nn.softmax(g_logits, axis=-1), grp[:, None], axis=-1)
    e_logits = (jnp.einsum('td,gde->tge', x, p['router_e_w'][l]) + p['router_e_b'][l]).astype(f32)
    e_logits = jnp.take_along_axis(e_logits, grp[:, None, None], axis=1)[:, 0]
    top_v, top_i = lax.top_k(e_logits, TOP_K)
    gates = p_grp * jax.nn.softmax(top_v, axis=-1)
    expert_ids = grp[:, None] * EXPERTS_PER_GROUP + top_i.astype(jnp.int32)
    y = routed_experts(x, expert_ids, gates, p['w_gate'][l], p['w_up'][l], p['w_down'][l])
    return y.reshape(B, L, D)

def trunk(x, c, S_hg, S_rw, h_prev, p):
    f32 = jnp.float32
    lb = jnp.cumsum(jax.nn.softmax(p['hg_lb_logits'].astype(f32), axis=0), axis=0)
    lb = lb - lb[0]
    cs = jax.nn.silu(c)
    new_hg, new_rw, new_shift = [], [], []
    v_first = None
    for l in range(DEPTH):
        mod = (cs @ p['w_ada'][l] + p['b_ada'][l])[:, None, :]
        sh1, sc1, g1, sh2, sc2, g2 = jnp.split(mod, 6, axis=-1)
        h = rmsnorm(x, p['norm_mix_w'][l]) * (1.0 + sc1) + sh1
        m, s_hg, s_rw, v_first, h_last = token_mixers(h, h_prev[l], S_hg[l], S_rw[l], v_first, l, lb, p)
        x = x + g1 * m
        h2 = rmsnorm(x, p['norm_ffn_w'][l]) * (1.0 + sc2) + sh2
        x = x + g2 * hier_moe(h2, l, p)
        new_hg.append(s_hg.astype(x.dtype))
        new_rw.append(s_rw.astype(x.dtype))
        new_shift.append(h_last.astype(x.dtype))
    y = rmsnorm(x, p['final_norm_w'])
    return y, jnp.stack(new_hg), jnp.stack(new_rw), jnp.stack(new_shift)

def setup_inputs(seed: int = 0) -> dict:
    key = jax.random.key(seed)
    ks = iter(jax.random.split(key, 48))
    f32 = jnp.float32

    def nrm(shape, scale):
        return jax.random.normal(next(ks), shape, f32) * scale

    def uni(shape, lo, hi):
        return jax.random.uniform(next(ks), shape, f32, lo, hi)

    D = D_MODEL
    inv = D ** -0.5
    return {
        'x_prompt': nrm((BATCH, SEQ, D), 1.0),
        'x_sample': nrm((DEC_BATCH, DEC_SEQ, D), 1.0),
        'state_hgrn': nrm((DEPTH, DEC_BATCH, HG_HEADS, HG_DK, HG_DV), 0.5),
        'state_rwkv': nrm((DEPTH, DEC_BATCH, RW_HEADS, RW_HEAD, RW_HEAD), 0.2),
        'state_shift': nrm((DEPTH, DEC_BATCH, D), 1.0),
        'c_prompt': nrm((BATCH, D), 1.0),
        'c_sample': nrm((DEC_BATCH, D), 1.0),
        'w_ada': nrm((DEPTH, D, 6 * D), 0.5 * inv),
        'b_ada': nrm((DEPTH, 6 * D), 0.02),
        'norm_mix_w': 1.0 + nrm((DEPTH, D), 0.05),
        'norm_ffn_w': 1.0 + nrm((DEPTH, D), 0.05),
        'w_in': nrm((DEPTH, D, IN_WIDTH), inv),
        'w_out': nrm((DEPTH, MIX_WIDTH, D), MIX_WIDTH ** -0.5),
        'hg_lb_logits': nrm((DEPTH, HG_HEADS * HG_DK), 1.0),
        'hg_norm_w': 1.0 + nrm((DEPTH, HG_WIDTH), 0.05),
        'rw_mu_proj': uni((DEPTH, RW_PROJ), 0.0, 1.0),
        'rw_mu_lora': uni((DEPTH, 3, D), 0.0, 1.0),
        'rw_w0': uni((DEPTH, RW_WIDTH), -6.0, -1.0),
        'rw_w1': nrm((DEPTH, D, RW_DECAY_LORA), inv),
        'rw_w2': nrm((DEPTH, RW_DECAY_LORA, RW_WIDTH), 0.5 * RW_DECAY_LORA ** -0.5),
        'rw_a0': nrm((DEPTH, RW_WIDTH), 0.1),
        'rw_a1': nrm((DEPTH, D, RW_ICLR_LORA), inv),
        'rw_a2': nrm((DEPTH, RW_ICLR_LORA, RW_WIDTH), 0.5 * RW_ICLR_LORA ** -0.5),
        'rw_g1': nrm((DEPTH, D, RW_GATE_LORA), inv),
        'rw_g2': nrm((DEPTH, RW_GATE_LORA, RW_WIDTH), RW_GATE_LORA ** -0.5),
        'rw_mu_vres': uni((DEPTH - 1, D), 0.0, 1.0),
        'rw_v0': nrm((DEPTH - 1, RW_WIDTH), 0.1),
        'rw_v1': nrm((DEPTH - 1, D, RW_VRES_LORA), inv),
        'rw_v2': nrm((DEPTH - 1, RW_VRES_LORA, RW_WIDTH), 0.5 * RW_VRES_LORA ** -0.5),
        'rw_kk': 0.85 + nrm((DEPTH, RW_WIDTH), 0.05),
        'rw_ka': 1.0 + nrm((DEPTH, RW_WIDTH), 0.05),
        'rw_rk': nrm((DEPTH, RW_HEADS, RW_HEAD), 0.1),
        'rw_ln_w': 1.0 + nrm((DEPTH, RW_WIDTH), 0.05),
        'rw_ln_b': nrm((DEPTH, RW_WIDTH), 0.02),
        'router_g_w': nrm((DEPTH, D, N_GROUPS), inv),
        'router_g_b': nrm((DEPTH, N_GROUPS), 0.01),
        'router_e_w': nrm((DEPTH, N_GROUPS, D, EXPERTS_PER_GROUP), inv),
        'router_e_b': nrm((DEPTH, N_GROUPS, EXPERTS_PER_GROUP), 0.01),
        'w_gate': nrm((DEPTH, N_EXPERTS, D, D_EXPERT), inv),
        'w_up': nrm((DEPTH, N_EXPERTS, D, D_EXPERT), inv),
        'w_down': nrm((DEPTH, N_EXPERTS, D_EXPERT, D), D_EXPERT ** -0.5),
        'final_norm_w': 1.0 + nrm((D,), 0.05),
    }

def reference(x_prompt, x_sample, state_hgrn, state_rwkv, state_shift, c_prompt, c_sample,
              w_ada, b_ada, norm_mix_w, norm_ffn_w, w_in, w_out, hg_lb_logits, hg_norm_w,
              rw_mu_proj, rw_mu_lora, rw_w0, rw_w1, rw_w2, rw_a0, rw_a1, rw_a2, rw_g1, rw_g2,
              rw_mu_vres, rw_v0, rw_v1, rw_v2, rw_kk, rw_ka, rw_rk, rw_ln_w, rw_ln_b,
              router_g_w, router_g_b, router_e_w, router_e_b, w_gate, w_up, w_down, final_norm_w):
    p = dict(w_ada=w_ada, b_ada=b_ada, norm_mix_w=norm_mix_w, norm_ffn_w=norm_ffn_w,
             w_in=w_in, w_out=w_out, hg_lb_logits=hg_lb_logits, hg_norm_w=hg_norm_w,
             rw_mu_proj=rw_mu_proj, rw_mu_lora=rw_mu_lora, rw_w0=rw_w0, rw_w1=rw_w1, rw_w2=rw_w2,
             rw_a0=rw_a0, rw_a1=rw_a1, rw_a2=rw_a2, rw_g1=rw_g1, rw_g2=rw_g2,
             rw_mu_vres=rw_mu_vres, rw_v0=rw_v0, rw_v1=rw_v1, rw_v2=rw_v2,
             rw_kk=rw_kk, rw_ka=rw_ka, rw_rk=rw_rk, rw_ln_w=rw_ln_w, rw_ln_b=rw_ln_b,
             router_g_w=router_g_w, router_g_b=router_g_b, router_e_w=router_e_w,
             router_e_b=router_e_b, w_gate=w_gate, w_up=w_up, w_down=w_down,
             final_norm_w=final_norm_w)
    B = x_prompt.shape[0]
    dt = x_prompt.dtype
    zero_hg = jnp.zeros((DEPTH, B) + state_hgrn.shape[2:], dt)
    zero_rw = jnp.zeros((DEPTH, B) + state_rwkv.shape[2:], dt)
    zero_sh = jnp.zeros((DEPTH, B) + state_shift.shape[2:], dt)
    y_prompt, hg_p, rw_p, sh_p = trunk(x_prompt, c_prompt, zero_hg, zero_rw, zero_sh, p)
    y_sample, hg_s, rw_s, sh_s = trunk(x_sample, c_sample, state_hgrn, state_rwkv, state_shift, p)
    return (y_prompt, y_sample, hg_p, rw_p, sh_p, hg_s, rw_s, sh_s)


_drawn_inputs = setup_inputs


def setup_inputs(seed=0):
    import zlib

    import numpy as np

    out = dict(_drawn_inputs(seed))
    spreads = {}
    factors = {'state_hgrn': 8.0,
     'norm_ffn_w': 2.869,
     'hg_norm_w': 6.298,
     'rw_ln_w': 6.321,
     'rw_ln_b': 8.0,
     'router_g_b': 7.326,
     'router_e_b': 8.0}
    for name, (base, spread) in spreads.items():
        noise = np.random.default_rng([zlib.crc32(name.encode()), seed]).standard_normal(out[name].shape)
        drawn = base * np.exp(spread * noise) if base else spread * noise
        out[name] = __import__('jax').numpy.asarray(drawn.astype(out[name].dtype))
    for name, factor in factors.items():
        out[name] = (out[name] * factor).astype(out[name].dtype)
    return out
```

```python
from contextlib import ExitStack

import numpy as np
import concourse.bass as bass
from concourse import mybir
from concourse.bass import ds

F32 = mybir.dt.float32
I32 = mybir.dt.int32
U32 = mybir.dt.uint32
ALU = mybir.AluOpType
ACT = mybir.ActivationFunctionType
AX = mybir.AxisListType

D = 1024
KD = D // 128
SEQ = 2048
NSEQ, DEC = 8, 16
T = SEQ + NSEQ * DEC
NT = T // 128
PT = SEQ // 128
CH = 64
HG_HEADS, RW_HEADS, RW_N = 4, 8, 64
HG_W = HG_HEADS * 128
RW_W = RW_HEADS * RW_N
IN_W = 4 * HG_W + 3 * RW_W
LORA = 256
W_ALL = IN_W + 2 * LORA
ADA = 6 * D
NORM_EPS = 1e-6
GN_EPS = 64e-5
CM_COLS = [128 * c for c in range(8)] + [4 * HG_W + 128 * c for c in range(12)] + [IN_W + 128 * c for c in range(4)]
NCM = len(CM_COLS)
TM_COLS = [2 * HG_W, 3 * HG_W]
DEC_W = NSEQ * (DEC + 1)

PRM = {"mu_proj": 0, "w0": 12, "a0": 16, "kk": 20, "ka": 24, "rk": 28, "mu_lora": 32}
N_PRM = 56

SHIFT1, SCALE1, GATE1, SHIFT2, SCALE2, GATE2 = range(6)


def at(i, per, const):
    return const if i is None else i * per + const


def sem_of(nc, names, name):
    names.append(nc.alloc_semaphore(name))
    return names[-1]


def finish(nc, names):
    nc.clear_and_free_semaphores(names)
    nc.all_engine_barrier()


def project(nc, t):
    names = []
    with ExitStack() as ctx:
        def sb(name, shape, dt=F32):
            return ctx.enter_context(nc.sbuf_tensor(name, shape, dt))

        def sem(name):
            return sem_of(nc, names, name)

        w = sb("w", [128, KD, W_ALL])
        hT = sb("hT", [128, 2, KD, 512])
        hT_dec = sb("hT_dec", [128, KD, 128])
        hT_pad = sb("hT_pad", [128, KD, NSEQ, DEC + 1])
        x = sb("x", [128, 2, D])
        h = sb("h", [128, 2, D])
        scale_map = sb("scale_map", [128, D])
        shift_map = sb("shift_map", [128, D])
        stage = sb("stage", [128, 4, 512])
        ident = sb("ident", [128, 128])
        stat = sb("stat", [128, 2, 4])
        mu = sb("mu", [128, 24])
        ada = hT
        mod = stage[:, :, :].rearrange("p a b -> p (a b)")
        lora = x[:, :, :].rearrange("p a b -> p (a b)").rearrange("p (k n) -> p k n", k=KD)
        crow = h[:, 0, :]
        csig = h[:, 1, :]
        cT = hT_dec[:, 0, 0:72].rearrange("p (k n) -> p k n", k=KD)
        ones = hT_dec[0:1, 1, 0:9]
        prm_rows = hT_dec[0:24, 2, :]
        bias = hT_pad[:, :, :, :].rearrange("p k s t -> p (k s t)")
        norm_w = scale_map
        shift_rows = h[0:NSEQ, 1, :]

        psT = ctx.enter_context(nc.psum_tensor("psT", [128, KD, 128], F32))
        psG = [ctx.enter_context(nc.psum_tensor(f"psG{b}", [128, 512], F32)) for b in range(4)]

        small_in = sem("small_in")
        lora_in = sem("lora_in")
        norm_in = [sem("norm_in0"), sem("norm_in1")]
        bias_in = [sem("bias_in0"), sem("bias_in1")]
        ada_in = [sem("ada_in0"), sem("ada_in1")]
        w_in = sem("w_in")
        c_exp = sem("c_exp")
        c_ready = sem("c_ready")
        cT_made = sem("cT_made")
        cT_ready = sem("cT_ready")
        mod_made = sem("mod_made")
        mod_kept = sem("mod_kept")
        mod_done = sem("mod_done")
        mod_out = sem("mod_out")
        mu_ready = sem("mu_ready")
        lora_ready = sem("lora_ready")
        maps_in = sem("maps_in")
        maps2_in = sem("maps2_in")
        shift_in = sem("shift_in")
        x_in = [sem("x_in0"), sem("x_in1")]
        squared = sem("squared")
        var_ready = sem("var_ready")
        root_ready = sem("root_ready")
        h_ready = sem("h_ready")
        turned = sem("turned")
        hT_act = sem("hT_act")
        hT_dve = sem("hT_dve")
        last_out = [sem("last_out0"), sem("last_out1")]
        made = sem("made")
        kept = [sem("kept_dve"), sem("kept_act")]
        stage_out = [sem(f"stage_out{s}") for s in range(4)]
        dve_step = sem("dve_step")
        zero_made = sem("zero_made")
        zero_out = sem("zero_out")

        GD = NCM + 2
        GP = NCM + 8
        ADA_G = ADA // 512

        def schedule(groups):
            for g in range(groups):
                yield "gemm", g
                if g % 6 == 1 and g // 6 < 4:
                    yield "norm", g // 6
                if g % 6 == 4 and g // 6 < 4:
                    yield "turn", g // 6

        block = ctx.enter_context(nc.Block())

        @block.sync
        def _(eng):
            eng.dma_start(ident[:, :], t["const"][:, 0:128]).then_inc(small_in, 16)
            eng.dma_start(crow[0:1, :], t["c_prompt"]).then_inc(small_in, 16)
            eng.dma_start(crow[1:9, :], t["c_sample"]).then_inc(small_in, 16)
            eng.dma_start(prm_rows, t["rw_mu_lora"][0].rearrange("j (k p) -> (j k) p", p=128)).then_inc(small_in, 16)
            w_ada = t["w_ada"][0].rearrange("(k p) n -> p k n", p=128)
            b_ada = t["b_ada"]
            for g in range(ADA_G):
                if g >= 2:
                    eng.wait_ge(mod_made, g - 1)
                eng.dma_start(ada[:, g % 2], w_ada[:, :, 512 * g:512 * g + 512]).then_inc(ada_in[g % 2], 16)
                eng.dma_start(bias[0:1, 512 * (g % 2):512 * (g % 2) + 512],
                              b_ada[:, 512 * g:512 * g + 512]).then_inc(bias_in[g % 2], 16)
                if g == 1:
                    eng.dma_start(norm_w[0:9, :], t["norm_mix_w"].to_broadcast([9, D])).then_inc(norm_in[0], 16)
                if g % 4 == 3:
                    eng.wait_ge(mod_done, g // 4 + 1)
                    eng.dma_start(t["mods"][:, 4 * (g // 4) * 512:4 * (g // 4 + 1) * 512],
                                  mod[0:9, :]).then_inc(mod_out, 16)
                    if g == 3:
                        eng.dma_start(norm_w[0:9, :], t["norm_ffn_w"].to_broadcast([9, D])).then_inc(norm_in[1], 16)
                if g == 3:
                    for n, name in enumerate(("rw_w1", "rw_a1", "rw_g1")):
                        c0, cn = 64 * n, 64 if n < 2 else 128
                        eng.dma_start(lora[:, :, c0:c0 + cn],
                                      t[name][0].rearrange("(k p) n -> p k n", p=128)).then_inc(lora_in, 16)
            eng.wait_ge(mod_out, 48)
            for s in range(NSEQ):
                for m, row in ((scale_map, SCALE1), (shift_map, SHIFT1)):
                    eng.dma_start(m[DEC * s:DEC * s + DEC, :],
                                  t["mods"][1 + s:2 + s, row * D:row * D + D].to_broadcast([DEC, D])).then_inc(maps_in, 16)
            eng.wait_ge(lora_ready, 1)
            eng.dma_start(x[:, 0, :], t["x_sample"].rearrange("b t d -> (b t) d")).then_inc(x_in[0], 16)
            eng.dma_start(shift_rows, t["state_shift"][0]).then_inc(shift_in, 16)
            eng.wait_ge(h_ready, 1)
            eng.dma_start(t["shift_s"][0], h[DEC - 1:128:DEC, 0, :]).then_inc(last_out[0], 16)
            for m, row in ((scale_map, SCALE1), (shift_map, SHIFT1)):
                eng.dma_start(m[:, :], t["mods"][0:1, row * D:row * D + D].to_broadcast([128, D])).then_inc(maps2_in, 16)

            def x_load(i, m):
                eng.wait_ge(h_ready, at(i, 8, m - 1))
                if i is None:
                    row = 128 * (m - 1)
                    src = t["x_prompt"][0, row:row + 128, :]
                else:
                    src = t["x_prompt"][0, ds((i * 8 + m - 1) % PT * 128, 128), :]
                eng.dma_start(x[:, m % 2, :], src).then_inc(x_in[m % 2], 16)

            def last_store(i, m):
                eng.wait_ge(h_ready, at(i, 8, m + 1))
                tile = m - 1 if i is None else (i * 8 + m - 1)
                eng.dma_start(t["h_last"][ds(tile, 1), :], h[127:128, m % 2, :]).then_inc(last_out[m % 2], 16)

            def store(i, n, dst):
                eng.wait_ge(kept[n % 2], at(i, GP, n // 2 + 1))
                eng.dma_start(dst, stage[:, n % 4, 0:dst.shape[-1]]).then_inc(stage_out[n % 4], 16)

            eng.wait_ge(zero_made, 1)
            eng.dma_start(t["cm_p"][:, 0:1].rearrange("(c p) o -> p c o", p=128), mu[:, 0:NCM].unsqueeze(2),
                          allow_slow_non_contiguous=True).then_inc(zero_out, 16)
            eng.wait_ge(zero_out, 16)
            x_load(None, 1)
            for what, k in schedule(GD):
                if what == "norm" and k < 3:
                    x_load(None, k + 2)
                if what == "turn":
                    last_store(None, 1 + k)
                if what == "gemm":
                    dst = t["cm_s"][128 * k:128 * k + 128, :] if k < NCM else \
                        t["tm"][SEQ:T, 512 * (k - NCM):512 * (k - NCM) + 512]
                    store(None, k, dst)
            x_load(None, 5)
            with eng.Fori(0, 2) as i:
                for s in range(2):
                    for what, k in schedule(GP):
                        if what == "norm":
                            x_load(i, 6 + 4 * s + k)
                        if what == "turn":
                            last_store(i, 5 + 4 * s + k)
                        if what == "gemm":
                            if k < NCM:
                                dst = t["cm_p"][128 * k:128 * k + 128, ds((i * 2 + s) * 512 + 1, 512)]
                            else:
                                q, half = (k - NCM) // 2, (k - NCM) % 2
                                dst = t["tm"][ds((i * 2 + s) * 512 + 128 * q, 128), 512 * half:512 * half + 512]
                            store(i, GD + GP * s + k, dst)
            total = GD + 4 * GP
            for s in range(4):
                eng.wait_ge(stage_out[s], 16 * len(range(s, total, 4)))
            for s in range(2):
                eng.wait_ge(x_in[s], 16 * 11)
                eng.wait_ge(last_out[s], 16 * (11 - s))
            eng.dma_start(t["shift_p"][0], t["h_last"][PT - 1:PT, :]).then_inc(zero_out, 16)
            eng.wait_ge(zero_out, 32)

        @block.gpsimd
        def _(eng):
            for k in range(KD):
                eng.dma_start(w[:, k, 0:IN_W], t["w_in"][0, 128 * k:128 * k + 128, :]).then_inc(w_in, 16)

        @block.scalar
        def _(eng):
            eng.wait_ge(small_in, 64)
            eng.activation(csig[0:9, :], crow[0:9, :], ACT.Exp, scale=-1.0).then_inc(c_exp, 1)
            for g in range(ADA_G):
                eng.wait_ge(mod_made, g + 1)
                if g % 4 == 0 and g:
                    eng.wait_ge(mod_out, 16 * (g // 4))
                eng.copy(mod[0:9, 512 * (g % 4):512 * (g % 4) + 512], psG[g % 4][0:9, :]).then_inc(mod_kept, 1)

            def norm(i, m):
                eng.wait_ge(x_in[m % 2], at(i, 64, 16 * (m // 2 + 1)))
                if m >= 1:
                    eng.wait_ge(turned, at(i, 8, max(m - 1, 1)))
                if m >= 2:
                    eng.wait_ge(last_out[m % 2], at(i, 64, 16 * (m // 2)))
                eng.activation(h[:, m % 2, :], x[:, m % 2, :], ACT.Square,
                               accum_out=stat[:, m % 2, 0:1]).then_inc(squared, 1)
                eng.wait_ge(var_ready, at(i, 8, m + 1))
                eng.activation(stat[:, m % 2, 2:3], stat[:, m % 2, 1:2], ACT.Sqrt).then_inc(root_ready, 1)

            def turn(i, m, slot, q):
                eng.wait_ge(turned, at(i, 8, m + 1))
                eng.copy(hT[:, slot, 4:8, 128 * q:128 * q + 128], psT[:, 4:8, :]).then_inc(hT_act, 1)

            def keep(i, n, cols):
                eng.wait_ge(made, at(i, 2 * GP, n + 1))
                eng.wait_ge(stage_out[n % 4], at(i, 16 * GP // 2, 16 * (n // 4)))
                eng.copy(stage[:, n % 4, 0:cols], psG[n % 4][:, 0:cols]).then_inc(kept[1], 1)

            eng.wait_ge(lora_ready, 1)
            norm(None, 0)
            eng.wait_ge(turned, 1)
            eng.copy(hT_dec[:, 4:8, :], psT[:, 4:8, :])
            eng.copy(hT_pad[:, 4:8, :, 1:], psT[:, 4:8, :].rearrange("p k (s t) -> p k s t", s=NSEQ)).then_inc(hT_act, 1)
            eng.wait_ge(mod_out, 48)
            for what, k in schedule(GD):
                if what == "gemm" and k % 2:
                    keep(None, k, DEC_W if k < NCM else 512)
                if what == "norm":
                    norm(None, 1 + k)
                if what == "turn":
                    turn(None, 1 + k, 0, k)
            with eng.Fori(0, 2) as i:
                for s in range(2):
                    for what, k in schedule(GP):
                        if what == "gemm" and k % 2:
                            keep(i, GD + GP * s + k, 512)
                        if what == "norm":
                            norm(i, 5 + 4 * s + k)
                        if what == "turn":
                            turn(i, 5 + 4 * s + k, 1 - s, k)

        @block.vector
        def _(eng):
            steps = 0

            def step(ins):
                nonlocal steps
                steps += 1
                ins.then_inc(dve_step, 1)
                eng.wait_ge(dve_step, steps)

            eng.wait_ge(c_exp, 1)
            step(eng.tensor_scalar(csig[0:9, :], csig[0:9, :], 1.0, None, ALU.add))
            step(eng.reciprocal(csig[0:9, :], csig[0:9, :]))
            step(eng.memset(ones, 1.0))
            eng.tensor_tensor(csig[0:9, :], csig[0:9, :], crow[0:9, :], ALU.mult).then_inc(c_ready, 1)
            eng.wait_ge(cT_made, 1)
            step(eng.tensor_copy(mu[:, :], psG[0][:, 128:152]))
            eng.tensor_copy(cT, psG[0][:, 0:72].rearrange("p (k n) -> p k n", k=KD)).then_inc(cT_ready, 1)
            for third in range(3):
                eng.wait_ge(mod_kept, 4 * (third + 1))
                if third != 1:
                    row = mod[0:9, D:2 * D] if third == 0 else mod[0:9, 0:D]
                    eng.wait_ge(norm_in[third // 2], 16)
                    eng.scalar_tensor_tensor(row, row, 1.0, norm_w[0:9, :], ALU.add, ALU.mult).then_inc(mod_done, 1)
                else:
                    eng.sem_inc(mod_done, 1)
            eng.wait_ge(lora_in, 48)
            for k in range(KD):
                for n in range(3):
                    c0, cn = 64 * n, 64 if n < 2 else 128
                    ins = eng.tensor_scalar(w[:, k, IN_W + LORA + c0:IN_W + LORA + c0 + cn], lora[:, k, c0:c0 + cn],
                                            mu[:, KD * n + k:KD * n + k + 1], None, ALU.mult)
            step(ins)
            step(eng.tensor_tensor(w[:, :, IN_W:IN_W + LORA], lora, w[:, :, IN_W + LORA:W_ALL], ALU.subtract))
            eng.sem_inc(lora_ready, 1)
            eng.memset(mu[:, :], 0.0).then_inc(zero_made, 1)

            def norm(i, m):
                eng.wait_ge(squared, at(i, 8, m + 1))
                eng.tensor_scalar(stat[:, m % 2, 1:2], stat[:, m % 2, 0:1], 1.0 / D, NORM_EPS,
                                  ALU.mult, ALU.add).then_inc(var_ready, 1)
                eng.wait_ge(root_ready, at(i, 8, m + 1))
                eng.reciprocal(stat[:, m % 2, 3:4], stat[:, m % 2, 2:3]).then_inc(dve_step, 1)
                eng.wait_ge(dve_step, at(i, 16, steps + 2 * m + 1))
                eng.scalar_tensor_tensor(h[:, m % 2, :], x[:, m % 2, :], stat[:, m % 2, 3:4], scale_map[:, :],
                                         ALU.mult, ALU.mult).then_inc(dve_step, 1)
                eng.wait_ge(dve_step, at(i, 16, steps + 2 * m + 2))
                eng.tensor_tensor(h[:, m % 2, :], h[:, m % 2, :], shift_map[:, :], ALU.add).then_inc(h_ready, 1)

            def turn(i, m, slot, q):
                eng.wait_ge(turned, at(i, 8, m + 1))
                eng.tensor_copy(hT[:, slot, 0:4, 128 * q:128 * q + 128], psT[:, 0:4, :]).then_inc(hT_dve, 1)

            def keep(i, n, cols):
                eng.wait_ge(made, at(i, 2 * GP, n + 1))
                if n >= 4:
                    eng.wait_ge(stage_out[n % 4], at(i, 16 * GP // 2, 16 * (n // 4)))
                eng.tensor_copy(stage[:, n % 4, 0:cols], psG[n % 4][:, 0:cols]).then_inc(kept[0], 1)

            eng.wait_ge(maps_in, 32 * NSEQ)
            norm(None, 0)
            eng.wait_ge(turned, 1)
            eng.tensor_copy(hT_dec[:, 0:4, :], psT[:, 0:4, :])
            eng.tensor_copy(hT_pad[:, 0:4, :, 1:],
                            psT[:, 0:4, :].rearrange("p k (s t) -> p k s t", s=NSEQ))
            eng.tensor_copy(hT_pad[:, :, :, 0], psG[3][:, 0:64].rearrange("p (k s) -> p k s", k=KD)).then_inc(hT_dve, 1)
            eng.wait_ge(mod_out, 48)
            eng.wait_ge(maps2_in, 32)
            for what, k in schedule(GD):
                if what == "gemm" and k % 2 == 0:
                    keep(None, k, DEC_W if k < NCM else 512)
                if what == "norm":
                    norm(None, 1 + k)
                if what == "turn":
                    turn(None, 1 + k, 0, k)
            with eng.Fori(0, 2) as i:
                for s in range(2):
                    for what, k in schedule(GP):
                        if what == "gemm" and k % 2 == 0:
                            keep(i, GD + GP * s + k, 512)
                        if what == "norm":
                            norm(i, 5 + 4 * s + k)
                        if what == "turn":
                            turn(i, 5 + 4 * s + k, 1 - s, k)

        @block.tensor
        def _(eng):
            eng.wait_ge(small_in, 64)
            eng.wait_ge(c_ready, 1)
            for k in range(KD):
                eng.transpose(psG[0][:, 9 * k:9 * k + 9], csig[0:9, 128 * k:128 * k + 128], ident[0:9, 0:9])
            eng.transpose(psG[0][:, 128:152], prm_rows, ident[0:24, 0:24]).then_inc(cT_made, 1)
            eng.wait_ge(cT_ready, 1)
            for g in range(ADA_G):
                eng.wait_ge(ada_in[g % 2], 16 * (g // 2 + 1))
                eng.wait_ge(bias_in[g % 2], 16 * (g // 2 + 1))
                if g >= 4:
                    eng.wait_ge(mod_kept, g - 3)
                for k in range(KD):
                    eng.matmul(psG[g % 4][0:9, :], cT[:, k, :], ada[:, g % 2, k, :], start=(k == 0), stop=False)
                eng.matmul(psG[g % 4][0:9, :], ones, bias[0:1, 512 * (g % 2):512 * (g % 2) + 512],
                           start=False, stop=True).then_inc(mod_made, 1)

            def turn(i, m):
                eng.wait_ge(h_ready, at(i, 8, m + 1))
                if m >= 1:
                    eng.wait_ge(hT_act, at(i, 8, m))
                    eng.wait_ge(hT_dve, at(i, 8, m))
                for k in range(KD):
                    ins = eng.transpose(psT[:, k, :], h[:, m % 2, 128 * k:128 * k + 128], ident[:, :])
                ins.then_inc(turned, 1)

            def free(i, n):
                if n >= 4:
                    eng.wait_ge(kept[n % 2], at(i, GP, (n - 4) // 2 + 1))

            eng.wait_ge(mod_kept, ADA_G)
            eng.wait_ge(shift_in, 16)
            for k in range(KD):
                eng.transpose(psG[3][:, 8 * k:8 * k + 8], shift_rows[:, 128 * k:128 * k + 128], ident[0:8, 0:8])
            turn(None, 0)
            eng.wait_ge(hT_act, 1)
            eng.wait_ge(hT_dve, 1)
            eng.wait_ge(w_in, 16 * KD)
            eng.wait_ge(lora_ready, 1)
            for what, g in schedule(GD):
                if what == "turn":
                    turn(None, 1 + g)
                if what != "gemm":
                    continue
                free(None, g)
                for k in range(KD):
                    if g < NCM:
                        ins = eng.matmul(psG[g % 4][:, 0:DEC_W], w[:, k, CM_COLS[g]:CM_COLS[g] + 128],
                                         hT_pad[:, k, :, :].rearrange("p s t -> p (s t)"), start=(k == 0), stop=(k == KD - 1))
                    else:
                        c0 = TM_COLS[g - NCM]
                        ins = eng.matmul(psG[g % 4][:, :], hT_dec[:, k, :], w[:, k, c0:c0 + 512],
                                         start=(k == 0), stop=(k == KD - 1))
                ins.then_inc(made, 1)
            with eng.Fori(0, 2) as i:
                for s in range(2):
                    eng.wait_ge(hT_act, at(i, 8, 5 + 4 * s))
                    eng.wait_ge(hT_dve, at(i, 8, 5 + 4 * s))
                    for what, g in schedule(GP):
                        if what == "turn":
                            turn(i, 5 + 4 * s + g)
                        if what != "gemm":
                            continue
                        n = GD + GP * s + g
                        free(i, n)
                        for k in range(KD):
                            if g < NCM:
                                ins = eng.matmul(psG[n % 4][:, :], w[:, k, CM_COLS[g]:CM_COLS[g] + 128],
                                                 hT[:, s, k, :], start=(k == 0), stop=(k == KD - 1))
                            else:
                                q, c0 = (g - NCM) // 2, TM_COLS[(g - NCM) % 2]
                                ins = eng.matmul(psG[n % 4][:, :], hT[:, s, k, 128 * q:128 * q + 128],
                                                 w[:, k, c0:c0 + 512], start=(k == 0), stop=(k == KD - 1))
                        ins.then_inc(made, 1)
    finish(nc, names)


N_LEVELS = 6
C_ID, C_LEVEL, C_LEVEL_T = 0, 1, 1 + N_LEVELS
C_STRICT, C_INCL, C_LOWER, C_LOWER2, C_HEAD, C_PAD = [1 + 2 * N_LEVELS + n for n in range(6)]
C_CUM, C_ONES = C_PAD + 1, C_PAD + 2
N_CONST = C_PAD + 3


def constants():
    s, u = np.arange(128)[:, None], np.arange(128)[None, :]
    same = s // CH == u // CH
    out = [s == u]
    levels = [(s // (2 << n) == u // (2 << n)) & (s // (1 << n) % 2 == 0) & (u // (1 << n) % 2 == 1)
              for n in range(N_LEVELS)]
    out += levels + [x.T for x in levels]
    out += [same & (s < u), same & (s <= u), same & (u < s), same & (u < s), same, (u % CH < DEC) & (s >= 0), s <= u, (s >= 0) & (u >= 0)]
    return np.concatenate([x.astype(np.float32) for x in out], axis=1)


def resets():
    return np.broadcast_to((np.arange(512) % CH != 0).astype(np.float32), (128, 512)).copy()


DECAY = float(np.exp(-0.5))


def recur(nc, t, running):
    part = "run_" if running else "prompt_"
    names = []
    with ExitStack() as ctx:
        def sb(name, shape, dt=F32):
            return ctx.enter_context(nc.sbuf_tensor(part + name, shape, dt))

        sems = {}

        def ev(name):
            if name not in sems:
                sems[name] = sem_of(nc, names, part + name)
            return sems[name]

        n_tiles = NSEQ // 2 if running else PT
        n_zeroed = 4 if running else 2

        const = sb("const", [128, N_CONST, 128])
        prm = sb("prm", [128, N_PRM])
        rows = sb("rows", [128, 3, 512])
        one = sb("one", [128, 1])
        fw2 = sb("fw2", [128, RW_W])
        fg2 = sb("fg2", [128, RW_W])
        reset = sb("reset", [128, 4, 2, CH])
        prm_rows = sb("prm_rows", [N_PRM, 128])
        hin = sb("hin", [128, 8, 128])
        vin = sb("vin", [128, 2, 512])
        z = sb("z", [128, 8, 128])
        sk = sb("sk", [128, 8, 128])
        lf = sb("lf", [128, 4, 128])
        dd = sb("dd", [128, 8, 4, 128])
        q = sb("q", [128, 4, 128])
        gs = sb("gs", [128, 512])
        hdec = sb("hdec", [128, 4, 2])
        at_ = sb("at_", [128, 4, 128])
        kdT = sb("kdT", [128, 4, 128])
        S = sb("S", [128, 4 if running else 2, 4, 128])
        osq = sb("osq", [128, 512])
        hst = sb("hst", [128, 2, 4])
        rin = sb("rin", [128, 16, 129])
        pm = sb("pm", [128, 12, 128])
        tl = sb("tl", [128, 2, 128])
        te = sb("te", [128, 2, 128])
        u = sb("u", [128, 8, 128])
        cs = sb("cs", [128, 4, 128])
        cx = sb("cx", [128, 4, 128])
        e1 = sb("e1", [128, 4, 128])
        e2 = sb("e2", [128, 4, 128])
        e3 = sb("e3", [128, 4, 128])
        kr = sb("kr", [128, 4, 128])
        sq = sb("sq", [128, 4, 128])
        kn = sb("kn", [128, 4, 128])
        bon = sb("bon", [128, 4, 128])
        AR = sb("AR", [128, 4, 2, 128])
        BK = sb("BK", [128, 4, 2, 128])
        gate = sb("gate", [128, 512])
        tok = sb("tok", [128, 4, 512])
        LB = sb("LB", [128, 8, 2, 128])
        LM = sb("LM", [128, 8, 2, 128])
        KR = sb("KR", [128, 8, 128])
        X = sb("X", [128, 8, 128])
        XT = sb("XT", [128, 8, 128])
        Y = sb("Y", [128, 8, 128])
        XA = sb("XA", [128, 4, 128])
        MX = sb("MX", [128, 8, 128])
        SA = sb("SA", [128, 512])
        ST = sb("ST", [128, 4 if running else 2, 4, 128])
        wm = sb("wm", [128, 2, 4, 128])
        bonus = sb("bonus", [128, 8])
        rst = sb("rst", [128, 3, 8])
        yc = sb("yc", [128, 512])
        ysq = sb("ysq", [128, 512])
        mix = sb("mix", [128, D])
        srow = sb("srow", [128, 2, 4, 128])
        sout = sb("sout", [128, 2, 4, RW_N])
        P = [ctx.enter_context(nc.psum_tensor(f"{part}P{b}", [128, 512], F32)) for b in range(8)]

        def cm(n):
            return const[:, n, :]

        def heads(x, n=4):
            return x.rearrange("p (h c) -> p h c", h=n)

        ident = cm(C_ID)

        def column(name, n=4):
            c = PRM[name]
            return prm[:, c:c + n].unsqueeze(2).to_broadcast([128, n, 128])

        block = ctx.enter_context(nc.Block())

        @block.sync
        def _(eng):
            eng.dma_start(const[:, :, :].rearrange("p a b -> p (a b)"), t["const"]).then_inc(ev("const_in"), 16)
            eng.dma_start(reset[:, :, :, :].rearrange("p a b c -> p (a b c)"), t["reset"]).then_inc(ev("const_in"), 16)
            for name, n in (("rw_mu_proj", 12), ("rw_w0", 4), ("rw_a0", 4), ("rw_kk", 4), ("rw_ka", 4)):
                r0 = PRM[name[3:]]
                eng.dma_start(prm_rows[r0:r0 + n, :], t[name][0].rearrange("(c p) -> c p", p=128)).then_inc(ev("const_in"), 16)
            r0 = PRM["rk"]
            eng.dma_start(prm_rows[r0:r0 + 4, :], t["rw_rk"][0].rearrange("(c h) n -> c (h n)", h=2)).then_inc(ev("const_in"), 16)
            eng.dma_start(prm_rows[PRM["mu_lora"]:N_PRM, :],
                          t["rw_mu_lora"][0].rearrange("j (k p) -> (j k) p", p=128)).then_inc(ev("const_in"), 16)
            for n, name in enumerate(("hg_norm_w", "rw_ln_w", "rw_ln_b")):
                eng.dma_start(rows[:, n, :], t[name].to_broadcast([128, 512])).then_inc(ev("const_in"), 16)
            eng.dma_start(fw2[0:64, :], t["rw_w2"][0]).then_inc(ev("const_in"), 16)
            eng.dma_start(fw2[64:128, :], t["rw_a2"][0]).then_inc(ev("const_in"), 16)
            eng.dma_start(fg2[:, :], t["rw_g2"][0]).then_inc(ev("const_in"), 16)
            if running:
                eng.wait_ge(ev("zeroed"), n_zeroed)

            def load_h(i, n):
                if running:
                    cmp_ = t["cm_s"].rearrange("(c p) (s w) -> p c s w", p=128, s=NSEQ)
                    tmp_ = t["tm"][SEQ:T, :].rearrange("(s w) c -> s w c", s=NSEQ)
                    for c in range(2):
                        s = c if i is None else (i * 2 + (2 * n + c)) % NSEQ
                        for g in range(2):
                            eng.dma_start(hin[:, 4 * g:4 * g + 4, CH * c:CH * c + DEC],
                                          cmp_[:, 4 * g:4 * g + 4, ds(s, 1), 1:].rearrange("p c s w -> p c (s w)")).then_inc(ev("h_in"), 16)
                        eng.dma_start(vin[CH * c:CH * c + DEC, :, :].rearrange("p a b -> p (a b)"),
                                      tmp_[ds(s, 1)].rearrange("s w c -> (s w) c")).then_inc(ev("h_in"), 16)
                else:
                    k = 0 if i is None else (i + n) % PT * 128
                    eng.dma_start(hin[:, :, :], t["cm_p"][0:1024, :].rearrange("(c p) w -> p c w", p=128)[:, :, ds(k + 1, 128)]).then_inc(ev("h_in"), 16)
                    eng.dma_start(vin[:, :, :].rearrange("p a b -> p (a b)"), t["tm"][ds(k, 128), :]).then_inc(ev("h_in"), 16)

            def load_r(i):
                if running:
                    cmp_ = t["cm_s"].rearrange("(c p) (s w) -> p c s w", p=128, s=NSEQ)
                    for c in range(2):
                        eng.dma_start(rin[:, :, CH * c:CH * c + DEC + 1],
                                      cmp_[:, 8:24, ds(i * 2 + c, 1), :].rearrange("p c s w -> p c (s w)")).then_inc(ev("r_in"), 16)
                else:
                    eng.dma_start(rin[:, :, :], t["cm_p"][1024:3072, :].rearrange("(c p) w -> p c w", p=128)[:, :, ds(i * 128, 129)]).then_inc(ev("r_in"), 16)

            load_h(None, 0)
            with eng.Fori(0, n_tiles) as i:
                if running:
                    eng.wait_ge(ev("h_updated"), i * 2)
                    eng.wait_ge(ev("st_turned"), i * 2)
                    for c in range(2):
                        eng.dma_start(S[:, c, :, :], t["state_hgrn"][0, ds(i * 2 + c, 1)].rearrange("s h k v -> k (s h) v")).then_inc(ev("s_in"), 16)
                        for g in range(2):
                            eng.dma_start(srow[64 * g:64 * g + 64, c, :, 64 * g:64 * g + 64],
                                          t["state_rwkv"][0, ds(i * 2 + c, 1), g:8:2].rearrange("s h v k -> v (s h) k")).then_inc(ev("s_in"), 16)
                eng.wait_ge(ev("r_used"), i)
                load_r(i)
                eng.wait_ge(ev("h_used"), i + 1)
                load_h(i, 1)
                if running:
                    eng.wait_ge(ev("h_updated"), i * 2 + 2)
                    for c in range(2):
                        eng.dma_start(t["new_hgrn_s"][0, ds(i * 2 + c, 1)].rearrange("s h k v -> k (s h) v"), S[:, 2 + c, :, :]).then_inc(ev("s_out"), 16)
                    eng.wait_ge(ev("st_turned_back"), i + 1)
                    for c in range(2):
                        eng.dma_start(t["new_rwkv_s"][0, ds(i * 2 + c, 1)].rearrange("s (h g) v k -> (s g v) h k", g=2), sout[:, c, :, :]).then_inc(ev("s_out"), 16)
                    eng.wait_ge(ev("s_out"), i * 64 + 64)
                eng.wait_ge(ev("mixed"), i + 1)
                if running:
                    for c in range(2):
                        eng.dma_start(t["mix"][ds(i * (2 * DEC) + (SEQ + DEC * c), DEC), :], mix[CH * c:CH * c + DEC, :]).then_inc(ev("mix_out"), 16)
                else:
                    eng.dma_start(t["mix"][ds(i * 128, 128), :], mix[:, :]).then_inc(ev("mix_out"), 16)
            eng.wait_ge(ev("mix_out"), (32 if running else 16) * n_tiles)
            eng.wait_ge(ev("h_in"), (96 if running else 32) * (n_tiles + 1))
            if not running:
                eng.dma_start(t["new_hgrn_p"][0, 0].rearrange("h k v -> k h v"), S[:, 0, :, :]).then_inc(ev("s_out"), 16)
                eng.wait_ge(ev("st_turned_back"), 1)
                eng.dma_start(t["new_rwkv_p"][0, 0].rearrange("(h g) v k -> (g v) h k", g=2), sout[:, 0, :, :]).then_inc(ev("s_out"), 16)
                eng.wait_ge(ev("s_out"), 32)

        @block.gpsimd
        def _(eng):
            eng.memset(one[:, :], 1.0).then_inc(ev("one_made"), 1)
            if running:
                for buffer in (hin[:, :, :], vin[:, :, :], rin[:, :, :]):
                    eng.memset(buffer, 0.0).then_inc(ev("zeroed"), 1)
                eng.memset(srow[:, :, :, :], 0.0).then_inc(ev("zeroed"), 1)
            else:
                eng.memset(S[:, 0, :, :], 0.0).then_inc(ev("zeroed"), 1)
                eng.memset(ST[:, 0, :, :], 0.0).then_inc(ev("zeroed"), 1)
            with eng.Fori(0, n_tiles) as i:
                eng.wait_ge(ev("r_in"), i * (32 if running else 16) + (32 if running else 16))
                eng.wait_ge(ev("v_turned"), i)
                eng.tensor_tensor(pm[:, :, :], rin[:, 0:12, 0:128], rin[:, 0:12, 1:129], ALU.subtract).then_inc(ev("shifted"), 1)

        def h_prep_scalar(eng, i, n):
            got = (96 if running else 32)
            eng.wait_ge(ev("h_in"), at(i, got, got * (n + 1)))
            eng.activation(z[:, :, :], hin[:, :, :], ACT.Abs).then_inc(ev("a_z1"), 1)
            eng.wait_ge(ev("a_z1"), at(i, 1, n + 1))
            eng.activation(z[:, :, :], z[:, :, :], ACT.Exp, scale=-1.0).then_inc(ev("a_z2"), 1)
            eng.wait_ge(ev("a_z2"), at(i, 1, n + 1))
            eng.activation(z[:, :, :], z[:, :, :], ACT.Ln, bias=one[:, :]).then_inc(ev("a_z3"), 1)
            if n:
                eng.wait_ge(ev("h_mixed"), at(i, 1, n))
            eng.activation(gs[:, :], vin[:, 1, :], ACT.Exp, scale=-1.0).then_inc(ev("a_gs"), 1)
            yield
            eng.wait_ge(ev("v_z"), at(i, 1, n + 1))
            eng.activation(sk[:, :, :], z[:, :, :], ACT.Exp).then_inc(ev("a_sk"), 1)
            yield
            eng.wait_ge(ev("v_dd"), at(i, 1, n + 1))
            for g in range(4):
                ins = eng.activation(dd[:, 2 * g:2 * g + 2, :, :], dd[:, 2 * g:2 * g + 2, :, :], ACT.Exp)
            ins.then_inc(ev("a_dd"), 1)
            yield

        def h_prep_vector(eng, i, n, step, settle):
            eng.wait_ge(ev("a_z3"), at(i, 1, n + 1))
            step(eng.scalar_tensor_tensor(lf[:, :, :], hin[:, 4:8, :], 0.0, z[:, 4:8, :], ALU.min, ALU.subtract))
            step(eng.scalar_tensor_tensor(z[:, 0:4, :], hin[:, 0:4, :], 0.0, z[:, 0:4, :], ALU.min, ALU.subtract))
            settle()
            eng.tensor_tensor(z[:, 4:8, :], lf[:, :, :], hin[:, 4:8, :], ALU.subtract).then_inc(ev("v_z"), 1)
            if running:
                eng.wait_ge(ev("v_z"), at(i, 1, n + 1))
                step(eng.tensor_tensor(lf[:, :, :], lf[:, :, :], cm(C_PAD).unsqueeze(1).to_broadcast([128, 4, 128]), ALU.mult))
                settle()
            if n:
                eng.wait_ge(ev("h_used"), at(i, 1, n))
            step(eng.tensor_tensor_scan(dd[:, 6, :, :].rearrange("p h c -> p (h c)"), reset[:, :, :, :].rearrange("p a b c -> p (a b c)"),
                                        lf[:, :, :].rearrange("p h c -> p (h c)"), 0.0, ALU.mult, ALU.add))
            eng.wait_ge(ev("a_gs"), at(i, 1, n + 1))
            step(eng.tensor_scalar(gs[:, :], gs[:, :], 1.0, None, ALU.add))
            settle()
            step(eng.reciprocal(gs[:, :], gs[:, :]))
            settle()
            step(eng.tensor_tensor(gs[:, :], gs[:, :], vin[:, 1, :], ALU.mult))
            yield
            b = dd[:, 6, :, :].rearrange("p h c -> p (h c)")
            for lv in range(N_LEVELS):
                half = 1 << lv
                src = b.rearrange("p (n a l) -> p n a l", a=2, l=half)
                dst = dd[:, lv, :, :].rearrange("p h c -> p (h c)").rearrange("p (n a l) -> p n a l", a=2, l=half)
                mid = src[:, :, 0, half - 1:half].to_broadcast([128, 256 // half, half])
                step(eng.tensor_tensor(dst[:, :, 0, :], mid, src[:, :, 0, :], ALU.subtract))
                step(eng.tensor_tensor(dst[:, :, 1, :], src[:, :, 1, :], mid, ALU.subtract))
            bc = b.rearrange("p (n l) -> p n l", l=CH)
            settle()
            eng.tensor_tensor(dd[:, 7, :, :].rearrange("p h c -> p (h c)").rearrange("p (n l) -> p n l", l=CH),
                              bc[:, :, CH - 1:CH].to_broadcast([128, 8, CH]), bc, ALU.subtract).then_inc(ev("v_dd"), 1)
            yield
            eng.wait_ge(ev("a_sk"), at(i, 1, n + 1))
            step(eng.tensor_tensor(q[:, :, :], hin[:, 0:4, :], sk[:, 0:4, :], ALU.mult))
            if running:
                step(eng.tensor_tensor(sk[:, 4:8, :], sk[:, 4:8, :], cm(C_PAD).unsqueeze(1).to_broadcast([128, 4, 128]), ALU.mult))
            eng.wait_ge(ev("a_dd"), at(i, 1, n + 1))
            settle()
            step(eng.tensor_copy(hdec[:, :, :], dd[:, 6, :, :].rearrange("p h (c l) -> p h c l", l=CH)[:, :, :, CH - 1]))
            for lv in range(N_LEVELS):
                half = 1 << lv
                cut = [y.rearrange("p h c -> p (h c)").rearrange("p (n a l) -> p n a l", a=2, l=half)
                       for y in (dd[:, lv, :, :], sk[:, 4:8, :], q[:, :, :])]
                step(eng.tensor_tensor(cut[0][:, :, 0, :], cut[0][:, :, 0, :], cut[1][:, :, 0, :], ALU.mult))
                step(eng.tensor_tensor(cut[0][:, :, 1, :], cut[0][:, :, 1, :], cut[2][:, :, 1, :], ALU.mult))
            yield
            step(eng.tensor_tensor(dd[:, 7, :, :], dd[:, 7, :, :], sk[:, 4:8, :], ALU.mult))
            settle()
            eng.tensor_tensor(dd[:, 6, :, :], dd[:, 6, :, :], q[:, :, :], ALU.mult).then_inc(ev("h_ready"), 1)
            yield

        @block.tensor
        def _(eng):
            eng.wait_ge(ev("const_in"), 16 * 15)
            eng.transpose(P[0][:, 0:N_PRM], prm_rows[:, :], ident[0:N_PRM, 0:N_PRM]).then_inc(ev("prm_turned"), 1)
            eng.wait_ge(ev("prm_ready"), 1)
            eng.wait_ge(ev("zeroed"), n_zeroed)
            with eng.Fori(0, n_tiles) as i:
                eng.wait_ge(ev("h_ready"), i + 1)
                eng.wait_ge(ev("p_mix_read"), i)
                for h in range(4):
                    ins = eng.transpose(P[3][:, 128 * h:128 * h + 128], dd[:, 7, h, :], ident)
                ins.then_inc(ev("kd_turned"), 1)
                for n in range(1 + N_LEVELS):
                    bank = P[4 + n % 2]
                    if n >= 2:
                        eng.wait_ge(ev("scored"), i * 7 + n - 1)
                    for h in range(4):
                        a, b = (sk[:, 4 + h, :], q[:, h, :]) if n == 0 else (dd[:, n - 1, h, :], dd[:, n - 1, h, :])
                        ins = eng.matmul(bank[:, 128 * h:128 * h + 128], a, b, start=(h == 0), stop=(h == 3), skip_group_check=True)
                    ins.then_inc(ev("score_made"), 1)
                eng.wait_ge(ev("lora_ready"), i + 1)
                for c in range(4):
                    ins = eng.matmul(P[0][:, 128 * c:128 * c + 128], fw2[0:64, 128 * c:128 * c + 128], te[0:64, 0, :],
                                     start=(c == 0), stop=(c == 3), skip_group_check=True)
                for c in range(4):
                    ins = eng.matmul(P[1][:, 128 * c:128 * c + 128], fw2[64:128, 128 * c:128 * c + 128], te[64:128, 0, :],
                                     start=(c == 0), stop=(c == 3), skip_group_check=True)
                ins.then_inc(ev("wa_made"), 1)
                eng.matmul(P[2][:, :], te[:, 1, :], fg2[:, :], start=True, stop=True).then_inc(ev("gate_made"), 1)
                eng.wait_ge(ev("k_squared"), i + 1)
                eng.matmul(P[6][:, :], cm(C_HEAD), sq[:, :, :].rearrange("p a b -> p (a b)"), start=True, stop=True).then_inc(ev("norm_made"), 1)
                if running:
                    eng.wait_ge(ev("s_in"), i * 96 + 96)
                eng.wait_ge(ev("scored"), i * 7 + 7)
                for h in range(4):
                    eng.matmul(P[7][:, 128 * h:128 * h + 128], at_[:, h, :], vin[:, 0, 128 * h:128 * h + 128],
                               start=(h == 0), stop=False, skip_group_check=True)
                eng.wait_ge(ev("kd_kept"), i + 1)
                for c in range(2):
                    r = slice(CH * c, CH * c + CH)
                    if c or not running:
                        eng.wait_ge(ev("h_updated"), i * 2 + c)
                    for h in range(4):
                        ins = eng.matmul(P[7][r, 128 * h:128 * h + 128], dd[:, 6, h, r], S[:, c, h, :],
                                         start=False, stop=(h == 3 and c == 1), skip_group_check=True)
                    for h in range(4):
                        ins = eng.matmul(P[4 + c][:, 128 * h:128 * h + 128], kdT[r, h, :], vin[r, 0, 128 * h:128 * h + 128],
                                         start=(h == 0), stop=(h == 3), skip_group_check=True)
                    ins.then_inc(ev("h_update_made"), 1)
                eng.wait_ge(ev("h_update_made"), i * 2 + 2)
                eng.sem_inc(ev("h_used"), 1)
                if running:
                    eng.wait_ge(ev("gate_read"), i + 1)
                    for c in range(2):
                        for y in range(4):
                            ins = eng.transpose(P[3 - c][:, 128 * y:128 * y + 128], srow[:, c, y, :], ident)
                        ins.then_inc(ev("st_turned"), 1)
                eng.wait_ge(ev("wa_read"), i + 1)
                eng.wait_ge(ev("mixed_rkv"), i + 1)
                for c in range(4):
                    ins = eng.transpose(P[0][:, 128 * c:128 * c + 128], pm[:, 8 + c, :], ident)
                ins.then_inc(ev("v_turned"), 1)
                eng.wait_ge(ev("rw_ready"), i + 1)
                eng.wait_ge(ev("gate_read"), i + 1)
                if running:
                    eng.wait_ge(ev("st_kept"), i * 2 + 2)
                for bank, x, j in ((1, AR, 0), (2, BK, 0), (3, BK, 1)):
                    for c in range(4):
                        ins = eng.transpose(P[bank][:, 128 * c:128 * c + 128], x[:, c, j, :], ident)
                    ins.then_inc(ev("tok_turned"), 1)
                eng.wait_ge(ev("norm_read"), i + 1)
                for c in range(4):
                    ins = eng.matmul(P[6][:, 2 * c:2 * c + 2], bon[:, c, :], cm(C_HEAD)[:, 0:128:64], start=(c == 0), stop=(c == 3),
                                     skip_group_check=True)
                ins.then_inc(ev("bonus_made"), 1)
                eng.wait_ge(ev("h_updated"), i * 2 + 2)
                banks = [4, 5, 0, 3]
                n = 0
                for pairs in range(2):
                    for kind, j in ((0, 0), (0, 1), (1, 0), (1, 1)):
                        bank = P[banks[n % 4]]
                        if n == 2:
                            eng.wait_ge(ev("v_kept"), i + 1)
                        if n == 3:
                            eng.wait_ge(ev("tok_kept"), i + 1)
                        if n >= 4:
                            eng.wait_ge(ev("product_kept"), i * 10 + n - 3)
                        o = slice(64 * j, 64 * j + 64)
                        a, b = (BK, AR) if kind == 0 else (AR, BK)
                        for m in range(2):
                            ins = eng.matmul(bank[:, 256 * m:256 * m + 256], a[o, 2 * pairs + m, 0, :],
                                             b[o, 2 * pairs + m, :, :].rearrange("p a b -> p (a b)"), start=(m == 0), stop=(m == 1),
                                             skip_group_check=True)
                        ins.then_inc(ev("product_made"), 1)
                        n += 1
                for g in range(2):
                    eng.wait_ge(ev("product_kept"), i * 10 + n - 3)
                    o = slice(64 * g, 64 * g + 64)
                    for h in range(4):
                        ins = eng.matmul(P[banks[n % 4]][:, 128 * h:128 * h + 128], BK[o, h, 1, :], AR[o, h, 1, :],
                                         start=(h == 0), stop=(h == 3), skip_group_check=True)
                    ins.then_inc(ev("product_made"), 1)
                    n += 1
                eng.wait_ge(ev("product_kept"), i * 10 + 10)
                eng.wait_ge(ev("x_begun"), i + 1)
                for g in range(2):
                    eng.matmul(P[g][:, :], ident, X[:, 4 * g:4 * g + 4, :].rearrange("p a b -> p (a b)"), start=True, stop=False, skip_group_check=True)
                    eng.matmul(P[2 + g][:, :], ident, XT[:, 4 * g:4 * g + 4, :].rearrange("p a b -> p (a b)"), start=True, stop=False, skip_group_check=True)
                for lv in range(1, N_LEVELS):
                    k = lv - 1
                    for g in range(2):
                        if lv > 1:
                            eng.wait_ge(ev("x_kept"), i * 8 + 2 * (k - 1) + g + 1)
                        for h in range(4 * g, 4 * g + 4):
                            ins = eng.matmul(P[4 + g][:, 128 * (h % 4):128 * (h % 4) + 128], LB[:, h, 0, :], X[:, h, :],
                                             start=(h % 4 == 0), stop=(h % 4 == 3), skip_group_check=True)
                        ins.then_inc(ev("y_made"), 1)
                    for g in range(2):
                        eng.wait_ge(ev("y_kept"), i * 10 + 2 * k + g + 1)
                        if lv > 1:
                            eng.wait_ge(ev("xt_kept"), i * 10 + 2 * (k - 1) + g + 1)
                        if lv < N_LEVELS - 1:
                            for h in range(4 * g, 4 * g + 4):
                                ins = eng.matmul(P[g][:, 128 * (h % 4):128 * (h % 4) + 128], XT[:, h, :], Y[:, h, :],
                                                 start=False, stop=False, skip_group_check=True)
                            ins.then_inc(ev("x_made"), 1)
                        for h in range(4 * g, 4 * g + 4):
                            ins = eng.matmul(P[2 + g][:, 128 * (h % 4):128 * (h % 4) + 128], Y[:, h, :], XT[:, h, :],
                                             start=False, stop=(lv == N_LEVELS - 1 and h % 4 == 3), skip_group_check=True)
                        ins.then_inc(ev("xt_made"), 1)
                eng.wait_ge(ev("xt_kept"), i * 10 + 9)
                for g in range(2):
                    if g:
                        eng.wait_ge(ev("xt_kept"), i * 10 + 10)
                    for h in range(4 * g, 4 * g + 4):
                        ins = eng.matmul(P[g][:, 128 * (h % 4):128 * (h % 4) + 128], LM[:, h, 1, :], XT[:, h, :],
                                         start=(h % 4 == 0), stop=(h % 4 == 3), skip_group_check=True)
                    ins.then_inc(ev("mx_made"), 1)
                for h in range(8):
                    o = slice(64 * (h % 2), 64 * (h % 2) + 64)
                    ins = eng.matmul(P[4][o, 128 * (h // 2):128 * (h // 2) + 128], tok[:, 1, 64 * h:64 * h + 64], XT[:, h, :],
                                     start=(h < 2), stop=(h >= 6), skip_group_check=True)
                ins.then_inc(ev("ax_made"), 1)
                eng.wait_ge(ev("v_kept"), i + 1)
                for h in range(8):
                    eng.matmul(P[3][:, 64 * h:64 * h + 64], KR[:, h, :], tok[:, 0, 64 * h:64 * h + 64],
                               start=(h == 0), stop=False, skip_group_check=True)
                eng.wait_ge(ev("mx_kept"), i + 1)
                for h in range(8):
                    eng.matmul(P[2][:, 64 * h:64 * h + 64], MX[:, h, :], tok[:, 0, 64 * h:64 * h + 64],
                               start=(h == 0), stop=False, skip_group_check=True)
                eng.wait_ge(ev("ax_kept"), i + 1)
                for c in range(2):
                    r = slice(CH * c, CH * c + CH)
                    if c or not running:
                        eng.wait_ge(ev("st_updated"), i * 2 + c)
                    for m in range(4):
                        o = slice(128 * m, 128 * m + 128)
                        ins = eng.matmul(P[2][r, o], XA[:, m, r], ST[:, c, m, :], start=False, stop=(m == 3), skip_group_check=True)
                    ins.then_inc(ev("sa_made"), 1)
                    for m in range(4):
                        o = slice(128 * m, 128 * m + 128)
                        eng.matmul(P[c][:, o], tok[r, 3, o], tok[r, 0, o], start=(m == 0), stop=False, skip_group_check=True)
                    for m in range(4):
                        o = slice(128 * m, 128 * m + 128)
                        eng.matmul(P[3][r, o], AR[:, m, 1, r], ST[:, c, m, :], start=False, stop=False, skip_group_check=True)
                    eng.wait_ge(ev("sa_kept"), i * 2 + c + 1)
                    for m in range(4):
                        o = slice(128 * m, 128 * m + 128)
                        ins = eng.matmul(P[c][:, o], tok[r, 2, o], SA[r, o], start=False, stop=(m == 3), skip_group_check=True)
                    ins.then_inc(ev("st_made"), 1)
                for h in range(8):
                    ins = eng.matmul(P[3][:, 64 * h:64 * h + 64], LB[:, h, 1, :], SA[:, 64 * h:64 * h + 64],
                                     start=False, stop=(h == 7), skip_group_check=True)
                ins.then_inc(ev("y_out_made"), 1)
                if running:
                    eng.wait_ge(ev("st_updated"), i * 2 + 2)
                    for c in range(2):
                        for y in range(4):
                            ins = eng.transpose(P[4 + c][:, 128 * y:128 * y + 128], ST[:, 2 + c, y, :], ident)
                    ins.then_inc(ev("st_back_made"), 1)
            if not running:
                eng.wait_ge(ev("st_updated"), 2 * n_tiles)
                for y in range(4):
                    ins = eng.transpose(P[4][:, 128 * y:128 * y + 128], ST[:, 0, y, :], ident)
                ins.then_inc(ev("st_back_made"), 1)

        @block.scalar
        def _(eng):
            eng.wait_ge(ev("one_made"), 1)
            eng.wait_ge(ev("zeroed"), n_zeroed)
            for _ in h_prep_scalar(eng, None, 0):
                pass
            with eng.Fori(0, n_tiles) as i:
                eng.wait_ge(ev("tl_ready"), i + 1)
                eng.activation(te[0:64, 0, :], tl[0:64, 0, :], ACT.Exp, scale=-2.0)
                eng.activation(te[:, 1, :], tl[:, 1, :], ACT.Exp, scale=-1.0).then_inc(ev("te_ready"), 1)
                eng.wait_ge(ev("kd_turned"), i + 1)
                eng.copy(kdT[:, :, :].rearrange("p a b -> p (a b)"), P[3][:, :]).then_inc(ev("kd_kept"), 1)
                eng.wait_ge(ev("u_ready"), i + 1)
                eng.activation(u[:, :, :], u[:, :, :], ACT.Exp, scale=-1.0).then_inc(ev("u_exp"), 1)
                eng.wait_ge(ev("gate_made"), i + 1)
                eng.copy(gate[:, :], P[2][:, :]).then_inc(ev("gate_read"), 1)
                eng.wait_ge(ev("cs_ready"), i + 1)
                eng.activation(e1[:, :, :], cs[:, :, :], ACT.Exp, scale=-DECAY)
                eng.activation(e2[:, :, :], cs[:, :, :], ACT.Exp, scale=DECAY)
                eng.activation(e3[:, :, :], cx[:, :, :], ACT.Exp, scale=-DECAY).then_inc(ev("e_ready"), 1)
                eng.wait_ge(ev("norm_max"), i + 1)
                eng.activation(sq[:, :, :], sq[:, :, :], ACT.Sqrt).then_inc(ev("norm_root"), 1)
                eng.wait_ge(ev("h_used"), i + 1)
                eng.activation(osq[:, :], P[7][:, :], ACT.Square).then_inc(ev("o_squared"), 1)
                eng.wait_ge(ev("o_var"), i + 1)
                eng.activation(hst[:, 1, :], hst[:, 1, :], ACT.Ln).then_inc(ev("a_o1"), 1)
                eng.wait_ge(ev("a_o1"), i + 1)
                eng.activation(hst[:, 1, :], hst[:, 1, :], ACT.Exp, scale=-0.5).then_inc(ev("o_scale"), 1)
                if running:
                    for c in range(2):
                        eng.wait_ge(ev("st_turned"), i * 2 + c + 1)
                        eng.copy(ST[:, c, :, :].rearrange("p b c -> p (b c)"), P[3 - c][:, :]).then_inc(ev("st_kept"), 1)
                eng.wait_ge(ev("v_turned"), i + 1)
                eng.copy(tok[:, 0, :], P[0][:, :]).then_inc(ev("v_kept"), 1)
                for n in range(3):
                    eng.wait_ge(ev("tok_turned"), i * 3 + n + 1)
                    ins = eng.copy(tok[:, 1 + n, :], P[1 + n][:, :])
                ins.then_inc(ev("tok_kept"), 1)
                prep = h_prep_scalar(eng, i, 1)
                for lv in range(1, N_LEVELS):
                    k = lv - 1
                    for g in range(2):
                        if lv < N_LEVELS - 1:
                            eng.wait_ge(ev("x_made"), i * 8 + 2 * k + g + 1)
                            eng.copy(X[:, 4 * g:4 * g + 4, :].rearrange("p a b -> p (a b)"), P[g][:, :]).then_inc(ev("x_kept"), 1)
                        eng.wait_ge(ev("xt_made"), i * 10 + 2 * k + g + 1)
                        eng.copy(XT[:, 4 * g:4 * g + 4, :].rearrange("p a b -> p (a b)"), P[2 + g][:, :]).then_inc(ev("xt_kept"), 1)
                    if lv in (1, 2, 4):
                        next(prep)
                for g in range(2):
                    eng.wait_ge(ev("mx_made"), i * 2 + g + 1)
                    ins = eng.copy(MX[:, 4 * g:4 * g + 4, :].rearrange("p a b -> p (a b)"), P[g][:, :])
                ins.then_inc(ev("mx_kept"), 1)
                for c in range(2):
                    r = slice(CH * c, CH * c + CH)
                    eng.wait_ge(ev("sa_made"), i * 2 + c + 1)
                    eng.copy(SA[r, :], P[2][r, :]).then_inc(ev("sa_kept"), 1)
                if running:
                    eng.wait_ge(ev("st_back_made"), i + 1)
                    for c in range(2):
                        for g in range(2):
                            o = slice(64 * g, 64 * g + 64)
                            ins = eng.copy(sout[o, c, :, :], heads(P[4 + c][:, :])[o, :, o])
                    ins.then_inc(ev("st_turned_back"), 1)
                eng.wait_ge(ev("y_centred"), i + 1)
                eng.activation(ysq[:, :], yc[:, :], ACT.Square).then_inc(ev("y_squared"), 1)
                eng.wait_ge(ev("y_var"), i + 1)
                eng.activation(rst[:, 2, :], rst[:, 1, :], ACT.Ln).then_inc(ev("a_y1"), 1)
                eng.wait_ge(ev("a_y1"), i + 1)
                eng.activation(rst[:, 2, :], rst[:, 2, :], ACT.Exp, scale=-0.5).then_inc(ev("y_scale"), 1)
            if not running:
                eng.wait_ge(ev("st_back_made"), 1)
                for g in range(2):
                    o = slice(64 * g, 64 * g + 64)
                    ins = eng.copy(sout[o, 0, :, :], heads(P[4][:, :])[o, :, o])
                ins.then_inc(ev("st_turned_back"), 1)

        @block.vector
        def _(eng):
            count = 0
            vstep = ev("vector_step")

            def step(ins):
                nonlocal count
                count += 1
                ins.then_inc(vstep, 1)

            def settle():
                eng.wait_ge(vstep, count)

            def restart():
                nonlocal count
                settle()
                eng.sem_clear(vstep)
                count = 0

            pad4 = cm(C_PAD).unsqueeze(1).to_broadcast([128, 4, 128])
            eng.wait_ge(ev("prm_turned"), 1)
            eng.tensor_copy(prm[:, :], P[0][:, 0:N_PRM]).then_inc(ev("prm_ready"), 1)
            eng.wait_ge(ev("prm_ready"), 1)
            eng.wait_ge(ev("zeroed"), n_zeroed)
            for _ in h_prep_vector(eng, None, 0, step, settle):
                pass
            restart()
            with eng.Fori(0, n_tiles) as i:
                eng.wait_ge(ev("shifted"), i + 1)
                eng.tensor_tensor(tl[:, :, :], rin[:, 12:14, 1:129], rin[:, 14:16, 0:128], ALU.add).then_inc(ev("tl_ready"), 1)
                eng.wait_ge(ev("tl_ready"), i + 1)
                for c in range(12):
                    ins = eng.scalar_tensor_tensor(pm[:, c, :], pm[:, c, :], prm[:, c:c + 1], rin[:, c, 1:129], ALU.mult, ALU.add)
                ins.then_inc(ev("mixed_rkv"), 1)
                eng.wait_ge(ev("mixed_rkv"), i + 1)
                eng.sem_inc(ev("r_used"), 1)
                eng.wait_ge(ev("te_ready"), i + 1)
                step(eng.tensor_scalar(te[0:64, 0, :], te[0:64, 0, :], 1.0, None, ALU.add))
                step(eng.tensor_scalar(te[:, 1, :], te[:, 1, :], 1.0, None, ALU.add))
                settle()
                step(eng.reciprocal(te[0:64, 0, :], te[0:64, 0, :]))
                step(eng.reciprocal(te[:, 1, :], te[:, 1, :]))
                step(eng.tensor_copy(te[64:128, 0, :], tl[64:128, 0, :]))
                settle()
                eng.tensor_scalar(te[0:64, 0, :], te[0:64, 0, :], 2.0, -1.0, ALU.mult, ALU.add).then_inc(ev("lora_ready"), 1)
                step(eng.tensor_tensor(kr[:, :, :], pm[:, 4:8, :], column("kk"), ALU.mult))
                settle()
                eng.tensor_tensor(sq[:, :, :], kr[:, :, :], kr[:, :, :], ALU.mult).then_inc(ev("k_squared"), 1)
                for n in range(1 + N_LEVELS):
                    eng.wait_ge(ev("score_made"), i * 7 + n + 1)
                    eng.sem_inc(ev("score_seen"), 1)
                    bank = heads(P[4 + n % 2][:, :])
                    if n == 0:
                        eng.tensor_tensor(at_[:, :, :], bank, ident.unsqueeze(1).to_broadcast([128, 4, 128]), ALU.mult).then_inc(ev("scored"), 1)
                    else:
                        eng.wait_ge(ev("scored"), i * 7 + n)
                        eng.sem_inc(ev("score_seen"), 1)
                        eng.copy_predicated(at_[:, :, :], cm(C_LEVEL + n - 1).bitcast(U32).unsqueeze(1).to_broadcast([128, 4, 128]), bank).then_inc(ev("scored"), 1)
                eng.wait_ge(ev("wa_made"), i + 1)
                step(eng.tensor_tensor(u[:, 0:4, :], heads(P[0][:, :]), column("w0"), ALU.add))
                eng.tensor_tensor(u[:, 4:8, :], heads(P[1][:, :]), column("a0"), ALU.add).then_inc(ev("wa_read"), 1)
                eng.wait_ge(ev("wa_read"), i + 1)
                settle()
                eng.sem_inc(ev("u_ready"), 1)
                eng.wait_ge(ev("u_exp"), i + 1)
                step(eng.tensor_scalar(u[:, :, :], u[:, :, :], 1.0, None, ALU.add))
                settle()
                step(eng.reciprocal(u[:, :, :], u[:, :, :]))
                settle()
                if running:
                    step(eng.tensor_tensor(u[:, 0:4, :], u[:, 0:4, :], pad4, ALU.mult))
                    settle()
                step(eng.tensor_tensor_scan(cs[:, :, :].rearrange("p a b -> p (a b)"), reset[:, :, :, :].rearrange("p a b c -> p (a b c)"),
                                            u[:, 0:4, :].rearrange("p a b -> p (a b)"), 0.0, ALU.mult, ALU.add))
                settle()
                eng.tensor_tensor(cx[:, :, :], cs[:, :, :], u[:, 0:4, :], ALU.subtract).then_inc(ev("cs_ready"), 1)
                eng.wait_ge(ev("norm_made"), i + 1)
                eng.tensor_scalar(sq[:, :, :], heads(P[6][:, :]), 1e-24, None, ALU.max).then_inc(ev("norm_max"), 1)
                eng.wait_ge(ev("norm_max"), i + 1)
                eng.sem_inc(ev("norm_read"), 1)
                step(eng.scalar_tensor_tensor(kn[:, :, :], u[:, 4:8, :], -1.0, column("ka"), ALU.add, ALU.mult))
                settle()
                step(eng.scalar_tensor_tensor(kn[:, :, :], kn[:, :, :], 1.0, pm[:, 4:8, :], ALU.add, ALU.mult))
                settle()
                if running:
                    step(eng.tensor_tensor(kn[:, :, :], kn[:, :, :], pad4, ALU.mult))
                    settle()
                step(eng.tensor_tensor(bon[:, :, :], kn[:, :, :], pm[:, 0:4, :], ALU.mult))
                settle()
                step(eng.tensor_tensor(bon[:, :, :], bon[:, :, :], column("rk"), ALU.mult))
                for c in range(2):
                    eng.wait_ge(ev("h_update_made"), i * 2 + c + 1)
                    if running and c == 0:
                        eng.wait_ge(ev("s_in"), i * 96 + 96)
                    to = 2 + c if running else 1 - c
                    for h in range(4):
                        ins = eng.scalar_tensor_tensor(S[:, to, h, :], S[:, c, h, :], hdec[:, h, c:c + 1],
                                                       P[4 + c][:, 128 * h:128 * h + 128], ALU.mult, ALU.add)
                    ins.then_inc(ev("h_updated"), 1)
                    if not running:
                        eng.wait_ge(ev("h_updated"), i * 2 + c + 1)
                eng.wait_ge(ev("norm_root"), i + 1)
                step(eng.reciprocal(sq[:, :, :], sq[:, :, :]))
                settle()
                step(eng.tensor_tensor(kr[:, :, :], kr[:, :, :], sq[:, :, :], ALU.mult))
                settle()
                if running:
                    step(eng.tensor_tensor(kr[:, :, :], kr[:, :, :], pad4, ALU.mult))
                    settle()
                eng.wait_ge(ev("e_ready"), i + 1)
                step(eng.scalar_tensor_tensor(AR[:, :, 0, :], kr[:, :, :], -1.0, e3[:, :, :], ALU.mult, ALU.mult))
                step(eng.tensor_tensor(AR[:, :, 1, :], pm[:, 0:4, :], e1[:, :, :], ALU.mult))
                step(eng.tensor_tensor(BK[:, :, 1, :], kn[:, :, :], e2[:, :, :], ALU.mult))
                step(eng.tensor_tensor(kr[:, :, :], kr[:, :, :], u[:, 4:8, :], ALU.mult))
                for c in range(2):
                    step(eng.tensor_tensor(wm[:, c, :, :], cm(C_HEAD).unsqueeze(1).to_broadcast([128, 4, 128]),
                                           e1[:, :, CH * c + CH - 1:CH * c + CH].to_broadcast([128, 4, 128]), ALU.mult))
                settle()
                eng.tensor_tensor(BK[:, :, 0, :], kr[:, :, :], e2[:, :, :], ALU.mult).then_inc(ev("rw_ready"), 1)
                eng.wait_ge(ev("o_squared"), i + 1)
                step(eng.tensor_reduce(hst[:, 0, :], heads(osq[:, :]), AX.X, ALU.add))
                settle()
                eng.tensor_scalar(hst[:, 1, :], hst[:, 0, :], 1.0 / 128, NORM_EPS, ALU.mult, ALU.add).then_inc(ev("o_var"), 1)
                step(eng.tensor_tensor(gs[:, :], gs[:, :], rows[:, 0, :], ALU.mult))
                eng.wait_ge(ev("o_scale"), i + 1)
                eng.wait_ge(ev("mix_out"), i * (32 if running else 16))
                step(eng.tensor_tensor(heads(mix[:, 0:512]), heads(P[7][:, :]), hst[:, 1, :].unsqueeze(2).to_broadcast([128, 4, 128]), ALU.mult))
                settle()
                eng.tensor_tensor(mix[:, 0:512], mix[:, 0:512], gs[:, :], ALU.mult).then_inc(ev("h_mixed"), 1)
                n = 0
                banks = [4, 5, 0, 3]
                masks = (const[:, C_STRICT:C_STRICT + 2, :], const[:, C_LOWER:C_LOWER + 2, :])
                for pairs in range(2):
                    for kind, j in ((0, 0), (0, 1), (1, 0), (1, 1)):
                        eng.wait_ge(ev("product_made"), i * 10 + n + 1)
                        out = (LB, LM)[kind][:, 4 * pairs + j:4 * pairs + j + 3:2, :, :]
                        m = masks[kind].rearrange("p a b -> p (a b)").unsqueeze(1).to_broadcast([128, 2, 256])
                        eng.tensor_tensor(out.rearrange("p h a b -> p h (a b)"), P[banks[n % 4]][:, :].rearrange("p (h c) -> p h c", h=2),
                                          m, ALU.mult).then_inc(ev("product_kept"), 1)
                        n += 1
                eng.wait_ge(ev("product_kept"), i * 10 + n)
                for kind, x, lv in ((1, X, C_LEVEL_T), (0, XT, C_LEVEL)):
                    src = (LB, LM)[kind][:, :, 0, :]
                    step(eng.tensor_tensor(x[:, :, :], src, cm(lv).unsqueeze(1).to_broadcast([128, 8, 128]), ALU.mult))
                settle()
                for x in (X, XT):
                    step(eng.tensor_tensor(x[:, :, :], x[:, :, :], ident.unsqueeze(1).to_broadcast([128, 8, 128]), ALU.add))
                settle()
                eng.sem_inc(ev("x_begun"), 1)
                for g in range(2):
                    eng.wait_ge(ev("product_made"), i * 10 + n + 1)
                    eng.tensor_tensor(KR[:, g:8:2, :], heads(P[banks[n % 4]][:, :]),
                                      cm(C_INCL).unsqueeze(1).to_broadcast([128, 4, 128]), ALU.mult).then_inc(ev("product_kept"), 1)
                    n += 1
                eng.wait_ge(ev("bonus_made"), i + 1)
                step(eng.tensor_copy(bonus[:, :], P[6][:, 0:8]))
                prep = h_prep_vector(eng, i, 1, step, settle)
                for lv in range(1, N_LEVELS):
                    k = lv - 1
                    for g in range(2):
                        eng.wait_ge(ev("y_made"), i * 10 + 2 * k + g + 1)
                        eng.tensor_tensor(Y[:, 4 * g:4 * g + 4, :], heads(P[4 + g][:, :]),
                                          cm(C_LEVEL_T + lv).unsqueeze(1).to_broadcast([128, 4, 128]), ALU.mult).then_inc(ev("y_kept"), 1)
                    if lv >= 2:
                        next(prep)
                eng.wait_ge(ev("ax_made"), i + 1)
                eng.tensor_copy(XA[:, :, :], heads(P[4][:, :])).then_inc(ev("ax_kept"), 1)
                for c in range(2):
                    eng.wait_ge(ev("st_made"), i * 2 + c + 1)
                    to = 2 + c if running else 1 - c
                    if running:
                        eng.wait_ge(ev("st_kept"), i * 2 + 2)
                    step(eng.tensor_tensor(ST[:, to, :, :], ST[:, c, :, :], heads(P[c][:, :]), ALU.add))
                    settle()
                    eng.tensor_tensor(ST[:, to, :, :], ST[:, to, :, :], wm[:, c, :, :], ALU.mult).then_inc(ev("st_updated"), 1)
                    if not running:
                        eng.wait_ge(ev("st_updated"), i * 2 + c + 1)
                eng.wait_ge(ev("y_out_made"), i + 1)
                y8 = heads(P[3][:, :], 8)

                def by_head(x):
                    return x.unsqueeze(2).to_broadcast([128, 8, RW_N])

                step(eng.tensor_reduce(rst[:, 0, :], y8, AX.X, ALU.add))
                settle()
                step(eng.tensor_scalar(rst[:, 0, :], rst[:, 0, :], 1.0 / RW_N, None, ALU.mult))
                settle()
                eng.tensor_tensor(heads(yc[:, :], 8), y8, by_head(rst[:, 0, :]), ALU.subtract).then_inc(ev("y_centred"), 1)
                eng.wait_ge(ev("y_squared"), i + 1)
                eng.sem_inc(ev("p_mix_read"), 1)
                step(eng.tensor_reduce(rst[:, 1, :], heads(ysq[:, :], 8), AX.X, ALU.add))
                settle()
                step(eng.tensor_tensor(heads(ysq[:, :], 8), heads(tok[:, 0, :], 8), by_head(bonus[:, :]), ALU.mult))
                eng.tensor_scalar(rst[:, 1, :], rst[:, 1, :], 1.0 / RW_N, GN_EPS, ALU.mult, ALU.add).then_inc(ev("y_var"), 1)
                eng.wait_ge(ev("y_scale"), i + 1)
                step(eng.tensor_tensor(heads(yc[:, :], 8), heads(yc[:, :], 8), by_head(rst[:, 2, :]), ALU.mult))
                settle()
                step(eng.tensor_tensor(yc[:, :], yc[:, :], rows[:, 1, :], ALU.mult))
                step(eng.tensor_tensor(ysq[:, :], ysq[:, :], rows[:, 2, :], ALU.add))
                settle()
                step(eng.tensor_tensor(yc[:, :], yc[:, :], ysq[:, :], ALU.add))
                settle()
                eng.tensor_tensor(mix[:, 512:1024], yc[:, :], gate[:, :], ALU.mult).then_inc(ev("mixed"), 1)
                restart()
    finish(nc, names)


N_GROUPS, PER_GROUP = 4, 8
N_EXPERTS = N_GROUPS * PER_GROUP
TOP_K = 2
D_EXPERT = 512
BLOCK = 128
MAX_BLOCKS = T * TOP_K // BLOCK + N_EXPERTS
LOWEST = -3.0e38


def merge(nc, t, expert, gates):
    names = []
    with ExitStack() as ctx:
        def sb(name, shape, dt=F32):
            return ctx.enter_context(nc.sbuf_tensor("merge_" + name, shape, dt))

        sems = {}

        def ev(name):
            if name not in sems:
                sems[name] = sem_of(nc, names, "merge_" + name)
            return sems[name]

        NR = N_GROUPS + N_EXPERTS
        w = sb("w", [128, KD, D])
        wr = sb("wr", [128, KD, NR])
        wr_bias = sb("wr_bias", [128, NR])
        maps = sb("maps", [128, 2, 3, D])
        ident = sb("ident", [128, 128])
        iota = sb("iota", [128, N_EXPERTS])
        m_in = sb("m_in", [128, 2, D])
        x = sb("x", [128, 2, D])
        mT = sb("mT", [128, KD, 128])
        x1 = sb("x1", [128, 2, D])
        h2 = sb("h2", [128, 2, D])
        h2T = sb("h2T", [128, KD, 128])
        stat = sb("stat", [128, 4])
        lg = sb("lg", [128, NR])
        g8 = sb("g8", [128, 8])
        top = sb("top", [128, 2, 8])
        idx = sb("idx", [128, 2, 8], U32)
        idf = sb("idf", [128, 4])
        sel = sb("sel", [128, N_GROUPS])
        pick = sb("pick", [128, N_GROUPS, PER_GROUP])
        es = sb("es", [128, PER_GROUP])
        ex = sb("ex", [128, 8])
        PT0 = ctx.enter_context(nc.psum_tensor("merge_PT0", [128, KD, 128], F32))
        PT1 = ctx.enter_context(nc.psum_tensor("merge_PT1", [128, KD, 128], F32))
        PO = ctx.enter_context(nc.psum_tensor("merge_PO", [128, 2, 512], F32))
        PR = ctx.enter_context(nc.psum_tensor("merge_PR", [128, 512], F32))

        block = ctx.enter_context(nc.Block())
        LOOP = (NT - 3) // 2

        def tiles(eng, body):
            body(None, 0)
            with eng.Fori(0, LOOP) as i:
                body(i, 1)
                body(i, 2)
            for n in range(2 * LOOP + 1, NT):
                body(None, n)

        @block.sync
        def _(eng):
            eng.dma_start(ident[:, :], t["const"][:, 0:128]).then_inc(ev("w_in"), 16)
            eng.dma_start(w[:, :, :], t["w_out"][0].rearrange("(k p) n -> p k n", p=128)).then_inc(ev("w_in"), 16)
            eng.dma_start(wr[:, :, 0:N_GROUPS], t["router_g_w"][0].rearrange("(k p) n -> p k n", p=128)).then_inc(ev("w_in"), 16)
            for g in range(N_GROUPS):
                c = N_GROUPS + PER_GROUP * g
                eng.dma_start(wr[:, :, c:c + PER_GROUP], t["router_e_w"][0, g].rearrange("(k p) n -> p k n", p=128)).then_inc(ev("w_in"), 16)
            eng.dma_start(wr_bias[:, 0:N_GROUPS], t["router_g_b"].to_broadcast([128, N_GROUPS])).then_inc(ev("w_in"), 16)
            eng.dma_start(wr_bias[:, N_GROUPS:NR], t["router_e_b"].rearrange("a g e -> a (g e)").to_broadcast([128, N_EXPERTS])).then_inc(ev("w_in"), 16)
            eng.dma_start(iota[:, :], t["iota"]).then_inc(ev("w_in"), 16)
            for n, row in enumerate((GATE1, SCALE2, SHIFT2)):
                eng.dma_start(maps[:, 0, n, :], t["mods"][0:1, row * D:row * D + D].to_broadcast([128, D])).then_inc(ev("w_in"), 16)
                for s in range(NSEQ):
                    eng.dma_start(maps[DEC * s:DEC * s + DEC, 1, n, :],
                                  t["mods"][1 + s:2 + s, row * D:row * D + D].to_broadcast([DEC, D])).then_inc(ev("w_in"), 16)

            def load(i, n):
                p = n % 2
                if n >= 2:
                    eng.wait_ge(ev("m_turned"), at(i, 2, n - 1))
                    eng.wait_ge(ev("x1_ready"), at(i, 2, n - 1))
                k = n * 128 if i is None else i * 256 + n * 128
                if i is None and n == NT - 1:
                    src = t["x_sample"].rearrange("b t d -> (b t) d")
                else:
                    src = t["x_prompt"][0, ds(k, 128), :]
                eng.dma_start(m_in[:, p, :], t["mix"][ds(k, 128), :]).then_inc(ev(f"m_in{p}"), 16)
                eng.dma_start(x[:, p, :], src).then_inc(ev(f"x_in{p}"), 16)

            def store(i, n):
                p = n % 2
                k = n * 128 if i is None else i * 256 + n * 128
                eng.wait_ge(ev("x1_ready"), at(i, 2, n + 1))
                eng.dma_start(t["x1"][ds(k, 128), :], x1[:, p, :]).then_inc(ev(f"x1_out{p}"), 16)
                eng.wait_ge(ev("h2_ready"), at(i, 2, n + 1))
                eng.dma_start(t["h2"][ds(k, 128), :], h2[:, p, :]).then_inc(ev(f"h2_out{p}"), 16)

            def body(i, n):
                if not (i is None and n == NT - 1):
                    load(i, n + 1)
                store(i, n)

            load(None, 0)
            tiles(eng, body)
            for p in range(2):
                eng.wait_ge(ev(f"x1_out{p}"), 16 * ((NT + 1 - p) // 2))
                eng.wait_ge(ev(f"h2_out{p}"), 16 * ((NT + 1 - p) // 2))

        @block.tensor
        def _(eng):
            eng.wait_ge(ev("w_in"), 16 * (10 + 3 * (1 + NSEQ)))

            def turn_m(i, n):
                eng.wait_ge(ev(f"m_in{n % 2}"), at(i, 16, 16 * (n // 2 + 1)))
                if n:
                    eng.wait_ge(ev("mT_kept"), at(i, 4, 2 * n))
                for k in range(KD):
                    ins = eng.transpose(PT0[:, k, :], m_in[:, n % 2, 128 * k:128 * k + 128], ident[:, :])
                ins.then_inc(ev("m_turned"), 1)

            def out(i, n):
                eng.wait_ge(ev("mT_kept"), at(i, 4, 2 * n + 2))
                if n:
                    eng.wait_ge(ev("out_read"), at(i, 2, n))
                for half in range(2):
                    for k in range(KD):
                        ins = eng.matmul(PO[:, half, :], mT[:, k, :], w[:, k, 512 * half:512 * half + 512],
                                         start=(k == 0), stop=(k == KD - 1))
                ins.then_inc(ev("out_made"), 1)

            def route(i, n):
                eng.wait_ge(ev("h2_ready"), at(i, 2, n + 1))
                if n:
                    eng.wait_ge(ev("h2T_kept"), at(i, 2, n))
                for k in range(KD):
                    ins = eng.transpose(PT1[:, k, :], h2[:, n % 2, 128 * k:128 * k + 128], ident[:, :])
                ins.then_inc(ev("h2_turned"), 1)
                eng.wait_ge(ev("h2T_kept"), at(i, 2, n + 1))
                if n:
                    eng.wait_ge(ev("logits_read"), at(i, 2, n))
                for k in range(KD):
                    ins = eng.matmul(PR[:, 0:NR], h2T[:, k, :], wr[:, k, :], start=(k == 0), stop=(k == KD - 1))
                ins.then_inc(ev("logits_made"), 1)

            def body(i, n):
                out(i, n)
                if not (i is None and n == NT - 1):
                    turn_m(i, n + 1)
                if n:
                    route(i, n - 1)

            turn_m(None, 0)
            tiles(eng, body)
            route(None, NT - 1)

        @block.scalar
        def _(eng):
            def body(i, n):
                eng.wait_ge(ev("m_turned"), at(i, 2, n + 1))
                if n:
                    eng.wait_ge(ev("out_made"), at(i, 2, n))
                for half in range(2):
                    eng.copy(mT[:, 4 * half:4 * half + 4, :], PT0[:, 4 * half:4 * half + 4, :]).then_inc(ev("mT_kept"), 1)
                eng.wait_ge(ev("x1_ready"), at(i, 2, n + 1))
                if n >= 2:
                    eng.wait_ge(ev(f"h2_out{n % 2}"), at(i, 16, 16 * (n // 2)))
                    eng.wait_ge(ev("h2_turned"), at(i, 2, n - 1))
                eng.activation(h2[:, n % 2, :], x1[:, n % 2, :], ACT.Square, accum_out=stat[:, 0:1]).then_inc(ev("squared"), 1)
                eng.wait_ge(ev("var_ready"), at(i, 2, n + 1))
                eng.activation(stat[:, 2:3], stat[:, 1:2], ACT.Sqrt).then_inc(ev("root_ready"), 1)
                if n:
                    back(i, n - 1)

            def back(i, n):
                eng.wait_ge(ev("h2_turned"), at(i, 2, n + 1))
                if n:
                    eng.wait_ge(ev("logits_made"), at(i, 2, n))
                for half in range(2):
                    ins = eng.copy(h2T[:, 4 * half:4 * half + 4, :], PT1[:, 4 * half:4 * half + 4, :])
                ins.then_inc(ev("h2T_kept"), 1)
                eng.wait_ge(ev("ex_ready"), at(i, 2, n + 1))
                eng.activation(ex[:, 0:5], ex[:, 0:5], ACT.Exp).then_inc(ev("ex_made"), 1)

            tiles(eng, body)
            back(None, NT - 1)

        @block.vector
        def _(eng):
            count = 0
            vstep = ev("vector_step")

            def step(ins):
                nonlocal count
                count += 1
                ins.then_inc(vstep, 1)

            def settle():
                eng.wait_ge(vstep, count)

            def restart():
                nonlocal count
                settle()
                eng.sem_clear(vstep)
                count = 0

            def norm(i, n):
                p = n % 2
                m = maps[:, 1 if i is None and n == NT - 1 else 0, :, :]
                eng.wait_ge(ev("out_made"), at(i, 2, n + 1))
                if n >= 2:
                    eng.wait_ge(ev(f"x1_out{p}"), at(i, 16, 16 * (n // 2)))
                eng.tensor_tensor(x1[:, p, :], PO[:, :, :].rearrange("p a b -> p (a b)"), m[:, 0, :], ALU.mult).then_inc(ev("out_read"), 1)
                eng.wait_ge(ev("out_read"), at(i, 2, n + 1))
                eng.wait_ge(ev(f"x_in{p}"), at(i, 16, 16 * (n // 2 + 1)))
                eng.tensor_tensor(x1[:, p, :], x1[:, p, :], x[:, p, :], ALU.add).then_inc(ev("x1_ready"), 1)
                eng.wait_ge(ev("squared"), at(i, 2, n + 1))
                eng.tensor_scalar(stat[:, 1:2], stat[:, 0:1], 1.0 / D, NORM_EPS, ALU.mult, ALU.add).then_inc(ev("var_ready"), 1)
                eng.wait_ge(ev("root_ready"), at(i, 2, n + 1))
                step(eng.reciprocal(stat[:, 3:4], stat[:, 2:3]))
                settle()
                step(eng.scalar_tensor_tensor(h2[:, p, :], x1[:, p, :], stat[:, 3:4], m[:, 1, :], ALU.mult, ALU.mult))
                settle()
                eng.tensor_tensor(h2[:, p, :], h2[:, p, :], m[:, 2, :], ALU.add).then_inc(ev("h2_ready"), 1)

            def route(i, n):
                tile = n if i is None else i * 2 + n
                eng.wait_ge(ev("logits_made"), at(i, 2, n + 1))
                eng.tensor_tensor(lg[:, :], PR[:, 0:NR], wr_bias[:, :], ALU.add).then_inc(ev("logits_read"), 1)
                eng.wait_ge(ev("logits_read"), at(i, 2, n + 1))
                step(eng.tensor_copy(g8[:, 0:N_GROUPS], lg[:, 0:N_GROUPS]))
                settle()
                step(eng.max(top[:, 0, :], g8[:, :]))
                settle()
                step(eng.max_index(idx[:, 0, :], top[:, 0, :], g8[:, :]))
                settle()
                step(eng.tensor_copy(idf[:, 0:1], idx[:, 0, 0:1]))
                settle()
                step(eng.tensor_scalar(sel[:, :], iota[:, 0:N_GROUPS], idf[:, 0:1], None, ALU.is_equal))
                settle()
                step(eng.tensor_tensor(pick[:, :, :], lg[:, N_GROUPS:NR].rearrange("p (g e) -> p g e", g=N_GROUPS),
                                       sel[:, :].unsqueeze(2).to_broadcast([128, N_GROUPS, PER_GROUP]), ALU.mult))
                settle()
                step(eng.tensor_reduce(es[:, :], pick[:, :, :].rearrange("p g e -> p e g"), AX.X, ALU.add))
                settle()
                step(eng.max(top[:, 1, :], es[:, :]))
                settle()
                step(eng.max_index(idx[:, 1, :], top[:, 1, :], es[:, :]))
                step(eng.tensor_scalar(ex[:, 0:4], lg[:, 0:N_GROUPS], top[:, 0, 0:1], None, ALU.subtract))
                settle()
                eng.tensor_tensor(ex[:, 4:5], top[:, 1, 1:2], top[:, 1, 0:1], ALU.subtract).then_inc(ev("ex_ready"), 1)
                step(eng.tensor_copy(idf[:, 2:4], idx[:, 1, 0:2]))
                settle()
                step(eng.scalar_tensor_tensor(expert[:, ds(tile, 1), :].rearrange("p a b -> p (a b)"), idf[:, 0:1].to_broadcast([128, 2]),
                                              float(PER_GROUP), idf[:, 2:4], ALU.mult, ALU.add))
                eng.wait_ge(ev("ex_made"), at(i, 2, n + 1))
                step(eng.tensor_reduce(ex[:, 5:6], ex[:, 0:4], AX.X, ALU.add))
                step(eng.tensor_scalar(ex[:, 6:7], ex[:, 4:5], 1.0, None, ALU.add))
                settle()
                step(eng.tensor_tensor(ex[:, 5:6], ex[:, 5:6], ex[:, 6:7], ALU.mult))
                settle()
                step(eng.reciprocal(ex[:, 7:8], ex[:, 5:6]))
                settle()
                g = gates[:, ds(tile, 1), :].rearrange("p a b -> p (a b)")
                step(eng.tensor_copy(g[:, 0:1], ex[:, 7:8]))
                step(eng.tensor_tensor(g[:, 1:2], ex[:, 7:8], ex[:, 4:5], ALU.mult))
                restart()

            def body(i, n):
                norm(i, n)
                if n:
                    route(i, n - 1)
                else:
                    restart()

            step(eng.memset(g8[:, :], LOWEST))
            eng.wait_ge(ev("w_in"), 16 * (10 + 3 * (1 + NSEQ)))
            tiles(eng, body)
            route(None, NT - 1)
    finish(nc, names)


def experts(nc, t, expert, gates):
    names = []
    with ExitStack() as ctx:
        def sb(name, shape, dt=F32):
            return ctx.enter_context(nc.sbuf_tensor("moe_" + name, shape, dt))

        sems = {}

        def ev(name):
            if name not in sems:
                sems[name] = sem_of(nc, names, "moe_" + name)
            return sems[name]

        NA = NT * TOP_K
        KE = D_EXPERT // 128
        wgu = sb("wgu", [128, 2, 2, KD, D_EXPERT])
        wd = sb("wd", [128, 2, KE, D])
        const = sb("const", [128, 3, 128])
        iota = sb("iota", [128, N_EXPERTS])
        tokens = sb("tokens", [128, NT, TOP_K], I32)
        onehot = sb("onehot", [128, NT, TOP_K, N_EXPERTS])
        member = sb("member", [128, NT, N_EXPERTS])
        carry = sb("carry", [128, NT + 1, N_EXPERTS])
        blocks_i = sb("blocks_i", [128, N_EXPERTS], I32)
        blocks_f = sb("blocks_f", [128, 2, N_EXPERTS])
        first_f = sb("first_f", [128, N_EXPERTS])
        table = sb("table", [128, 2, N_EXPERTS + 1], I32)
        dest_f = sb("dest_f", [128, NT, TOP_K])
        dest = sb("dest", [128, NT, TOP_K], I32)
        slots = sb("slots", [MAX_BLOCKS + 1, 128], I32)
        slots_f = sb("slots_f", [MAX_BLOCKS + 1, 128])
        rows = sb("rows", [128, MAX_BLOCKS + 1], I32)
        row = sb("row", [128, 2], I32)
        xg = sb("xg", [128, D])
        xT = sb("xT", [128, KD, 128])
        sg = sb("sg", [128, D_EXPERT])
        hid = sb("hid", [128, D_EXPERT])
        hT = sb("hT", [128, KE, 128])
        y = sb("y", [128, D])
        zeros = sb("zeros", [128, D])
        PT = ctx.enter_context(nc.psum_tensor("moe_PT", [128, KD, 128], F32))
        PG = ctx.enter_context(nc.psum_tensor("moe_PG", [128, 2, 512], F32))
        PH = ctx.enter_context(nc.psum_tensor("moe_PH", [128, KE, 128], F32))
        PY = ctx.enter_context(nc.psum_tensor("moe_PY", [128, 2, 512], F32))
        ident = const[:, 0, :]

        def total(eng):
            return eng.value_load(table[0:1, 1, N_EXPERTS:N_EXPERTS + 1], min_val=N_EXPERTS, max_val=MAX_BLOCKS)

        with nc.Block() as block:
            @block.sync
            def _(eng):
                for n, c in enumerate((C_ID, C_CUM, C_ONES)):
                    eng.dma_start(const[:, n, :], t["const"][:, 128 * c:128 * c + 128]).then_inc(ev("const_in"), 16)
                eng.dma_start(iota[:, :], t["iota"]).then_inc(ev("const_in"), 16)
                eng.dma_start(tokens[:, :, :].rearrange("p a b -> p (a b)"), t["token_ids"]).then_inc(ev("const_in"), 16)
                with eng.Fori(0, N_EXPERTS // 2) as i:
                    for p in range(2):
                        eng.wait_ge(ev("slot_free"), i * 2 + (p + 1))
                        for n, name in enumerate(("w_gate", "w_up")):
                            eng.dma_start(wgu[:, p, n, :, :], t[name][0, ds(i * 2 + p, 1)].rearrange("e (k p) n -> p (e k) n", p=128)).then_inc(ev(f"{name}_in{p}"), 16)
                        eng.dma_start(wd[:, p, :, :], t["w_down"][0, ds(i * 2 + p, 1)].rearrange("e (k p) n -> p (e k) n", p=128)).then_inc(ev(f"w_down_in{p}"), 16)

            @block.vector
            def _(eng):
                count = 0
                vstep = ev("vector_step")

                def step(ins):
                    nonlocal count
                    count += 1
                    ins.then_inc(vstep, 1)
                    eng.wait_ge(vstep, count)

                step(eng.memset(slots[:, :], 0))
                eng.sem_inc(ev("slots_zero"), 1)
                step(eng.memset(zeros[:, :], 0.0))
                step(eng.memset(carry[:, 0, :], 0.0))
                eng.wait_ge(ev("const_in"), 80)
                step(eng.tensor_tensor(onehot[:, :, :, :].rearrange("p a b e -> p (a b) e"), iota[:, :].unsqueeze(1).to_broadcast([128, NA, N_EXPERTS]),
                                       expert[:, :, :].rearrange("p a b -> p (a b)").unsqueeze(2).to_broadcast([128, NA, N_EXPERTS]), ALU.is_equal))
                step(eng.tensor_tensor(member[:, :, :], onehot[:, :, 0, :], onehot[:, :, 1, :], ALU.add))
                eng.sem_inc(ev("member_ready"), 1)
                eng.wait_ge(ev("counted"), 1)
                for n in range(NT):
                    src = PT[:, :, :].rearrange("p a b -> p (a b)")[:, 32 * n:32 * n + 32] if n < NT - 1 else PY[:, 0, 0:32]
                    step(eng.tensor_tensor(carry[:, n + 1, :], carry[:, n, :], src, ALU.add))
                step(eng.tensor_scalar(blocks_f[:, 0, :], carry[:, NT, :], float(BLOCK - 1), None, ALU.add))
                step(eng.tensor_copy(blocks_i[:, :], blocks_f[:, 0, :]))
                step(eng.tensor_scalar(blocks_i[:, :], blocks_i[:, :], 7, None, ALU.logical_shift_right))
                step(eng.tensor_copy(blocks_f[:, 0, :], blocks_i[:, :]))
                step(eng.tensor_scalar(blocks_f[:, 0, :], blocks_f[:, 0, :], 1.0, None, ALU.max))
                step(eng.tensor_copy(table[:, 0, 0:N_EXPERTS], blocks_f[:, 0, :]))
                step(eng.memset(blocks_f[:, 1, :], 1.0))
                step(eng.tensor_tensor_scan(first_f[:, :], blocks_f[:, 1, :], blocks_f[:, 0, :], 0.0, ALU.mult, ALU.add))
                step(eng.tensor_copy(table[:, 1, 1:N_EXPERTS + 1], first_f[:, :]))
                step(eng.memset(table[:, 1, 0:1], 0))
                step(eng.tensor_tensor(first_f[:, :], first_f[:, :], blocks_f[:, 0, :], ALU.subtract))
                eng.sem_inc(ev("table_ready"), 1)
                step(eng.tensor_scalar(first_f[:, :], first_f[:, :], float(BLOCK), -1.0, ALU.mult, ALU.add))
                step(eng.tensor_tensor(member[:, 0:NT - 1, :], carry[:, 0:NT - 1, :], PG[:, 0, :].rearrange("p (a e) -> p a e", e=N_EXPERTS), ALU.add))
                step(eng.tensor_tensor(member[:, NT - 1, :], carry[:, NT - 1, :], PG[:, 1, 0:N_EXPERTS], ALU.add))
                step(eng.tensor_tensor(member[:, :, :], member[:, :, :], first_f[:, :].unsqueeze(1).to_broadcast([128, NT, N_EXPERTS]), ALU.add))
                for j in range(TOP_K):
                    step(eng.tensor_tensor(onehot[:, :, j, :], onehot[:, :, j, :], member[:, :, :], ALU.mult))
                step(eng.tensor_reduce(dest_f[:, :, :].rearrange("p a b -> p (a b)"), onehot[:, :, :, :].rearrange("p a b e -> p (a b) e"), AX.X, ALU.add))
                step(eng.tensor_copy(dest[:, :, :], dest_f[:, :, :]))
                eng.sem_inc(ev("dest_ready"), 1)
                eng.wait_ge(ev("slots_in"), 16)
                step(eng.tensor_copy(slots_f[:, :], slots[:, :]))
                eng.sem_inc(ev("slots_ready"), 1)
                eng.wait_ge(ev("slots_turned"), 1)
                step(eng.tensor_copy(rows[:, :], PH[:, 0, 0:MAX_BLOCKS + 1]))
                eng.sem_inc(ev("rows_ready"), 1)

                with eng.Fori(0, total(eng)) as g:
                    eng.wait_ge(ev("x_turned"), g + 1)
                    eng.wait_ge(ev("gu_made"), g)
                    eng.tensor_copy(xT[:, 0:4, :], PT[:, 0:4, :]).then_inc(ev("xT_dve"), 1)
                    eng.wait_ge(ev("sigmoid_made"), g + 1)
                    eng.tensor_tensor(sg[:, :], sg[:, :], PG[:, 0, :], ALU.mult).then_inc(ev("silu_made"), 1)
                    eng.wait_ge(ev("gu_made"), g + 1)
                    eng.wait_ge(ev("silu_made"), g + 1)
                    eng.tensor_tensor(hid[:, :], sg[:, :], PG[:, 1, :], ALU.mult).then_inc(ev("hid_ready"), 1)
                    eng.wait_ge(ev("h_turned"), g + 1)
                    eng.tensor_copy(hT[:, :, :], PH[:, :, :]).then_inc(ev("hT_dve"), 1)
                    eng.wait_ge(ev("y_made"), g + 1)
                    eng.wait_ge(ev("y_out"), g * 16)
                    eng.tensor_copy(y[:, 0:512], PY[:, 0, :]).then_inc(ev("y_dve"), 1)

            @block.scalar
            def _(eng):
                eng.wait_ge(ev("table_ready"), 1)
                with eng.Fori(total(eng), MAX_BLOCKS + 1) as g:
                    eng.dma_start(t["y_rows"][ds(g * BLOCK, BLOCK), :], zeros[:, :]).then_inc(ev("row_blocks"), 16)
                with eng.Fori(0, total(eng)) as g:
                    eng.wait_ge(ev("x_turned"), g + 1)
                    eng.wait_ge(ev("gu_made"), g)
                    eng.copy(xT[:, 4:8, :], PT[:, 4:8, :]).then_inc(ev("xT_act"), 1)
                    eng.wait_ge(ev("g_made"), g + 1)
                    eng.wait_ge(ev("hid_ready"), g)
                    eng.activation(sg[:, :], PG[:, 0, :], ACT.Sigmoid).then_inc(ev("sigmoid_made"), 1)
                    eng.wait_ge(ev("y_made"), g + 1)
                    eng.wait_ge(ev("y_out"), g * 16)
                    eng.copy(y[:, 512:D], PY[:, 1, :]).then_inc(ev("y_act"), 1)
                    eng.wait_ge(ev("y_act"), g + 1)
                    eng.wait_ge(ev("y_dve"), g + 1)
                    eng.dma_start(t["y_rows"][ds(g * BLOCK, BLOCK), :], y[:, :]).then_inc(ev("y_out"), 16)
                    eng.sem_inc(ev("row_blocks"), 16)
                eng.wait_ge(ev("y_out"), total(eng) * 16)
                eng.sem_inc(ev("all_stored"), 1)
                eng.wait_ge(ev("row_blocks"), 16 * (MAX_BLOCKS + 1))

            @block.gpsimd
            def _(eng):
                eng.wait_ge(ev("slots_zero"), 1)
                eng.dma_start(t["slots"][:, :].rearrange("(b p) o -> b (p o)", p=BLOCK), slots[:, :]).then_inc(ev("slots_cleared"), 16)
                eng.wait_ge(ev("slots_cleared"), 16)
                eng.wait_ge(ev("dest_ready"), 1)
                for n in range(NT):
                    for j in range(TOP_K):
                        eng.indirect_dma_start(t["slots"][:, :], bass.IndirectOffsetOnAxis(ap=dest[:, n, j:j + 1], axis=0),
                                               tokens[:, n, j:j + 1], None).then_inc(ev("slots_filled"), 16)
                eng.wait_ge(ev("slots_filled"), 16 * NA)
                eng.dma_start(slots[:, :], t["slots"][:, :].rearrange("(b p) o -> b (p o)", p=BLOCK)).then_inc(ev("slots_in"), 16)
                eng.wait_ge(ev("rows_ready"), 1)
                n_blocks = total(eng)
                with eng.Fori(0, n_blocks + 1) as g:
                    eng.wait_ge(ev("x_turned"), g)
                    eng.tensor_copy(row[:, 0:1], rows[:, ds(g, 1)]).then_inc(ev("row_ready"), 1)
                    eng.wait_ge(ev("row_ready"), g + 1)
                    eng.sem_inc(ev("gather_begun"), 1)
                    eng.indirect_dma_start(xg[:, :], None, t["h2"][:, :], bass.IndirectOffsetOnAxis(ap=row[:, 0:1], axis=0)).then_inc(ev("gathered"), 16)
                eng.wait_ge(ev("gathered"), n_blocks * 16 + 16)

            @block.tensor
            def _(eng):
                eng.wait_ge(ev("const_in"), 80)
                eng.wait_ge(ev("member_ready"), 1)
                eng.sem_inc(ev("slot_free"), 2)
                flat = member[:, :, :].rearrange("p a e -> p (a e)")
                eng.matmul(PG[:, 0, :], const[:, 1, :], flat[:, 0:512], start=True, stop=True)
                eng.matmul(PG[:, 1, 0:32], const[:, 1, :], flat[:, 512:544], start=True, stop=True)
                eng.matmul(PT[:, 0:4, :].rearrange("p a b -> p (a b)"), const[:, 2, :], flat[:, 0:512], start=True, stop=True)
                eng.matmul(PY[:, 0, 0:32], const[:, 2, :], flat[:, 512:544], start=True, stop=True).then_inc(ev("counted"), 1)
                eng.wait_ge(ev("slots_ready"), 1)
                nb = MAX_BLOCKS + 1
                eng.transpose(PH[:, 0, 0:nb], slots_f[:, :], ident[0:nb, 0:nb]).then_inc(ev("slots_turned"), 1)
                eng.wait_ge(ev("rows_ready"), 1)

                def turn(g):
                    eng.wait_ge(ev("gathered"), g * 16 + 16)
                    for k in range(KD):
                        ins = eng.transpose(PT[:, k, :], xg[:, 128 * k:128 * k + 128], ident)
                    ins.then_inc(ev("x_turned"), 1)

                turn(0)
                with eng.Fori(0, N_EXPERTS // 2) as i:
                    for p in range(2):
                        before = eng.value_load(table[0:1, 1, ds(i * 2 + p, 1)], min_val=0, max_val=MAX_BLOCKS)
                        blocks = eng.value_load(table[0:1, 0, ds(i * 2 + p, 1)], min_val=1, max_val=T // BLOCK)
                        for name in ("w_gate", "w_up", "w_down"):
                            eng.wait_ge(ev(f"{name}_in{p}"), i * 16 + 16)
                        eng.sem_inc(ev("expert_begun"), 1)
                        with eng.Fori(0, blocks) as b:
                            g = before + b
                            eng.wait_ge(ev("xT_dve"), g + 1)
                            eng.wait_ge(ev("xT_act"), g + 1)
                            eng.wait_ge(ev("hid_ready"), g)
                            for n in range(2):
                                for k in range(KD):
                                    ins = eng.matmul(PG[:, n, :], xT[:, k, :], wgu[:, p, n, k, :], start=(k == 0), stop=(k == KD - 1))
                                ins.then_inc(ev("g_made" if n == 0 else "gu_made"), 1)
                            turn(g + 1)
                            eng.wait_ge(ev("hid_ready"), g + 1)
                            for k in range(KE):
                                ins = eng.transpose(PH[:, k, :], hid[:, 128 * k:128 * k + 128], ident)
                            ins.then_inc(ev("h_turned"), 1)
                            eng.wait_ge(ev("hT_dve"), g + 1)
                            eng.wait_ge(ev("y_dve"), g)
                            eng.wait_ge(ev("y_act"), g)
                            for n in range(2):
                                for k in range(KE):
                                    ins = eng.matmul(PY[:, n, :], hT[:, k, :], wd[:, p, k, 512 * n:512 * n + 512], start=(k == 0), stop=(k == KE - 1))
                            ins.then_inc(ev("y_made"), 1)
                            eng.nop()
                        eng.wait_ge(ev("y_made"), before + blocks)
                        eng.sem_inc(ev("slot_free"), 1)

        maps = wgu[:, 0, 0, 0:4, :].rearrange("p k n -> p (k n)").rearrange("p (a n) -> p a n", a=2)
        final = wgu[:, 0, 1, 0:2, :].rearrange("p k n -> p (k n)")
        pick = [[wgu[:, 1, n, 2 * j:2 * j + 2, :].rearrange("p k n -> p (k n)") for j in range(2)] for n in range(2)]
        xr = [wgu[:, 1, n, 4:6, :].rearrange("p k n -> p (k n)") for n in range(2)]
        out = [wgu[:, 1, n, 6:8, :].rearrange("p k n -> p (k n)") for n in range(2)]
        stat = dest_f

        with nc.Block() as block:
            def tiles(eng, body):
                with eng.Fori(0, NT // 2) as i:
                    body(i, 0)
                    body(i, 1)
                body(None, NT - 1)

            @block.sync
            def _(eng):
                eng.dma_start(maps[:, 0, :], t["mods"][0:1, GATE2 * D:GATE2 * D + D].to_broadcast([128, D])).then_inc(ev("maps_in"), 16)
                for s in range(NSEQ):
                    eng.dma_start(maps[DEC * s:DEC * s + DEC, 1, :], t["mods"][1 + s:2 + s, GATE2 * D:GATE2 * D + D].to_broadcast([DEC, D])).then_inc(ev("maps_in"), 16)
                eng.dma_start(final, t["final_norm_w"].rearrange("(o n) -> o n", o=1).to_broadcast([128, D])).then_inc(ev("maps_in"), 16)
                eng.sem_inc(ev("xr_free"), 2)

                def body(i, n):
                    p = n % 2
                    k = n * 128 if i is None else i * 256 + n * 128
                    eng.wait_ge(ev("xr_free"), at(i, 2, n + 1))
                    eng.dma_start(xr[p], t["x1"][ds(k, 128), :]).then_inc(ev(f"xr_in{p}"), 16)

                tiles(eng, body)

            @block.gpsimd
            def _(eng):
                eng.sem_inc(ev("pick_free"), 2)

                def body(i, n):
                    p = n % 2
                    tile = n if i is None else i * 2 + n
                    eng.wait_ge(ev("pick_free"), at(i, 2, n + 1))
                    eng.tensor_copy(row[:, 0:2], dest[:, ds(tile, 1), :].rearrange("p a b -> p (a b)")).then_inc(ev("pick_ready"), 1)
                    eng.wait_ge(ev("pick_ready"), at(i, 2, n + 1))
                    eng.sem_inc(ev("pick_begun"), 1)
                    for j in range(TOP_K):
                        eng.indirect_dma_start(pick[p][j], None, t["y_rows"][:, :], bass.IndirectOffsetOnAxis(ap=row[:, j:j + 1], axis=0)).then_inc(ev(f"picked{p}"), 16)
                    eng.wait_ge(ev(f"picked{p}"), at(i, 32, 32 * (n // 2 + 1)))

                tiles(eng, body)

            @block.scalar
            def _(eng):
                def body(i, n):
                    p = n % 2
                    k = n * 128 if i is None else i * 256 + n * 128
                    eng.wait_ge(ev("sum_ready"), at(i, 2, n + 1))
                    if i is None or n >= 2:
                        eng.wait_ge(ev(f"out{p}"), 16 * (n // 2))
                    else:
                        eng.wait_ge(ev(f"out{p}"), i * 16)
                    eng.activation(out[p], xr[p], ACT.Square, accum_out=stat[:, 0, 0:1]).then_inc(ev("final_squared"), 1)
                    eng.wait_ge(ev("final_var"), at(i, 2, n + 1))
                    eng.activation(stat[:, 1, 0:1], stat[:, 0, 1:2], ACT.Sqrt).then_inc(ev("final_root"), 1)
                    eng.wait_ge(ev("final_ready"), at(i, 2, n + 1))
                    if i is None and n == NT - 1:
                        dst = t["y_sample"].rearrange("b t d -> (b t) d")
                    else:
                        dst = t["y_prompt"][0, ds(k, 128), :]
                    eng.dma_start(dst, out[p]).then_inc(ev(f"out{p}"), 16)

                tiles(eng, body)
                for p in range(2):
                    eng.wait_ge(ev(f"out{p}"), 16 * ((NT + 1 - p) // 2))

            @block.vector
            def _(eng):
                fstep = ev("final_step")
                eng.wait_ge(ev("maps_in"), 16 * (2 + NSEQ))

                def body(i, n):
                    p = n % 2
                    tile = n if i is None else i * 2 + n
                    count = 0

                    def step(ins):
                        nonlocal count
                        count += 1
                        ins.then_inc(fstep, 1)
                        eng.wait_ge(fstep, count)

                    eng.wait_ge(ev(f"picked{p}"), at(i, 32, 32 * (n // 2 + 1)))
                    g = gates[:, ds(tile, 1), :].rearrange("p a b -> p (a b)")
                    a, b = pick[p]
                    step(eng.tensor_copy(stat[:, 2, :], g))
                    step(eng.tensor_scalar(a, a, stat[:, 2, 0:1], None, ALU.mult))
                    step(eng.scalar_tensor_tensor(a, b, stat[:, 2, 1:2], a, ALU.mult, ALU.add))
                    step(eng.tensor_tensor(a, a, maps[:, 1 if i is None and n == NT - 1 else 0, :], ALU.mult))
                    eng.wait_ge(ev(f"xr_in{p}"), at(i, 16, 16 * (n // 2 + 1)))
                    eng.tensor_tensor(xr[p], xr[p], a, ALU.add).then_inc(ev("sum_ready"), 1)
                    eng.wait_ge(ev("sum_ready"), at(i, 2, n + 1))
                    eng.sem_inc(ev("pick_free"), 1)
                    eng.wait_ge(ev("final_squared"), at(i, 2, n + 1))
                    eng.tensor_scalar(stat[:, 0, 1:2], stat[:, 0, 0:1], 1.0 / D, NORM_EPS, ALU.mult, ALU.add).then_inc(ev("final_var"), 1)
                    eng.wait_ge(ev("final_root"), at(i, 2, n + 1))
                    step(eng.reciprocal(stat[:, 1, 1:2], stat[:, 1, 0:1]))
                    eng.scalar_tensor_tensor(out[p], xr[p], stat[:, 1, 1:2], final, ALU.mult, ALU.mult).then_inc(ev("final_ready"), 1)
                    eng.wait_ge(ev("final_ready"), at(i, 2, n + 1))
                    eng.sem_inc(ev("xr_free"), 1)
                    eng.sem_clear(fstep)

                tiles(eng, body)
    finish(nc, names)


def program(nc, t):
    project(nc, t)
    recur(nc, t, False)
    recur(nc, t, True)
    with nc.sbuf_tensor("expert", [128, NT, TOP_K], F32) as expert, nc.sbuf_tensor("gates", [128, NT, TOP_K], F32) as gates:
        merge(nc, t, expert, gates)
        experts(nc, t, expert, gates)


SCRATCH = {
    "mods": ((1 + NSEQ, ADA), F32),
    "cm_p": ((NCM * 128, SEQ + 1), F32),
    "cm_s": ((NCM * 128, DEC_W), F32),
    "tm": ((T, 1024), F32),
    "h_last": ((PT + 4, D), F32),
    "mix": ((T, D), F32),
    "x1": ((T, D), F32),
    "h2": ((T, D), F32),
    "slots": (((MAX_BLOCKS + 1) * BLOCK, 1), I32),
    "y_rows": (((MAX_BLOCKS + 1) * BLOCK, D), F32),
}
OUTPUTS = [
    ("y_prompt", (1, SEQ, D)), ("y_sample", (NSEQ, DEC, D)),
    ("new_hgrn_p", (1, 1, HG_HEADS, 128, 128)), ("new_rwkv_p", (1, 1, RW_HEADS, RW_N, RW_N)), ("shift_p", (1, 1, D)),
    ("new_hgrn_s", (1, NSEQ, HG_HEADS, 128, 128)), ("new_rwkv_s", (1, NSEQ, RW_HEADS, RW_N, RW_N)), ("shift_s", (1, NSEQ, D)),
]
INPUTS = [
    "x_prompt", "x_sample", "state_hgrn", "state_rwkv", "state_shift", "c_prompt", "c_sample", "w_ada", "b_ada",
    "norm_mix_w", "norm_ffn_w", "w_in", "w_out", "hg_norm_w", "rw_mu_proj", "rw_mu_lora", "rw_w0", "rw_w1", "rw_w2",
    "rw_a0", "rw_a1", "rw_a2", "rw_g1", "rw_g2", "rw_kk", "rw_ka", "rw_rk", "rw_ln_w", "rw_ln_b", "router_g_w",
    "router_g_b", "router_e_w", "router_e_b", "w_gate", "w_up", "w_down", "final_norm_w",
]


def shape_constants():
    tok = np.arange(128)[:, None] + 128 * np.arange(NT)[None, :]
    return {
        "const": constants(),
        "reset": resets(),
        "iota": np.broadcast_to(np.arange(N_EXPERTS, dtype=np.float32), (128, N_EXPERTS)).copy(),
        "token_ids": np.repeat(tok, TOP_K, axis=1).astype(np.int32),
    }


def kernel(**inputs):
    import concourse.bacc as bacc
    from concourse.bass_utils import run_bass_kernel_spmd

    nc = bacc.Bacc("TRN2", target_bir_lowering=False, num_devices=1)
    arrays, t = {}, {}
    given = {name: np.ascontiguousarray(inputs[name]) for name in INPUTS}
    given.update(shape_constants())
    for name, a in given.items():
        arrays[f"in_{name}"] = a
        t[name] = nc.dram_tensor(f"in_{name}", a.shape, mybir.dt.from_np(a.dtype), kind="ExternalInput").ap()
    for name, (shape, dt) in SCRATCH.items():
        t[name] = nc.dram_tensor(f"scratch_{name}", shape, dt, kind="Internal").ap()
    for name, shape in OUTPUTS:
        t[name] = nc.dram_tensor(f"out_{name}", shape, F32, kind="ExternalOutput").ap()
    program(nc, t)
    r = run_bass_kernel_spmd(nc, [arrays], core_ids=[0])
    return tuple(r.results[0][f"out_{name}"] for name, _ in OUTPUTS)
```

```python
from contextlib import ExitStack

import numpy as np
import concourse.bass as bass
from concourse import mybir
from concourse.bass import ds

F32 = mybir.dt.float32
I32 = mybir.dt.int32
U32 = mybir.dt.uint32
ALU = mybir.AluOpType
ACT = mybir.ActivationFunctionType
AX = mybir.AxisListType

D = 1024
KD = D // 128
SEQ = 2048
NSEQ, DEC = 8, 16
T = SEQ + NSEQ * DEC
NT = T // 128
PT = SEQ // 128
CH = 64
HG_HEADS, RW_HEADS, RW_N = 4, 8, 64
HG_W = HG_HEADS * 128
RW_W = RW_HEADS * RW_N
IN_W = 4 * HG_W + 3 * RW_W
LORA = 256
W_ALL = IN_W + 2 * LORA
ADA = 6 * D
NORM_EPS = 1e-6
GN_EPS = 64e-5
CM_COLS = [128 * c for c in range(8)] + [4 * HG_W + 128 * c for c in range(12)] + [IN_W + 128 * c for c in range(4)]
NCM = len(CM_COLS)
TM_COLS = [2 * HG_W, 3 * HG_W]
DEC_W = NSEQ * (DEC + 1)

PRM = {"mu_proj": 0, "w0": 12, "a0": 16, "kk": 20, "ka": 24, "rk": 28, "mu_lora": 32}
N_PRM = 56

SHIFT1, SCALE1, GATE1, SHIFT2, SCALE2, GATE2 = range(6)


def at(i, per, const):
    return const if i is None else i * per + const


def sem_of(nc, names, name):
    names.append(nc.alloc_semaphore(name))
    return names[-1]


def finish(nc, names):
    nc.clear_and_free_semaphores(names)
    nc.all_engine_barrier()


def project(nc, t):
    names = []
    with ExitStack() as ctx:
        def sb(name, shape, dt=F32):
            return ctx.enter_context(nc.sbuf_tensor(name, shape, dt))

        def sem(name):
            return sem_of(nc, names, name)

        w = sb("w", [128, KD, W_ALL])
        hT = sb("hT", [128, 2, KD, 512])
        hT_dec = sb("hT_dec", [128, KD, 128])
        hT_pad = sb("hT_pad", [128, KD, NSEQ, DEC + 1])
        x = sb("x", [128, 2, D])
        h = sb("h", [128, 2, D])
        scale_map = sb("scale_map", [128, D])
        shift_map = sb("shift_map", [128, D])
        stage = sb("stage", [128, 4, 512])
        ident = sb("ident", [128, 128])
        stat = sb("stat", [128, 2, 4])
        mu = sb("mu", [128, 24])
        ada = hT
        mod = stage[:, :, :].rearrange("p a b -> p (a b)")
        lora = x[:, :, :].rearrange("p a b -> p (a b)").rearrange("p (k n) -> p k n", k=KD)
        crow = h[:, 0, :]
        csig = h[:, 1, :]
        cT = hT_dec[:, 0, 0:72].rearrange("p (k n) -> p k n", k=KD)
        ones = hT_dec[0:1, 1, 0:9]
        prm_rows = hT_dec[0:24, 2, :]
        bias = hT_pad[:, :, :, :].rearrange("p k s t -> p (k s t)")
        norm_w = scale_map
        shift_rows = h[0:NSEQ, 1, :]

        psT = ctx.enter_context(nc.psum_tensor("psT", [128, KD, 128], F32))
        psG = [ctx.enter_context(nc.psum_tensor(f"psG{b}", [128, 512], F32)) for b in range(4)]

        small_in = sem("small_in")
        lora_in = sem("lora_in")
        norm_in = [sem("norm_in0"), sem("norm_in1")]
        bias_in = [sem("bias_in0"), sem("bias_in1")]
        ada_in = [sem("ada_in0"), sem("ada_in1")]
        w_in = sem("w_in")
        c_exp = sem("c_exp")
        c_ready = sem("c_ready")
        cT_made = sem("cT_made")
        cT_ready = sem("cT_ready")
        mod_made = sem("mod_made")
        mod_kept = sem("mod_kept")
        mod_done = sem("mod_done")
        mod_out = sem("mod_out")
        mu_ready = sem("mu_ready")
        lora_ready = sem("lora_ready")
        maps_in = sem("maps_in")
        maps2_in = sem("maps2_in")
        shift_in = sem("shift_in")
        x_in = [sem("x_in0"), sem("x_in1")]
        squared = sem("squared")
        var_ready = sem("var_ready")
        root_ready = sem("root_ready")
        h_ready = sem("h_ready")
        turned = sem("turned")
        hT_act = sem("hT_act")
        hT_dve = sem("hT_dve")
        last_out = [sem("last_out0"), sem("last_out1")]
        made = sem("made")
        kept = [sem("kept_dve"), sem("kept_act")]
        stage_out = [sem(f"stage_out{s}") for s in range(4)]
        dve_step = sem("dve_step")
        zero_made = sem("zero_made")
        zero_out = sem("zero_out")

        GD = NCM + 2
        GP = NCM + 8
        ADA_G = ADA // 512

        def schedule(groups):
            for g in range(groups):
                yield "gemm", g
                if g % 6 == 1 and g // 6 < 4:
                    yield "norm", g // 6
                if g % 6 == 4 and g // 6 < 4:
                    yield "turn", g // 6

        block = ctx.enter_context(nc.Block())

        @block.sync
        def _(eng):
            eng.dma_start(ident[:, :], t["const"][:, 0:128]).then_inc(small_in, 16)
            eng.dma_start(crow[0:1, :], t["c_prompt"]).then_inc(small_in, 16)
            eng.dma_start(crow[1:9, :], t["c_sample"]).then_inc(small_in, 16)
            eng.dma_start(prm_rows, t["rw_mu_lora"][0].rearrange("j (k p) -> (j k) p", p=128)).then_inc(small_in, 16)
            w_ada = t["w_ada"][0].rearrange("(k p) n -> p k n", p=128)
            b_ada = t["b_ada"]
            for g in range(ADA_G):
                if g >= 2:
                    eng.wait_ge(mod_made, g - 1)
                eng.dma_start(ada[:, g % 2], w_ada[:, :, 512 * g:512 * g + 512]).then_inc(ada_in[g % 2], 16)
                eng.dma_start(bias[0:1, 512 * (g % 2):512 * (g % 2) + 512],
                              b_ada[:, 512 * g:512 * g + 512]).then_inc(bias_in[g % 2], 16)
                if g == 1:
                    eng.dma_start(norm_w[0:9, :], t["norm_mix_w"].to_broadcast([9, D])).then_inc(norm_in[0], 16)
                if g % 4 == 3:
                    eng.wait_ge(mod_done, g // 4 + 1)
                    eng.dma_start(t["mods"][:, 4 * (g // 4) * 512:4 * (g // 4 + 1) * 512],
                                  mod[0:9, :]).then_inc(mod_out, 16)
                    if g == 3:
                        eng.dma_start(norm_w[0:9, :], t["norm_ffn_w"].to_broadcast([9, D])).then_inc(norm_in[1], 16)
                if g == 3:
                    for n, name in enumerate(("rw_w1", "rw_a1", "rw_g1")):
                        c0, cn = 64 * n, 64 if n < 2 else 128
                        eng.dma_start(lora[:, :, c0:c0 + cn],
                                      t[name][0].rearrange("(k p) n -> p k n", p=128)).then_inc(lora_in, 16)
            eng.wait_ge(mod_out, 48)
            for s in range(NSEQ):
                for m, row in ((scale_map, SCALE1), (shift_map, SHIFT1)):
                    eng.dma_start(m[DEC * s:DEC * s + DEC, :],
                                  t["mods"][1 + s:2 + s, row * D:row * D + D].to_broadcast([DEC, D])).then_inc(maps_in, 16)
            eng.wait_ge(lora_ready, 1)
            eng.dma_start(x[:, 0, :], t["x_sample"].rearrange("b t d -> (b t) d")).then_inc(x_in[0], 16)
            eng.dma_start(shift_rows, t["state_shift"][0]).then_inc(shift_in, 16)
            eng.wait_ge(h_ready, 1)
            eng.dma_start(t["shift_s"][0], h[DEC - 1:128:DEC, 0, :]).then_inc(last_out[0], 16)
            for m, row in ((scale_map, SCALE1), (shift_map, SHIFT1)):
                eng.dma_start(m[:, :], t["mods"][0:1, row * D:row * D + D].to_broadcast([128, D])).then_inc(maps2_in, 16)

            def x_load(i, m):
                eng.wait_ge(h_ready, at(i, 8, m - 1))
                if i is None:
                    row = 128 * (m - 1)
                    src = t["x_prompt"][0, row:row + 128, :]
                else:
                    src = t["x_prompt"][0, ds((i * 8 + m - 1) % PT * 128, 128), :]
                eng.dma_start(x[:, m % 2, :], src).then_inc(x_in[m % 2], 16)

            def last_store(i, m):
                eng.wait_ge(h_ready, at(i, 8, m + 1))
                tile = m - 1 if i is None else (i * 8 + m - 1)
                eng.dma_start(t["h_last"][ds(tile, 1), :], h[127:128, m % 2, :]).then_inc(last_out[m % 2], 16)

            def store(i, n, dst):
                eng.wait_ge(kept[n % 2], at(i, GP, n // 2 + 1))
                eng.dma_start(dst, stage[:, n % 4, 0:dst.shape[-1]]).then_inc(stage_out[n % 4], 16)

            eng.wait_ge(zero_made, 1)
            eng.dma_start(t["cm_p"][:, 0:1].rearrange("(c p) o -> p c o", p=128), mu[:, 0:NCM].unsqueeze(2),
                          allow_slow_non_contiguous=True).then_inc(zero_out, 16)
            eng.wait_ge(zero_out, 16)
            x_load(None, 1)
            for what, k in schedule(GD):
                if what == "norm" and k < 3:
                    x_load(None, k + 2)
                if what == "turn":
                    last_store(None, 1 + k)
                if what == "gemm":
                    dst = t["cm_s"][128 * k:128 * k + 128, :] if k < NCM else \
                        t["tm"][SEQ:T, 512 * (k - NCM):512 * (k - NCM) + 512]
                    store(None, k, dst)
            x_load(None, 5)
            with eng.Fori(0, 2) as i:
                for s in range(2):
                    for what, k in schedule(GP):
                        if what == "norm":
                            x_load(i, 6 + 4 * s + k)
                        if what == "turn":
                            last_store(i, 5 + 4 * s + k)
                        if what == "gemm":
                            if k < NCM:
                                dst = t["cm_p"][128 * k:128 * k + 128, ds((i * 2 + s) * 512 + 1, 512)]
                            else:
                                q, half = (k - NCM) // 2, (k - NCM) % 2
                                dst = t["tm"][ds((i * 2 + s) * 512 + 128 * q, 128), 512 * half:512 * half + 512]
                            store(i, GD + GP * s + k, dst)
            total = GD + 4 * GP
            for s in range(4):
                eng.wait_ge(stage_out[s], 16 * len(range(s, total, 4)))
            for s in range(2):
                eng.wait_ge(x_in[s], 16 * 11)
                eng.wait_ge(last_out[s], 16 * (11 - s))
            eng.dma_start(t["shift_p"][0], t["h_last"][PT - 1:PT, :]).then_inc(zero_out, 16)
            eng.wait_ge(zero_out, 32)

        @block.gpsimd
        def _(eng):
            for k in range(KD):
                eng.dma_start(w[:, k, 0:IN_W], t["w_in"][0, 128 * k:128 * k + 128, :]).then_inc(w_in, 16)

        @block.scalar
        def _(eng):
            eng.wait_ge(small_in, 64)
            eng.activation(csig[0:9, :], crow[0:9, :], ACT.Exp, scale=-1.0).then_inc(c_exp, 1)
            for g in range(ADA_G):
                eng.wait_ge(mod_made, g + 1)
                if g % 4 == 0 and g:
                    eng.wait_ge(mod_out, 16 * (g // 4))
                eng.copy(mod[0:9, 512 * (g % 4):512 * (g % 4) + 512], psG[g % 4][0:9, :]).then_inc(mod_kept, 1)

            def norm(i, m):
                eng.wait_ge(x_in[m % 2], at(i, 64, 16 * (m // 2 + 1)))
                if m >= 1:
                    eng.wait_ge(turned, at(i, 8, max(m - 1, 1)))
                if m >= 2:
                    eng.wait_ge(last_out[m % 2], at(i, 64, 16 * (m // 2)))
                eng.activation(h[:, m % 2, :], x[:, m % 2, :], ACT.Square,
                               accum_out=stat[:, m % 2, 0:1]).then_inc(squared, 1)
                eng.wait_ge(var_ready, at(i, 8, m + 1))
                eng.activation(stat[:, m % 2, 2:3], stat[:, m % 2, 1:2], ACT.Sqrt).then_inc(root_ready, 1)

            def turn(i, m, slot, q):
                eng.wait_ge(turned, at(i, 8, m + 1))
                eng.copy(hT[:, slot, 4:8, 128 * q:128 * q + 128], psT[:, 4:8, :]).then_inc(hT_act, 1)

            def keep(i, n, cols):
                eng.wait_ge(made, at(i, 2 * GP, n + 1))
                eng.wait_ge(stage_out[n % 4], at(i, 16 * GP // 2, 16 * (n // 4)))
                eng.copy(stage[:, n % 4, 0:cols], psG[n % 4][:, 0:cols]).then_inc(kept[1], 1)

            eng.wait_ge(lora_ready, 1)
            norm(None, 0)
            eng.wait_ge(turned, 1)
            eng.copy(hT_dec[:, 4:8, :], psT[:, 4:8, :])
            eng.copy(hT_pad[:, 4:8, :, 1:], psT[:, 4:8, :].rearrange("p k (s t) -> p k s t", s=NSEQ)).then_inc(hT_act, 1)
            eng.wait_ge(mod_out, 48)
            for what, k in schedule(GD):
                if what == "gemm" and k % 2:
                    keep(None, k, DEC_W if k < NCM else 512)
                if what == "norm":
                    norm(None, 1 + k)
                if what == "turn":
                    turn(None, 1 + k, 0, k)
            with eng.Fori(0, 2) as i:
                for s in range(2):
                    for what, k in schedule(GP):
                        if what == "gemm" and k % 2:
                            keep(i, GD + GP * s + k, 512)
                        if what == "norm":
                            norm(i, 5 + 4 * s + k)
                        if what == "turn":
                            turn(i, 5 + 4 * s + k, 1 - s, k)

        @block.vector
        def _(eng):
            steps = 0

            def step(ins):
                nonlocal steps
                steps += 1
                ins.then_inc(dve_step, 1)
                eng.wait_ge(dve_step, steps)

            eng.wait_ge(c_exp, 1)
            step(eng.tensor_scalar(csig[0:9, :], csig[0:9, :], 1.0, None, ALU.add))
            step(eng.reciprocal(csig[0:9, :], csig[0:9, :]))
            step(eng.memset(ones, 1.0))
            eng.tensor_tensor(csig[0:9, :], csig[0:9, :], crow[0:9, :], ALU.mult).then_inc(c_ready, 1)
            eng.wait_ge(cT_made, 1)
            step(eng.tensor_copy(mu[:, :], psG[0][:, 128:152]))
            eng.tensor_copy(cT, psG[0][:, 0:72].rearrange("p (k n) -> p k n", k=KD)).then_inc(cT_ready, 1)
            for third in range(3):
                eng.wait_ge(mod_kept, 4 * (third + 1))
                if third != 1:
                    row = mod[0:9, D:2 * D] if third == 0 else mod[0:9, 0:D]
                    eng.wait_ge(norm_in[third // 2], 16)
                    eng.scalar_tensor_tensor(row, row, 1.0, norm_w[0:9, :], ALU.add, ALU.mult).then_inc(mod_done, 1)
                else:
                    eng.sem_inc(mod_done, 1)
            eng.wait_ge(lora_in, 48)
            for k in range(KD):
                for n in range(3):
                    c0, cn = 64 * n, 64 if n < 2 else 128
                    ins = eng.tensor_scalar(w[:, k, IN_W + LORA + c0:IN_W + LORA + c0 + cn], lora[:, k, c0:c0 + cn],
                                            mu[:, KD * n + k:KD * n + k + 1], None, ALU.mult)
            step(ins)
            step(eng.tensor_tensor(w[:, :, IN_W:IN_W + LORA], lora, w[:, :, IN_W + LORA:W_ALL], ALU.subtract))
            eng.sem_inc(lora_ready, 1)
            eng.memset(mu[:, :], 0.0).then_inc(zero_made, 1)

            def norm(i, m):
                eng.wait_ge(squared, at(i, 8, m + 1))
                eng.tensor_scalar(stat[:, m % 2, 1:2], stat[:, m % 2, 0:1], 1.0 / D, NORM_EPS,
                                  ALU.mult, ALU.add).then_inc(var_ready, 1)
                eng.wait_ge(root_ready, at(i, 8, m + 1))
                eng.reciprocal(stat[:, m % 2, 3:4], stat[:, m % 2, 2:3]).then_inc(dve_step, 1)
                eng.wait_ge(dve_step, at(i, 16, steps + 2 * m + 1))
                eng.scalar_tensor_tensor(h[:, m % 2, :], x[:, m % 2, :], stat[:, m % 2, 3:4], scale_map[:, :],
                                         ALU.mult, ALU.mult).then_inc(dve_step, 1)
                eng.wait_ge(dve_step, at(i, 16, steps + 2 * m + 2))
                eng.tensor_tensor(h[:, m % 2, :], h[:, m % 2, :], shift_map[:, :], ALU.add).then_inc(h_ready, 1)

            def turn(i, m, slot, q):
                eng.wait_ge(turned, at(i, 8, m + 1))
                eng.tensor_copy(hT[:, slot, 0:4, 128 * q:128 * q + 128], psT[:, 0:4, :]).then_inc(hT_dve, 1)

            def keep(i, n, cols):
                eng.wait_ge(made, at(i, 2 * GP, n + 1))
                if n >= 4:
                    eng.wait_ge(stage_out[n % 4], at(i, 16 * GP // 2, 16 * (n // 4)))
                eng.tensor_copy(stage[:, n % 4, 0:cols], psG[n % 4][:, 0:cols]).then_inc(kept[0], 1)

            eng.wait_ge(maps_in, 32 * NSEQ)
            norm(None, 0)
            eng.wait_ge(turned, 1)
            eng.tensor_copy(hT_dec[:, 0:4, :], psT[:, 0:4, :])
            eng.tensor_copy(hT_pad[:, 0:4, :, 1:],
                            psT[:, 0:4, :].rearrange("p k (s t) -> p k s t", s=NSEQ))
            eng.tensor_copy(hT_pad[:, :, :, 0], psG[3][:, 0:64].rearrange("p (k s) -> p k s", k=KD)).then_inc(hT_dve, 1)
            eng.wait_ge(mod_out, 48)
            eng.wait_ge(maps2_in, 32)
            for what, k in schedule(GD):
                if what == "gemm" and k % 2 == 0:
                    keep(None, k, DEC_W if k < NCM else 512)
                if what == "norm":
                    norm(None, 1 + k)
                if what == "turn":
                    turn(None, 1 + k, 0, k)
            with eng.Fori(0, 2) as i:
                for s in range(2):
                    for what, k in schedule(GP):
                        if what == "gemm" and k % 2 == 0:
                            keep(i, GD + GP * s + k, 512)
                        if what == "norm":
                            norm(i, 5 + 4 * s + k)
                        if what == "turn":
                            turn(i, 5 + 4 * s + k, 1 - s, k)

        @block.tensor
        def _(eng):
            eng.wait_ge(small_in, 64)
            eng.wait_ge(c_ready, 1)
            for k in range(KD):
                eng.transpose(psG[0][:, 9 * k:9 * k + 9], csig[0:9, 128 * k:128 * k + 128], ident[0:9, 0:9])
            eng.transpose(psG[0][:, 128:152], prm_rows, ident[0:24, 0:24]).then_inc(cT_made, 1)
            eng.wait_ge(cT_ready, 1)
            for g in range(ADA_G):
                eng.wait_ge(ada_in[g % 2], 16 * (g // 2 + 1))
                eng.wait_ge(bias_in[g % 2], 16 * (g // 2 + 1))
                if g >= 4:
                    eng.wait_ge(mod_kept, g - 3)
                for k in range(KD):
                    eng.matmul(psG[g % 4][0:9, :], cT[:, k, :], ada[:, g % 2, k, :], start=(k == 0), stop=False)
                eng.matmul(psG[g % 4][0:9, :], ones, bias[0:1, 512 * (g % 2):512 * (g % 2) + 512],
                           start=False, stop=True).then_inc(mod_made, 1)

            def turn(i, m):
                eng.wait_ge(h_ready, at(i, 8, m + 1))
                if m >= 1:
                    eng.wait_ge(hT_act, at(i, 8, m))
                    eng.wait_ge(hT_dve, at(i, 8, m))
                for k in range(KD):
                    ins = eng.transpose(psT[:, k, :], h[:, m % 2, 128 * k:128 * k + 128], ident[:, :])
                ins.then_inc(turned, 1)

            def free(i, n):
                if n >= 4:
                    eng.wait_ge(kept[n % 2], at(i, GP, (n - 4) // 2 + 1))

            eng.wait_ge(mod_kept, ADA_G)
            eng.wait_ge(shift_in, 16)
            for k in range(KD):
                eng.transpose(psG[3][:, 8 * k:8 * k + 8], shift_rows[:, 128 * k:128 * k + 128], ident[0:8, 0:8])
            turn(None, 0)
            eng.wait_ge(hT_act, 1)
            eng.wait_ge(hT_dve, 1)
            eng.wait_ge(w_in, 16 * KD)
            eng.wait_ge(lora_ready, 1)
            for what, g in schedule(GD):
                if what == "turn":
                    turn(None, 1 + g)
                if what != "gemm":
                    continue
                free(None, g)
                for k in range(KD):
                    if g < NCM:
                        ins = eng.matmul(psG[g % 4][:, 0:DEC_W], w[:, k, CM_COLS[g]:CM_COLS[g] + 128],
                                         hT_pad[:, k, :, :].rearrange("p s t -> p (s t)"), start=(k == 0), stop=(k == KD - 1))
                    else:
                        c0 = TM_COLS[g - NCM]
                        ins = eng.matmul(psG[g % 4][:, :], hT_dec[:, k, :], w[:, k, c0:c0 + 512],
                                         start=(k == 0), stop=(k == KD - 1))
                ins.then_inc(made, 1)
            with eng.Fori(0, 2) as i:
                for s in range(2):
                    eng.wait_ge(hT_act, at(i, 8, 5 + 4 * s))
                    eng.wait_ge(hT_dve, at(i, 8, 5 + 4 * s))
                    for what, g in schedule(GP):
                        if what == "turn":
                            turn(i, 5 + 4 * s + g)
                        if what != "gemm":
                            continue
                        n = GD + GP * s + g
                        free(i, n)
                        for k in range(KD):
                            if g < NCM:
                                ins = eng.matmul(psG[n % 4][:, :], w[:, k, CM_COLS[g]:CM_COLS[g] + 128],
                                                 hT[:, s, k, :], start=(k == 0), stop=(k == KD - 1))
                            else:
                                q, c0 = (g - NCM) // 2, TM_COLS[(g - NCM) % 2]
                                ins = eng.matmul(psG[n % 4][:, :], hT[:, s, k, 128 * q:128 * q + 128],
                                                 w[:, k, c0:c0 + 512], start=(k == 0), stop=(k == KD - 1))
                        ins.then_inc(made, 1)
    finish(nc, names)


N_LEVELS = 6
C_ID, C_LEVEL, C_LEVEL_T = 0, 1, 1 + N_LEVELS
C_STRICT, C_INCL, C_LOWER, C_LOWER2, C_HEAD, C_PAD = [1 + 2 * N_LEVELS + n for n in range(6)]
C_CUM, C_ONES = C_PAD + 1, C_PAD + 2
N_CONST = C_PAD + 3


def constants():
    s, u = np.arange(128)[:, None], np.arange(128)[None, :]
    same = s // CH == u // CH
    out = [s == u]
    levels = [(s // (2 << n) == u // (2 << n)) & (s // (1 << n) % 2 == 0) & (u // (1 << n) % 2 == 1)
              for n in range(N_LEVELS)]
    out += levels + [x.T for x in levels]
    out += [same & (s < u), same & (s <= u), same & (u < s), same & (u < s), same, (u % CH < DEC) & (s >= 0), s <= u, (s >= 0) & (u >= 0)]
    return np.concatenate([x.astype(np.float32) for x in out], axis=1)


def resets():
    return np.broadcast_to((np.arange(512) % CH != 0).astype(np.float32), (128, 512)).copy()


DECAY = float(np.exp(-0.5))


def recur(nc, t, running):
    part = "run_" if running else "prompt_"
    names = []
    with ExitStack() as ctx:
        def sb(name, shape, dt=F32):
            return ctx.enter_context(nc.sbuf_tensor(part + name, shape, dt))

        sems = {}

        def ev(name):
            if name not in sems:
                sems[name] = sem_of(nc, names, part + name)
            return sems[name]

        n_tiles = NSEQ // 2 if running else PT
        n_zeroed = 4 if running else 2
        levels = DEC.bit_length() - 1 if running else N_LEVELS
        n_y, n_x = 2 * (levels - 1), 2 * (levels - 2)
        got_h, got_r = (96, 32) if running else (32, 16)

        const = sb("const", [128, N_CONST, 128])
        prm = sb("prm", [128, N_PRM])
        rows = sb("rows", [128, 3, 512])
        one = sb("one", [128, 1])
        fw2 = sb("fw2", [128, RW_W])
        fg2 = sb("fg2", [128, RW_W])
        reset = sb("reset", [128, 4, 2, CH])
        prm_rows = sb("prm_rows", [N_PRM, 128])
        hin = sb("hin", [128, 8, 128])
        vin = sb("vin", [128, 2, 512])
        z = sb("z", [128, 12, 128])
        sk = sb("sk", [128, 8, 128])
        lf = sb("lf", [128, 4, 128])
        dd = sb("dd", [128, 8, 4, 128])
        q = sb("q", [128, 4, 128])
        gs = sb("gs", [128, 512])
        hdec = sb("hdec", [128, 4, 2])
        at_ = sb("at_", [128, 4, 128])
        kdT = sb("kdT", [128, 4, 128])
        S = sb("S", [128, 4 if running else 2, 4, 128])
        osq = sb("osq", [128, 512])
        hst = sb("hst", [128, 2, 4])
        rin = sb("rin", [128, 16, 129])
        pm = sb("pm", [128, 12, 128])
        tl = sb("tl", [128, 2, 128])
        te = sb("te", [128, 2, 128])
        u = sb("u", [128, 8, 128])
        uz = sb("uz", [128, 8, 128])
        kra = sb("kra", [128, 4, 128])
        cs = sb("cs", [128, 4, 128])
        cx = sb("cx", [128, 4, 128])
        e1 = sb("e1", [128, 4, 128])
        e2 = sb("e2", [128, 4, 128])
        e3 = sb("e3", [128, 4, 128])
        kr = sb("kr", [128, 4, 128])
        sq = sb("sq", [128, 4, 128])
        kn = sb("kn", [128, 4, 128])
        bon = sb("bon", [128, 4, 128])
        AR = sb("AR", [128, 4, 2, 128])
        BK = sb("BK", [128, 4, 2, 128])
        gate = sb("gate", [128, 512])
        tok = sb("tok", [128, 4, 512])
        LB = sb("LB", [128, 8, 2, 128])
        LM = sb("LM", [128, 8, 2, 128])
        KR = sb("KR", [128, 8, 128])
        X = sb("X", [128, 8, 128])
        XT = sb("XT", [128, 8, 128])
        Y = sb("Y", [128, 8, 128])
        XA = sb("XA", [128, 4, 128])
        MX = sb("MX", [128, 8, 128])
        SA = sb("SA", [128, 512])
        ST = sb("ST", [128, 4 if running else 2, 4, 128])
        wm = sb("wm", [128, 2, 4, 128])
        bonus = sb("bonus", [128, 8])
        rst = sb("rst", [128, 3, 8])
        yc = sb("yc", [128, 512])
        ysq = sb("ysq", [128, 512])
        vb = sb("vb", [128, 512])
        mix = sb("mix", [128, D])
        srow = sb("srow", [128, 2, 4, 128])
        sout = sb("sout", [128, 2, 4, RW_N])
        P = [ctx.enter_context(nc.psum_tensor(f"{part}P{b}", [128, 512], F32)) for b in range(8)]

        def cm(n):
            return const[:, n, :]

        def heads(x, n=4):
            return x.rearrange("p (h c) -> p h c", h=n)

        ident = cm(C_ID)

        def column(name, n=4):
            c = PRM[name]
            return prm[:, c:c + n].unsqueeze(2).to_broadcast([128, n, 128])

        block = ctx.enter_context(nc.Block())

        @block.sync
        def _(eng):
            eng.dma_start(const[:, :, :].rearrange("p a b -> p (a b)"), t["const"]).then_inc(ev("const_in"), 16)
            eng.dma_start(reset[:, :, :, :].rearrange("p a b c -> p (a b c)"), t["reset"]).then_inc(ev("const_in"), 16)
            for name, n in (("rw_mu_proj", 12), ("rw_w0", 4), ("rw_a0", 4), ("rw_kk", 4), ("rw_ka", 4)):
                r0 = PRM[name[3:]]
                eng.dma_start(prm_rows[r0:r0 + n, :], t[name][0].rearrange("(c p) -> c p", p=128)).then_inc(ev("const_in"), 16)
            r0 = PRM["rk"]
            eng.dma_start(prm_rows[r0:r0 + 4, :], t["rw_rk"][0].rearrange("(c h) n -> c (h n)", h=2)).then_inc(ev("const_in"), 16)
            eng.dma_start(prm_rows[PRM["mu_lora"]:N_PRM, :],
                          t["rw_mu_lora"][0].rearrange("j (k p) -> (j k) p", p=128)).then_inc(ev("const_in"), 16)
            for n, name in enumerate(("hg_norm_w", "rw_ln_w", "rw_ln_b")):
                eng.dma_start(rows[:, n, :], t[name].to_broadcast([128, 512])).then_inc(ev("const_in"), 16)
            eng.dma_start(fw2[0:64, :], t["rw_w2"][0]).then_inc(ev("const_in"), 16)
            eng.dma_start(fw2[64:128, :], t["rw_a2"][0]).then_inc(ev("const_in"), 16)
            eng.dma_start(fg2[:, :], t["rw_g2"][0]).then_inc(ev("const_in"), 16)
            if running:
                eng.wait_ge(ev("zeroed"), n_zeroed)

            def load_h(i, n):
                if running:
                    cmp_ = t["cm_s"].rearrange("(c p) (s w) -> p c s w", p=128, s=NSEQ)
                    tmp_ = t["tm"][SEQ:T, :].rearrange("(s w) c -> s w c", s=NSEQ)
                    for c in range(2):
                        s = c if i is None else (i * 2 + (2 * n + c)) % NSEQ
                        for g in range(2):
                            eng.dma_start(hin[:, 4 * g:4 * g + 4, CH * c:CH * c + DEC],
                                          cmp_[:, 4 * g:4 * g + 4, ds(s, 1), 1:].rearrange("p c s w -> p c (s w)")).then_inc(ev("h_in"), 16)
                        eng.dma_start(vin[CH * c:CH * c + DEC, :, :].rearrange("p a b -> p (a b)"),
                                      tmp_[ds(s, 1)].rearrange("s w c -> (s w) c")).then_inc(ev("h_in"), 16)
                else:
                    k = 0 if i is None else (i + n) % PT * 128
                    eng.dma_start(hin[:, :, :], t["cm_p"][0:1024, :].rearrange("(c p) w -> p c w", p=128)[:, :, ds(k + 1, 128)]).then_inc(ev("h_in"), 16)
                    eng.dma_start(vin[:, :, :].rearrange("p a b -> p (a b)"), t["tm"][ds(k, 128), :]).then_inc(ev("h_in"), 16)

            def load_r(i, n):
                if running:
                    cmp_ = t["cm_s"].rearrange("(c p) (s w) -> p c s w", p=128, s=NSEQ)
                    for c in range(2):
                        s = c if i is None else (i * 2 + (2 * n + c)) % NSEQ
                        eng.dma_start(rin[:, :, CH * c:CH * c + DEC + 1],
                                      cmp_[:, 8:24, ds(s, 1), :].rearrange("p c s w -> p c (s w)")).then_inc(ev("r_in"), 16)
                else:
                    k = 0 if i is None else (i + n) % PT * 128
                    eng.dma_start(rin[:, :, :], t["cm_p"][1024:3072, :].rearrange("(c p) w -> p c w", p=128)[:, :, ds(k, 129)]).then_inc(ev("r_in"), 16)

            load_r(None, 0)
            load_h(None, 0)
            with eng.Fori(0, n_tiles) as i:
                if running:
                    eng.wait_ge(ev("h_updated"), i * 2 + 1)
                    eng.wait_ge(ev("st_turned"), i * 2 + 1)
                    for c in range(2):
                        eng.dma_start(S[:, c, :, :], t["state_hgrn"][0, ds(i * 2 + c, 1)].rearrange("s h k v -> k (s h) v")).then_inc(ev("s_in"), 16)
                        for g in range(2):
                            eng.dma_start(srow[64 * g:64 * g + 64, c, :, 64 * g:64 * g + 64],
                                          t["state_rwkv"][0, ds(i * 2 + c, 1), g:8:2].rearrange("s h v k -> v (s h) k")).then_inc(ev("s_in"), 16)
                eng.wait_ge(ev("r_used"), i + 1)
                load_r(i, 1)
                eng.wait_ge(ev("h_used"), i + 1)
                eng.wait_ge(ev("gs_ready"), i + 1)
                load_h(i, 1)
                if running:
                    eng.wait_ge(ev("h_updated"), i * 2 + 2 + 1)
                    for c in range(2):
                        eng.dma_start(t["new_hgrn_s"][0, ds(i * 2 + c, 1)].rearrange("s h k v -> k (s h) v"), S[:, 2 + c, :, :]).then_inc(ev("s_out"), 16)
                    eng.wait_ge(ev("st_turned_back"), i + 1)
                    for c in range(2):
                        eng.dma_start(t["new_rwkv_s"][0, ds(i * 2 + c, 1)].rearrange("s (h g) v k -> (s g v) h k", g=2), sout[:, c, :, :]).then_inc(ev("s_out"), 16)
                    eng.wait_ge(ev("s_out"), i * 64 + 64)
                    eng.sem_inc(ev("s_out_seen"), 1)
                eng.wait_ge(ev("mixed"), i + 1 + 1)
                if running:
                    for c in range(2):
                        eng.dma_start(t["mix"][ds(i * (2 * DEC) + (SEQ + DEC * c), DEC), :], mix[CH * c:CH * c + DEC, :]).then_inc(ev("mix_out"), 16)
                else:
                    eng.dma_start(t["mix"][ds(i * 128, 128), :], mix[:, :]).then_inc(ev("mix_out"), 16)
            eng.wait_ge(ev("mix_out"), (32 if running else 16) * n_tiles + 16)
            eng.wait_ge(ev("h_in"), (96 if running else 32) * (n_tiles + 1))
            if not running:
                eng.dma_start(t["new_hgrn_p"][0, 0].rearrange("h k v -> k h v"), S[:, 0, :, :]).then_inc(ev("s_out"), 16)
                eng.wait_ge(ev("st_turned_back"), 1)
                eng.dma_start(t["new_rwkv_p"][0, 0].rearrange("(h g) v k -> (g v) h k", g=2), sout[:, 0, :, :]).then_inc(ev("s_out"), 16)
                eng.wait_ge(ev("s_out"), 32)

        @block.gpsimd
        def _(eng):
            for name in ("h_updated", "st_turned", "p_mix_read", "st_updated", "mixed"):
                eng.sem_inc(ev(name), 1)
            eng.sem_inc(ev("mix_out"), 16)
            eng.memset(one[:, :], 1.0).then_inc(ev("one_made"), 1)
            if running:
                for buffer in (hin[:, :, :], vin[:, :, :], rin[:, :, :]):
                    eng.memset(buffer, 0.0).then_inc(ev("zeroed"), 1)
                eng.memset(srow[:, :, :, :], 0.0).then_inc(ev("zeroed"), 1)
            else:
                eng.memset(S[:, 0, :, :], 0.0).then_inc(ev("zeroed"), 1)
                eng.memset(ST[:, 0, :, :], 0.0).then_inc(ev("zeroed"), 1)
            eng.wait_ge(ev("prm_ready"), 1)

            def r_prep_pool(i, n):
                eng.wait_ge(ev("r_in"), at(i, got_r, got_r * (n + 1)))
                if n:
                    eng.wait_ge(ev("rw_ready"), at(i, 1, n))
                eng.tensor_tensor(tl[:, :, :], rin[:, 12:14, 1:129], rin[:, 14:16, 0:128], ALU.add).then_inc(ev("tl_ready"), 1)
                if n:
                    eng.wait_ge(ev("v_turned"), at(i, 1, n))
                eng.tensor_tensor(pm[:, :, :], rin[:, 0:12, 0:128], rin[:, 0:12, 1:129], ALU.subtract).then_inc(ev("shifted"), 1)

            def keys_pool(i, n):
                eng.wait_ge(ev("mixed_rkv"), at(i, 1, n + 1))
                eng.tensor_tensor(kr[:, :, :], pm[:, 4:8, :], column("kk"), ALU.mult).then_inc(ev("kr_made"), 1)
                eng.wait_ge(ev("kr_made"), at(i, 1, n + 1))
                eng.tensor_tensor(sq[:, :, :], kr[:, :, :], kr[:, :, :], ALU.mult).then_inc(ev("k_squared"), 1)

            def prep_pool(i, n):
                eng.wait_ge(ev("norm_root"), at(i, 1, n + 1))
                eng.tensor_tensor(kr[:, :, :], kr[:, :, :], sq[:, :, :], ALU.mult).then_inc(ev("kr_scaled"), 1)
                eng.wait_ge(ev("kr_scaled"), at(i, 1, n + 1))
                if running:
                    eng.tensor_tensor(kr[:, :, :], kr[:, :, :], cm(C_PAD).unsqueeze(1).to_broadcast([128, 4, 128]), ALU.mult).then_inc(ev("kr_padded"), 1)
                    eng.wait_ge(ev("kr_padded"), at(i, 1, n + 1))
                eng.wait_ge(ev("u_exp"), at(i, 1, n + 1))
                eng.tensor_tensor(kra[:, :, :], kr[:, :, :], u[:, 4:8, :], ALU.mult).then_inc(ev("kr_ready"), 1)
                eng.wait_ge(ev("a_sk"), at(i, 1, n + 1))
                eng.tensor_tensor(q[:, :, :], hin[:, 0:4, :], sk[:, 0:4, :], ALU.mult).then_inc(ev("q_ready"), 1)
                if running:
                    eng.tensor_tensor(sk[:, 4:8, :], sk[:, 4:8, :], cm(C_PAD).unsqueeze(1).to_broadcast([128, 4, 128]), ALU.mult).then_inc(ev("sk_padded"), 1)
                    eng.wait_ge(ev("sk_padded"), at(i, 1, n + 1))
                eng.tensor_tensor(gs[:, :], gs[:, :], vin[:, 1, :], ALU.mult).then_inc(ev("gs_made"), 1)
                eng.wait_ge(ev("gs_made"), at(i, 1, n + 1))
                eng.tensor_tensor(gs[:, :], gs[:, :], rows[:, 0, :], ALU.mult).then_inc(ev("gs_ready"), 1)
                eng.wait_ge(ev("kn_ready"), at(i, 1, n + 1))
                eng.tensor_tensor(bon[:, :, :], kn[:, :, :], pm[:, 0:4, :], ALU.mult).then_inc(ev("bon_made"), 1)
                eng.wait_ge(ev("bon_made"), at(i, 1, n + 1))
                eng.tensor_tensor(bon[:, :, :], bon[:, :, :], column("rk"), ALU.mult).then_inc(ev("bon_ready"), 1)
                eng.wait_ge(ev("a_dd"), at(i, 1, n + 1))
                for lv in range(levels):
                    half = 1 << lv
                    cut = [y.rearrange("p h c -> p (h c)").rearrange("p (n a l) -> p n a l", a=2, l=half)
                           for y in (dd[:, lv, :, :], sk[:, 4:8, :])]
                    eng.tensor_tensor(cut[0][:, :, 0, :], cut[0][:, :, 0, :], cut[1][:, :, 0, :], ALU.mult)
                eng.tensor_tensor(dd[:, 7, :, :], dd[:, 7, :, :], sk[:, 4:8, :], ALU.mult).then_inc(ev("h_keys_ready"), 1)

            r_prep_pool(None, 0)
            keys_pool(None, 0)
            prep_pool(None, 0)
            with eng.Fori(0, n_tiles) as i:
                r_prep_pool(i, 1)
                eng.wait_ge(ev("product_kept"), i * 10 + 8)
                eng.tensor_tensor(XT[:, :, :], LB[:, :, 0, :], cm(C_LEVEL).unsqueeze(1).to_broadcast([128, 8, 128]), ALU.mult).then_inc(ev("xt_level0"), 1)
                eng.wait_ge(ev("xt_level0"), i + 1)
                eng.tensor_tensor(XT[:, :, :], XT[:, :, :], ident.unsqueeze(1).to_broadcast([128, 8, 128]), ALU.add).then_inc(ev("xt_begun"), 1)
                keys_pool(i, 1)
                eng.wait_ge(ev("bonus_kept"), i + 1)
                eng.wait_ge(ev("v_kept"), i + 1)
                eng.tensor_tensor(heads(vb[:, :], 8), heads(tok[:, 0, :], 8), bonus[:, :].unsqueeze(2).to_broadcast([128, 8, RW_N]), ALU.mult).then_inc(ev("vb_made"), 1)
                eng.wait_ge(ev("vb_made"), i + 1)
                eng.tensor_tensor(vb[:, :], vb[:, :], rows[:, 2, :], ALU.add).then_inc(ev("vb_ready"), 1)
                prep_pool(i, 1)
                eng.wait_ge(ev("y_scaled"), i + 1)
                eng.tensor_tensor(yc[:, :], yc[:, :], rows[:, 1, :], ALU.mult).then_inc(ev("y_weighed"), 1)
                eng.wait_ge(ev("y_weighed"), i + 1)
                eng.wait_ge(ev("vb_ready"), i + 1)
                eng.tensor_tensor(yc[:, :], yc[:, :], vb[:, :], ALU.add).then_inc(ev("y_summed"), 1)
                eng.wait_ge(ev("y_summed"), i + 1)
                eng.wait_ge(ev("gate_read"), i + 1)
                eng.tensor_tensor(mix[:, 512:1024], yc[:, :], gate[:, :], ALU.mult).then_inc(ev("mixed"), 1)

        def prep_scalar(eng, i, n):
            if n:
                eng.wait_ge(ev("gate_made"), at(i, 1, n))
            eng.wait_ge(ev("tl_ready"), at(i, 1, n + 1))
            eng.activation(te[0:64, 0, :], tl[0:64, 0, :], ACT.Exp, scale=-2.0)
            eng.activation(te[:, 1, :], tl[:, 1, :], ACT.Exp, scale=-1.0).then_inc(ev("te_ready"), 1)
            yield
            eng.wait_ge(ev("h_in"), at(i, got_h, got_h * (n + 1)))
            eng.activation(z[:, 0:8, :], hin[:, :, :], ACT.Abs)
            eng.activation(z[:, 8:12, :].rearrange("p a b -> p (a b)"), vin[:, 1, :], ACT.Abs).then_inc(ev("a_z1"), 1)
            eng.wait_ge(ev("a_z1"), at(i, 1, n + 1))
            eng.activation(z[:, :, :], z[:, :, :], ACT.Exp, scale=-1.0).then_inc(ev("a_z2"), 1)
            yield
            eng.wait_ge(ev("u_ready"), at(i, 1, n + 1))
            eng.activation(uz[:, :, :], u[:, :, :], ACT.Abs).then_inc(ev("a_u1"), 1)
            eng.wait_ge(ev("a_u1"), at(i, 1, n + 1))
            eng.activation(uz[:, :, :], uz[:, :, :], ACT.Exp, scale=-1.0).then_inc(ev("a_u2"), 1)
            eng.wait_ge(ev("a_u2"), at(i, 1, n + 1))
            eng.activation(uz[:, :, :], uz[:, :, :], ACT.Ln, bias=one[:, :]).then_inc(ev("u_log"), 1)
            yield
            eng.wait_ge(ev("a_z2"), at(i, 1, n + 1))
            eng.activation(z[:, :, :], z[:, :, :], ACT.Ln, bias=one[:, :]).then_inc(ev("a_z3"), 1)
            eng.wait_ge(ev("norm_max"), at(i, 1, n + 1))
            eng.activation(sq[:, :, :], sq[:, :, :], ACT.Ln).then_inc(ev("norm_log"), 1)
            eng.wait_ge(ev("norm_log"), at(i, 1, n + 1))
            eng.activation(sq[:, :, :], sq[:, :, :], ACT.Exp, scale=-0.5).then_inc(ev("norm_root"), 1)
            yield
            eng.wait_ge(ev("u_min"), at(i, 1, n + 1))
            eng.activation(u[:, :, :], u[:, :, :], ACT.Exp).then_inc(ev("u_exp"), 1)
            eng.wait_ge(ev("v_z"), at(i, 1, n + 1))
            eng.activation(sk[:, :, :], z[:, 0:8, :], ACT.Exp)
            if n:
                eng.wait_ge(ev("h_mixed"), at(i, 1, n))
            eng.activation(gs[:, :], z[:, 8:12, :].rearrange("p a b -> p (a b)"), ACT.Exp).then_inc(ev("a_sk"), 1)
            yield
            eng.wait_ge(ev("v_dd"), at(i, 1, n + 1))
            for g in range(levels // 2):
                eng.activation(dd[:, 2 * g:2 * g + 2, :, :], dd[:, 2 * g:2 * g + 2, :, :], ACT.Exp)
            yield
            eng.activation(dd[:, 6:8, :, :], dd[:, 6:8, :, :], ACT.Exp).then_inc(ev("a_dd"), 1)
            eng.wait_ge(ev("cs_ready"), at(i, 1, n + 1))
            eng.activation(e1[:, :, :], cs[:, :, :], ACT.Exp, scale=-DECAY)
            eng.activation(e2[:, :, :], cs[:, :, :], ACT.Exp, scale=DECAY)
            eng.activation(e3[:, :, :], cx[:, :, :], ACT.Exp, scale=-DECAY).then_inc(ev("e_ready"), 1)
            yield

        def prep_vector(eng, i, n, step, settle):
            eng.wait_ge(ev("te_ready"), at(i, 1, n + 1))
            step(eng.tensor_scalar(te[0:64, 0, :], te[0:64, 0, :], 1.0, None, ALU.add))
            step(eng.tensor_scalar(te[:, 1, :], te[:, 1, :], 1.0, None, ALU.add))
            settle()
            step(eng.reciprocal(te[0:64, 0, :], te[0:64, 0, :]))
            step(eng.reciprocal(te[:, 1, :], te[:, 1, :]))
            step(eng.tensor_copy(te[64:128, 0, :], tl[64:128, 0, :]))
            settle()
            eng.tensor_scalar(te[0:64, 0, :], te[0:64, 0, :], 2.0, -1.0, ALU.mult, ALU.add).then_inc(ev("lora_ready"), 1)
            yield
            eng.wait_ge(ev("wa_made"), at(i, 1, n + 1))
            step(eng.tensor_tensor(u[:, 0:4, :], heads(P[6][:, :]), column("w0"), ALU.add))
            eng.tensor_tensor(u[:, 4:8, :], heads(P[7][:, :]), column("a0"), ALU.add).then_inc(ev("wa_read"), 1)
            eng.wait_ge(ev("wa_read"), at(i, 1, n + 1))
            eng.sem_inc(ev("u_ready"), 1)
            yield
            eng.wait_ge(ev("shifted"), at(i, 1, n + 1))
            for c in range(12):
                ins = eng.scalar_tensor_tensor(pm[:, c, :], pm[:, c, :], prm[:, c:c + 1], rin[:, c, 1:129], ALU.mult, ALU.add)
            ins.then_inc(ev("mixed_rkv"), 1)
            eng.wait_ge(ev("mixed_rkv"), at(i, 1, n + 1))
            eng.sem_inc(ev("r_used"), 1)
            yield
            eng.wait_ge(ev("norm_made"), at(i, 1, n + 1))
            eng.tensor_scalar(sq[:, :, :], heads(P[6][:, :]), 1e-24, None, ALU.max).then_inc(ev("norm_max"), 1)
            eng.wait_ge(ev("norm_max"), at(i, 1, n + 1))
            eng.sem_inc(ev("norm_read"), 1)
            eng.wait_ge(ev("u_log"), at(i, 1, n + 1))
            eng.scalar_tensor_tensor(u[:, :, :], u[:, :, :], 0.0, uz[:, :, :], ALU.min, ALU.subtract).then_inc(ev("u_min"), 1)
            eng.wait_ge(ev("a_z3"), at(i, 1, n + 1))
            step(eng.scalar_tensor_tensor(lf[:, :, :], hin[:, 4:8, :], 0.0, z[:, 4:8, :], ALU.min, ALU.subtract))
            step(eng.scalar_tensor_tensor(z[:, 0:4, :], hin[:, 0:4, :], 0.0, z[:, 0:4, :], ALU.min, ALU.subtract))
            zg = z[:, 8:12, :].rearrange("p a b -> p (a b)")
            step(eng.scalar_tensor_tensor(zg, vin[:, 1, :], 0.0, zg, ALU.min, ALU.subtract))
            settle()
            eng.tensor_tensor(z[:, 4:8, :], lf[:, :, :], hin[:, 4:8, :], ALU.subtract).then_inc(ev("v_z"), 1)
            if running:
                eng.wait_ge(ev("v_z"), at(i, 1, n + 1))
                step(eng.tensor_tensor(lf[:, :, :], lf[:, :, :], cm(C_PAD).unsqueeze(1).to_broadcast([128, 4, 128]), ALU.mult))
                settle()
            if n:
                eng.wait_ge(ev("h_used"), at(i, 1, n))
            step(eng.tensor_tensor_scan(dd[:, 6, :, :].rearrange("p h c -> p (h c)"), reset[:, :, :, :].rearrange("p a b c -> p (a b c)"),
                                        lf[:, :, :].rearrange("p h c -> p (h c)"), 0.0, ALU.mult, ALU.add))
            yield
            settle()
            b = dd[:, 6, :, :].rearrange("p h c -> p (h c)")
            for lv in range(levels):
                half = 1 << lv
                src = b.rearrange("p (n a l) -> p n a l", a=2, l=half)
                dst = dd[:, lv, :, :].rearrange("p h c -> p (h c)").rearrange("p (n a l) -> p n a l", a=2, l=half)
                mid = src[:, :, 0, half - 1:half].to_broadcast([128, 256 // half, half])
                step(eng.tensor_tensor(dst[:, :, 0, :], mid, src[:, :, 0, :], ALU.subtract))
                step(eng.tensor_tensor(dst[:, :, 1, :], src[:, :, 1, :], mid, ALU.subtract))
            bc = b.rearrange("p (n l) -> p n l", l=CH)
            settle()
            eng.tensor_tensor(dd[:, 7, :, :].rearrange("p h c -> p (h c)").rearrange("p (n l) -> p n l", l=CH),
                              bc[:, :, CH - 1:CH].to_broadcast([128, 8, CH]), bc, ALU.subtract).then_inc(ev("v_dd"), 1)
            yield
            eng.wait_ge(ev("u_exp"), at(i, 1, n + 1))
            if running:
                step(eng.tensor_tensor(u[:, 0:4, :], u[:, 0:4, :], cm(C_PAD).unsqueeze(1).to_broadcast([128, 4, 128]), ALU.mult))
                settle()
            step(eng.tensor_tensor_scan(cs[:, :, :].rearrange("p a b -> p (a b)"), reset[:, :, :, :].rearrange("p a b c -> p (a b c)"),
                                        u[:, 0:4, :].rearrange("p a b -> p (a b)"), 0.0, ALU.mult, ALU.add))
            settle()
            eng.tensor_tensor(cx[:, :, :], cs[:, :, :], u[:, 0:4, :], ALU.subtract).then_inc(ev("cs_ready"), 1)
            step(eng.scalar_tensor_tensor(kn[:, :, :], u[:, 4:8, :], -1.0, column("ka"), ALU.add, ALU.mult))
            settle()
            if running:
                step(eng.scalar_tensor_tensor(kn[:, :, :], kn[:, :, :], 1.0, pm[:, 4:8, :], ALU.add, ALU.mult))
                settle()
                eng.tensor_tensor(kn[:, :, :], kn[:, :, :], cm(C_PAD).unsqueeze(1).to_broadcast([128, 4, 128]), ALU.mult).then_inc(ev("kn_ready"), 1)
            else:
                eng.scalar_tensor_tensor(kn[:, :, :], kn[:, :, :], 1.0, pm[:, 4:8, :], ALU.add, ALU.mult).then_inc(ev("kn_ready"), 1)
            yield
            eng.wait_ge(ev("q_ready"), at(i, 1, n + 1))
            eng.wait_ge(ev("a_dd"), at(i, 1, n + 1))
            step(eng.tensor_copy(hdec[:, :, :], dd[:, 6, :, :].rearrange("p h (c l) -> p h c l", l=CH)[:, :, :, CH - 1]))
            for lv in range(levels):
                half = 1 << lv
                cut = [y.rearrange("p h c -> p (h c)").rearrange("p (n a l) -> p n a l", a=2, l=half)
                       for y in (dd[:, lv, :, :], q[:, :, :])]
                step(eng.tensor_tensor(cut[0][:, :, 1, :], cut[0][:, :, 1, :], cut[1][:, :, 1, :], ALU.mult))
            settle()
            eng.tensor_tensor(dd[:, 6, :, :], dd[:, 6, :, :], q[:, :, :], ALU.mult).then_inc(ev("h_ready"), 1)
            yield

        @block.tensor
        def _(eng):
            eng.wait_ge(ev("const_in"), 16 * 15)
            eng.transpose(P[0][:, 0:N_PRM], prm_rows[:, :], ident[0:N_PRM, 0:N_PRM]).then_inc(ev("prm_turned"), 1)
            eng.wait_ge(ev("prm_ready"), 1)
            eng.wait_ge(ev("zeroed"), n_zeroed)

            def second_factors(i, n):
                if n:
                    eng.wait_ge(ev("bonus_kept"), at(i, 1, n))
                    eng.wait_ge(ev("h_mixed"), at(i, 1, n))
                eng.wait_ge(ev("lora_ready"), at(i, 1, n + 1))
                for c in range(4):
                    eng.matmul(P[6][:, 128 * c:128 * c + 128], fw2[0:64, 128 * c:128 * c + 128], te[0:64, 0, :],
                               start=(c == 0), stop=(c == 3), skip_group_check=True)
                for c in range(4):
                    ins = eng.matmul(P[7][:, 128 * c:128 * c + 128], fw2[64:128, 128 * c:128 * c + 128], te[64:128, 0, :],
                                     start=(c == 0), stop=(c == 3), skip_group_check=True)
                ins.then_inc(ev("wa_made"), 1)

            def key_norms(i, n):
                eng.wait_ge(ev("wa_read"), at(i, 1, n + 1))
                eng.wait_ge(ev("k_squared"), at(i, 1, n + 1))
                eng.matmul(P[6][:, :], cm(C_HEAD), sq[:, :, :].rearrange("p a b -> p (a b)"), start=True, stop=True).then_inc(ev("norm_made"), 1)

            second_factors(None, 0)
            key_norms(None, 0)
            with eng.Fori(0, n_tiles) as i:
                if running:
                    eng.wait_ge(ev("p_mix_read"), i + 1)
                eng.matmul(P[2][:, :], te[:, 1, :], fg2[:, :], start=True, stop=True).then_inc(ev("gate_made"), 1)
                eng.wait_ge(ev("mixed_rkv"), i + 1)
                for c in range(4):
                    ins = eng.transpose(P[0][:, 128 * c:128 * c + 128], pm[:, 8 + c, :], ident)
                ins.then_inc(ev("v_turned"), 1)
                eng.wait_ge(ev("h_ready"), i + 1)
                eng.wait_ge(ev("h_keys_ready"), i + 1)
                for n in range(1 + levels):
                    bank = P[4 + n % 2]
                    if n == 2:
                        eng.wait_ge(ev("p_mix_read"), i + 1)
                        for h in range(4):
                            ins = eng.transpose(P[3][:, 128 * h:128 * h + 128], dd[:, 7, h, :], ident)
                        ins.then_inc(ev("kd_turned"), 1)
                    if n >= 2:
                        eng.wait_ge(ev("scored"), i * (1 + levels) + n - 1)
                    for h in range(4):
                        a, b = (sk[:, 4 + h, :], q[:, h, :]) if n == 0 else (dd[:, n - 1, h, :], dd[:, n - 1, h, :])
                        ins = eng.matmul(bank[:, 128 * h:128 * h + 128], a, b, start=(h == 0), stop=(h == 3), skip_group_check=True)
                    ins.then_inc(ev("score_made"), 1)
                eng.wait_ge(ev("kd_kept"), i + 1)
                for c in range(2):
                    r = slice(CH * c, CH * c + CH)
                    eng.wait_ge(ev("scored"), i * (1 + levels) + levels + c)
                    for h in range(4):
                        ins = eng.matmul(P[5 - c][:, 128 * h:128 * h + 128], kdT[r, h, :], vin[r, 0, 128 * h:128 * h + 128],
                                         start=(h == 0), stop=(h == 3), skip_group_check=True)
                    ins.then_inc(ev("h_update_made"), 1)
                for h in range(4):
                    eng.matmul(P[7][:, 128 * h:128 * h + 128], at_[:, h, :], vin[:, 0, 128 * h:128 * h + 128],
                               start=(h == 0), stop=False, skip_group_check=True)
                if running:
                    eng.wait_ge(ev("s_in"), i * 96 + 96)
                for c in range(2):
                    r = slice(CH * c, CH * c + CH)
                    if c or not running:
                        eng.wait_ge(ev("h_updated"), i * 2 + c + 1)
                    for h in range(4):
                        ins = eng.matmul(P[7][r, 128 * h:128 * h + 128], dd[:, 6, h, r], S[:, c, h, :],
                                         start=False, stop=(h == 3 and c == 1), skip_group_check=True)
                    ins.then_inc(ev("o_made"), 1)
                eng.wait_ge(ev("o_made"), i * 2 + 2)
                eng.sem_inc(ev("h_used"), 1)
                if running:
                    eng.wait_ge(ev("gate_read"), i + 1)
                    for c in range(2):
                        for y in range(4):
                            ins = eng.transpose(P[3 - c][:, 128 * y:128 * y + 128], srow[:, c, y, :], ident)
                        ins.then_inc(ev("st_turned"), 1)
                eng.wait_ge(ev("rw_ready"), i + 1)
                eng.wait_ge(ev("gate_read"), i + 1)
                if running:
                    eng.wait_ge(ev("st_kept"), i * 2 + 2)
                for bank, x, j in ((1, AR, 0), (2, BK, 0), (3, BK, 1)):
                    for c in range(4):
                        ins = eng.transpose(P[bank][:, 128 * c:128 * c + 128], x[:, c, j, :], ident)
                    ins.then_inc(ev("tok_turned"), 1)
                eng.wait_ge(ev("norm_read"), i + 1)
                eng.wait_ge(ev("bon_ready"), i + 1)
                for c in range(4):
                    ins = eng.matmul(P[6][:, 2 * c:2 * c + 2], bon[:, c, :], cm(C_HEAD)[:, 0:128:64], start=(c == 0), stop=(c == 3),
                                     skip_group_check=True)
                ins.then_inc(ev("bonus_made"), 1)
                eng.wait_ge(ev("h_updated"), i * 2 + 2 + 1)
                banks = [4, 5, 0, 3]
                n = 0
                for pairs in range(2):
                    for kind, j in ((0, 0), (0, 1), (1, 0), (1, 1)):
                        bank = P[banks[n % 4]]
                        if n == 2:
                            eng.wait_ge(ev("v_kept"), i + 1)
                        if n == 3:
                            eng.wait_ge(ev("tok_kept"), i + 1)
                        if n >= 4:
                            eng.wait_ge(ev("product_kept"), i * 10 + n - 3)
                        o = slice(64 * j, 64 * j + 64)
                        a, b = (BK, AR) if kind == 0 else (AR, BK)
                        for m in range(2):
                            ins = eng.matmul(bank[:, 256 * m:256 * m + 256], a[o, 2 * pairs + m, 0, :],
                                             b[o, 2 * pairs + m, :, :].rearrange("p a b -> p (a b)"), start=(m == 0), stop=(m == 1),
                                             skip_group_check=True)
                        ins.then_inc(ev("product_made"), 1)
                        n += 1
                for g in range(2):
                    eng.wait_ge(ev("product_kept"), i * 10 + n - 3)
                    o = slice(64 * g, 64 * g + 64)
                    for h in range(4):
                        ins = eng.matmul(P[banks[n % 4]][:, 128 * h:128 * h + 128], BK[o, h, 1, :], AR[o, h, 1, :],
                                         start=(h == 0), stop=(h == 3), skip_group_check=True)
                    ins.then_inc(ev("product_made"), 1)
                    n += 1
                second_factors(i, 1)
                eng.wait_ge(ev("product_kept"), i * 10 + 10)
                eng.wait_ge(ev("x_begun"), i + 1)
                for g in range(2):
                    eng.matmul(P[g][:, :], ident, X[:, 4 * g:4 * g + 4, :].rearrange("p a b -> p (a b)"), start=True, stop=False, skip_group_check=True)
                for lv in range(1, levels):
                    k = lv - 1
                    for g in range(2):
                        if lv > 1:
                            eng.wait_ge(ev("x_kept"), i * n_x + 2 * (k - 1) + g + 1)
                        for h in range(4 * g, 4 * g + 4):
                            ins = eng.matmul(P[4 + g][:, 128 * (h % 4):128 * (h % 4) + 128], LB[:, h, 0, :], X[:, h, :],
                                             start=(h % 4 == 0), stop=(h % 4 == 3), skip_group_check=True)
                        ins.then_inc(ev("y_made"), 1)
                    if lv == 2:
                        key_norms(i, 1)
                    if lv == 1:
                        eng.wait_ge(ev("xt_begun"), i + 1)
                        for g in range(2):
                            eng.matmul(P[2 + g][:, :], ident, XT[:, 4 * g:4 * g + 4, :].rearrange("p a b -> p (a b)"), start=True, stop=False,
                                       skip_group_check=True)
                    for g in range(2):
                        eng.wait_ge(ev("y_kept"), i * n_y + 2 * k + g + 1)
                        if lv > 1:
                            eng.wait_ge(ev("xt_kept"), i * n_y + 2 * (k - 1) + g + 1)
                        if lv < levels - 1:
                            for h in range(4 * g, 4 * g + 4):
                                ins = eng.matmul(P[g][:, 128 * (h % 4):128 * (h % 4) + 128], XT[:, h, :], Y[:, h, :],
                                                 start=False, stop=False, skip_group_check=True)
                            ins.then_inc(ev("x_made"), 1)
                        for h in range(4 * g, 4 * g + 4):
                            ins = eng.matmul(P[2 + g][:, 128 * (h % 4):128 * (h % 4) + 128], Y[:, h, :], XT[:, h, :],
                                             start=False, stop=(lv == levels - 1 and h % 4 == 3), skip_group_check=True)
                        ins.then_inc(ev("xt_made"), 1)
                eng.wait_ge(ev("xt_kept"), i * n_y + n_y - 1)
                for g in range(2):
                    if g:
                        eng.wait_ge(ev("xt_kept"), i * n_y + n_y)
                    for h in range(4 * g, 4 * g + 4):
                        ins = eng.matmul(P[g][:, 128 * (h % 4):128 * (h % 4) + 128], LM[:, h, 1, :], XT[:, h, :],
                                         start=(h % 4 == 0), stop=(h % 4 == 3), skip_group_check=True)
                    ins.then_inc(ev("mx_made"), 1)
                for h in range(8):
                    o = slice(64 * (h % 2), 64 * (h % 2) + 64)
                    ins = eng.matmul(P[4][o, 128 * (h // 2):128 * (h // 2) + 128], tok[:, 1, 64 * h:64 * h + 64], XT[:, h, :],
                                     start=(h < 2), stop=(h >= 6), skip_group_check=True)
                ins.then_inc(ev("ax_made"), 1)
                eng.wait_ge(ev("v_kept"), i + 1)
                for h in range(8):
                    eng.matmul(P[3][:, 64 * h:64 * h + 64], KR[:, h, :], tok[:, 0, 64 * h:64 * h + 64],
                               start=(h == 0), stop=False, skip_group_check=True)
                eng.wait_ge(ev("mx_kept"), i + 1)
                for h in range(8):
                    eng.matmul(P[2][:, 64 * h:64 * h + 64], MX[:, h, :], tok[:, 0, 64 * h:64 * h + 64],
                               start=(h == 0), stop=False, skip_group_check=True)
                for c in range(2):
                    r = slice(CH * c, CH * c + CH)
                    for m in range(4):
                        o = slice(128 * m, 128 * m + 128)
                        eng.matmul(P[c][:, o], tok[r, 3, o], tok[r, 0, o], start=(m == 0), stop=False, skip_group_check=True)
                    if c == 0:
                        eng.wait_ge(ev("ax_kept"), i + 1)
                    if c or not running:
                        eng.wait_ge(ev("st_updated"), i * 2 + c + 1)
                    for m in range(4):
                        o = slice(128 * m, 128 * m + 128)
                        ins = eng.matmul(P[2][r, o], XA[:, m, r], ST[:, c, m, :], start=False, stop=(m == 3), skip_group_check=True)
                    ins.then_inc(ev("sa_made"), 1)
                    for m in range(4):
                        o = slice(128 * m, 128 * m + 128)
                        eng.matmul(P[3][r, o], AR[:, m, 1, r], ST[:, c, m, :], start=False, stop=False, skip_group_check=True)
                    eng.wait_ge(ev("sa_kept"), i * 2 + c + 1)
                    for m in range(4):
                        o = slice(128 * m, 128 * m + 128)
                        ins = eng.matmul(P[c][:, o], tok[r, 2, o], SA[r, o], start=False, stop=(m == 3), skip_group_check=True)
                    ins.then_inc(ev("st_made"), 1)
                for h in range(8):
                    ins = eng.matmul(P[3][:, 64 * h:64 * h + 64], LB[:, h, 1, :], SA[:, 64 * h:64 * h + 64],
                                     start=False, stop=(h == 7), skip_group_check=True)
                ins.then_inc(ev("y_out_made"), 1)
                if running:
                    eng.wait_ge(ev("st_updated"), i * 2 + 2 + 1)
                    for c in range(2):
                        for y in range(4):
                            ins = eng.transpose(P[4 + c][:, 128 * y:128 * y + 128], ST[:, 2 + c, y, :], ident)
                    ins.then_inc(ev("st_back_made"), 1)
            if not running:
                eng.wait_ge(ev("st_updated"), 2 * n_tiles + 1)
                for y in range(4):
                    ins = eng.transpose(P[4][:, 128 * y:128 * y + 128], ST[:, 0, y, :], ident)
                ins.then_inc(ev("st_back_made"), 1)

        @block.scalar
        def _(eng):
            eng.preload_act_table_set("natural_log_exp_and_others")
            eng.wait_ge(ev("one_made"), 1)
            eng.wait_ge(ev("zeroed"), n_zeroed)
            for _ in prep_scalar(eng, None, 0):
                pass
            with eng.Fori(0, n_tiles) as i:
                eng.wait_ge(ev("v_turned"), i + 1)
                eng.copy(tok[:, 0, :], P[0][:, :]).then_inc(ev("v_kept"), 1)
                eng.wait_ge(ev("kd_turned"), i + 1)
                eng.copy(kdT[:, :, :].rearrange("p a b -> p (a b)"), P[3][:, :]).then_inc(ev("kd_kept"), 1)
                eng.wait_ge(ev("gate_made"), i + 1)
                eng.wait_ge(ev("mixed"), i + 1)
                eng.copy(gate[:, :], P[2][:, :]).then_inc(ev("gate_read"), 1)
                eng.wait_ge(ev("h_used"), i + 1)
                eng.activation(osq[:, :], P[7][:, :], ACT.Square).then_inc(ev("o_squared"), 1)
                if running:
                    for c in range(2):
                        eng.wait_ge(ev("st_turned"), i * 2 + c + 1 + 1)
                        eng.copy(ST[:, c, :, :].rearrange("p b c -> p (b c)"), P[3 - c][:, :]).then_inc(ev("st_kept"), 1)
                eng.wait_ge(ev("o_var"), i + 1)
                eng.activation(hst[:, 1, :], hst[:, 1, :], ACT.Ln).then_inc(ev("a_o1"), 1)
                eng.wait_ge(ev("a_o1"), i + 1)
                eng.activation(hst[:, 1, :], hst[:, 1, :], ACT.Exp, scale=-0.5).then_inc(ev("o_scale"), 1)
                prep = prep_scalar(eng, i, 1)
                next(prep)
                for n in range(3):
                    eng.wait_ge(ev("tok_turned"), i * 3 + n + 1)
                    ins = eng.copy(tok[:, 1 + n, :], P[1 + n][:, :])
                ins.then_inc(ev("tok_kept"), 1)
                next(prep)
                for lv in range(1, levels):
                    k = lv - 1
                    next(prep, None)
                    for g in range(2):
                        if lv < levels - 1:
                            eng.wait_ge(ev("x_made"), i * n_x + 2 * k + g + 1)
                            eng.copy(X[:, 4 * g:4 * g + 4, :].rearrange("p a b -> p (a b)"), P[g][:, :]).then_inc(ev("x_kept"), 1)
                        eng.wait_ge(ev("xt_made"), i * n_y + 2 * k + g + 1)
                        eng.copy(XT[:, 4 * g:4 * g + 4, :].rearrange("p a b -> p (a b)"), P[2 + g][:, :]).then_inc(ev("xt_kept"), 1)
                for g in range(2):
                    eng.wait_ge(ev("mx_made"), i * 2 + g + 1)
                    ins = eng.copy(MX[:, 4 * g:4 * g + 4, :].rearrange("p a b -> p (a b)"), P[g][:, :])
                ins.then_inc(ev("mx_kept"), 1)
                for _ in prep:
                    pass
                for c in range(2):
                    r = slice(CH * c, CH * c + CH)
                    eng.wait_ge(ev("sa_made"), i * 2 + c + 1)
                    eng.copy(SA[r, :], P[2][r, :]).then_inc(ev("sa_kept"), 1)
                if running:
                    eng.wait_ge(ev("st_back_made"), i + 1)
                    for c in range(2):
                        for g in range(2):
                            o = slice(64 * g, 64 * g + 64)
                            ins = eng.copy(sout[o, c, :, :], heads(P[4 + c][:, :])[o, :, o])
                    ins.then_inc(ev("st_turned_back"), 1)
                eng.wait_ge(ev("y_centred"), i + 1)
                eng.activation(ysq[:, :], yc[:, :], ACT.Square).then_inc(ev("y_squared"), 1)
                eng.wait_ge(ev("y_var"), i + 1)
                eng.activation(rst[:, 2, :], rst[:, 1, :], ACT.Ln).then_inc(ev("a_y1"), 1)
                eng.wait_ge(ev("a_y1"), i + 1)
                eng.activation(rst[:, 2, :], rst[:, 2, :], ACT.Exp, scale=-0.5).then_inc(ev("y_scale"), 1)
            if not running:
                eng.wait_ge(ev("st_back_made"), 1)
                for g in range(2):
                    o = slice(64 * g, 64 * g + 64)
                    ins = eng.copy(sout[o, 0, :, :], heads(P[4][:, :])[o, :, o])
                ins.then_inc(ev("st_turned_back"), 1)

        @block.vector
        def _(eng):
            count = 0
            vstep = ev("vector_step")

            def step(ins):
                nonlocal count
                count += 1
                ins.then_inc(vstep, 1)

            def settle():
                eng.wait_ge(vstep, count)

            def restart():
                nonlocal count
                settle()
                eng.sem_clear(vstep)
                count = 0

            eng.wait_ge(ev("prm_turned"), 1)
            eng.tensor_copy(prm[:, :], P[0][:, 0:N_PRM]).then_inc(ev("prm_ready"), 1)
            eng.wait_ge(ev("prm_ready"), 1)
            eng.wait_ge(ev("zeroed"), n_zeroed)
            for _ in prep_vector(eng, None, 0, step, settle):
                pass
            restart()

            def operands(i):
                eng.wait_ge(ev("e_ready"), i + 1)
                eng.wait_ge(ev("kr_ready"), i + 1)
                step(eng.scalar_tensor_tensor(AR[:, :, 0, :], kr[:, :, :], -1.0, e3[:, :, :], ALU.mult, ALU.mult))
                step(eng.tensor_tensor(AR[:, :, 1, :], pm[:, 0:4, :], e1[:, :, :], ALU.mult))
                yield
                step(eng.tensor_tensor(BK[:, :, 1, :], kn[:, :, :], e2[:, :, :], ALU.mult))
                yield
                step(eng.tensor_tensor(BK[:, :, 0, :], kra[:, :, :], e2[:, :, :], ALU.mult))
                yield
                for c in range(2):
                    step(eng.tensor_tensor(wm[:, c, :, :], cm(C_HEAD).unsqueeze(1).to_broadcast([128, 4, 128]),
                                           e1[:, :, CH * c + CH - 1:CH * c + CH].to_broadcast([128, 4, 128]), ALU.mult))
                settle()
                eng.sem_inc(ev("rw_ready"), 1)

            with eng.Fori(0, n_tiles) as i:
                made = operands(i)
                for n in range(1 + levels):
                    eng.wait_ge(ev("score_made"), i * (1 + levels) + n + 1)
                    eng.sem_inc(ev("score_seen"), 1)
                    bank = heads(P[4 + n % 2][:, :])
                    if n == 0:
                        eng.tensor_tensor(at_[:, :, :], bank, ident.unsqueeze(1).to_broadcast([128, 4, 128]), ALU.mult).then_inc(ev("scored"), 1)
                    else:
                        eng.wait_ge(ev("scored"), i * (1 + levels) + n)
                        eng.sem_inc(ev("score_seen"), 1)
                        eng.copy_predicated(at_[:, :, :], cm(C_LEVEL + n - 1).bitcast(U32).unsqueeze(1).to_broadcast([128, 4, 128]), bank).then_inc(ev("scored"), 1)
                    if n:
                        next(made, None)
                for c in range(2):
                    eng.wait_ge(ev("h_update_made"), i * 2 + c + 1)
                    if running and c == 0:
                        eng.wait_ge(ev("s_in"), i * 96 + 96)
                    to = 2 + c if running else 1 - c
                    if c and not running:
                        eng.wait_ge(ev("o_made"), i * 2 + 1)
                    for h in range(4):
                        ins = eng.scalar_tensor_tensor(S[:, to, h, :], S[:, c, h, :], hdec[:, h, c:c + 1],
                                                       P[5 - c][:, 128 * h:128 * h + 128], ALU.mult, ALU.add)
                    ins.then_inc(ev("h_updated"), 1)
                    if not running:
                        eng.wait_ge(ev("h_updated"), i * 2 + c + 1 + 1)
                eng.wait_ge(ev("o_squared"), i + 1)
                step(eng.tensor_reduce(hst[:, 0, :], heads(osq[:, :]), AX.X, ALU.add))
                settle()
                eng.tensor_scalar(hst[:, 1, :], hst[:, 0, :], 1.0 / 128, NORM_EPS, ALU.mult, ALU.add).then_inc(ev("o_var"), 1)
                eng.wait_ge(ev("o_scale"), i + 1)
                eng.wait_ge(ev("mix_out"), i * (32 if running else 16) + 16)
                step(eng.tensor_tensor(heads(mix[:, 0:512]), heads(P[7][:, :]), hst[:, 1, :].unsqueeze(2).to_broadcast([128, 4, 128]), ALU.mult))
                settle()
                eng.wait_ge(ev("gs_ready"), i + 1)
                eng.tensor_tensor(mix[:, 0:512], mix[:, 0:512], gs[:, :], ALU.mult).then_inc(ev("h_mixed"), 1)
                n = 0
                banks = [4, 5, 0, 3]
                masks = (const[:, C_STRICT:C_STRICT + 2, :], const[:, C_LOWER:C_LOWER + 2, :])
                prep = prep_vector(eng, i, 1, step, settle)
                next(prep)
                eng.wait_ge(ev("bonus_made"), i + 1)
                eng.tensor_copy(bonus[:, :], P[6][:, 0:8]).then_inc(ev("bonus_kept"), 1)
                for pairs in range(2):
                    for kind, j in ((0, 0), (0, 1), (1, 0), (1, 1)):
                        eng.wait_ge(ev("product_made"), i * 10 + n + 1)
                        out = (LB, LM)[kind][:, 4 * pairs + j:4 * pairs + j + 3:2, :, :]
                        m = masks[kind].rearrange("p a b -> p (a b)").unsqueeze(1).to_broadcast([128, 2, 256])
                        eng.tensor_tensor(out.rearrange("p h a b -> p h (a b)"), P[banks[n % 4]][:, :].rearrange("p (h c) -> p h c", h=2),
                                          m, ALU.mult).then_inc(ev("product_kept"), 1)
                        n += 1
                    eng.wait_ge(ev("product_kept"), i * 10 + n)
                    xs = X[:, 4 * pairs:4 * pairs + 4, :]
                    step(eng.tensor_tensor(xs, LM[:, 4 * pairs:4 * pairs + 4, 0, :], cm(C_LEVEL_T).unsqueeze(1).to_broadcast([128, 4, 128]), ALU.mult))
                    settle()
                    step(eng.tensor_tensor(xs, xs, ident.unsqueeze(1).to_broadcast([128, 4, 128]), ALU.add))
                settle()
                eng.sem_inc(ev("x_begun"), 1)
                for g in range(2):
                    eng.wait_ge(ev("product_made"), i * 10 + n + 1)
                    eng.tensor_tensor(KR[:, g:8:2, :], heads(P[banks[n % 4]][:, :]),
                                      cm(C_INCL).unsqueeze(1).to_broadcast([128, 4, 128]), ALU.mult).then_inc(ev("product_kept"), 1)
                    n += 1
                next(prep)
                for lv in range(1, levels):
                    k = lv - 1
                    for g in range(2):
                        eng.wait_ge(ev("y_made"), i * n_y + 2 * k + g + 1)
                        eng.tensor_tensor(Y[:, 4 * g:4 * g + 4, :], heads(P[4 + g][:, :]),
                                          cm(C_LEVEL_T + lv).unsqueeze(1).to_broadcast([128, 4, 128]), ALU.mult).then_inc(ev("y_kept"), 1)
                    next(prep, None)
                for _ in prep:
                    pass
                eng.wait_ge(ev("ax_made"), i + 1)
                eng.tensor_copy(XA[:, :, :], heads(P[4][:, :])).then_inc(ev("ax_kept"), 1)
                for c in range(2):
                    eng.wait_ge(ev("st_made"), i * 2 + c + 1)
                    to = 2 + c if running else 1 - c
                    if running:
                        eng.wait_ge(ev("st_kept"), i * 2 + 2)
                    step(eng.tensor_tensor(ST[:, to, :, :], ST[:, c, :, :], heads(P[c][:, :]), ALU.add))
                    settle()
                    eng.tensor_tensor(ST[:, to, :, :], ST[:, to, :, :], wm[:, c, :, :], ALU.mult).then_inc(ev("st_updated"), 1)
                    if not running:
                        eng.wait_ge(ev("st_updated"), i * 2 + c + 1 + 1)
                eng.wait_ge(ev("y_out_made"), i + 1)
                y8 = heads(P[3][:, :], 8)

                def by_head(x):
                    return x.unsqueeze(2).to_broadcast([128, 8, RW_N])

                step(eng.tensor_reduce(rst[:, 0, :], y8, AX.X, ALU.add))
                settle()
                step(eng.tensor_scalar(rst[:, 0, :], rst[:, 0, :], 1.0 / RW_N, None, ALU.mult))
                settle()
                eng.wait_ge(ev("mixed"), i + 1)
                eng.tensor_tensor(heads(yc[:, :], 8), y8, by_head(rst[:, 0, :]), ALU.subtract).then_inc(ev("y_centred"), 1)
                if not running:
                    eng.wait_ge(ev("y_centred"), i + 1)
                    eng.sem_inc(ev("p_mix_read"), 1)
                eng.wait_ge(ev("y_squared"), i + 1)
                if running:
                    eng.sem_inc(ev("p_mix_read"), 1)
                step(eng.tensor_reduce(rst[:, 1, :], heads(ysq[:, :], 8), AX.X, ALU.add))
                settle()
                eng.tensor_scalar(rst[:, 1, :], rst[:, 1, :], 1.0 / RW_N, GN_EPS, ALU.mult, ALU.add).then_inc(ev("y_var"), 1)
                eng.wait_ge(ev("y_scale"), i + 1)
                eng.tensor_tensor(heads(yc[:, :], 8), heads(yc[:, :], 8), by_head(rst[:, 2, :]), ALU.mult).then_inc(ev("y_scaled"), 1)
                restart()
    finish(nc, names)


N_GROUPS, PER_GROUP = 4, 8
N_EXPERTS = N_GROUPS * PER_GROUP
TOP_K = 2
D_EXPERT = 512
BLOCK = 128
MAX_BLOCKS = T * TOP_K // BLOCK + N_EXPERTS
PACK = 32
LOWEST = -3.0e38


def load_expert(eng, t, e, gate_up, down, loaded):
    for n, name in enumerate(("w_gate", "w_up")):
        eng.dma_start(gate_up[:, n, :, :], t[name][0, ds(e, 1)].rearrange("e (k p) n -> p (e k) n", p=128)).then_inc(loaded[n], 16)
    eng.dma_start(down[:, :, :], t["w_down"][0, ds(e, 1)].rearrange("e (k p) n -> p (e k) n", p=128)).then_inc(loaded[2], 16)


def merge(nc, t, expert, gates, slot0, slot0_loaded):
    names = []
    with ExitStack() as ctx:
        def sb(name, shape, dt=F32):
            return ctx.enter_context(nc.sbuf_tensor("merge_" + name, shape, dt))

        sems = {}

        def ev(name):
            if name not in sems:
                sems[name] = sem_of(nc, names, "merge_" + name)
            return sems[name]

        NR = N_GROUPS + N_EXPERTS
        w = sb("w", [128, KD, D])
        wr = sb("wr", [128, KD, NR])
        wr_bias = sb("wr_bias", [128, NR])
        maps = sb("maps", [128, 2, 3, D])
        ident = sb("ident", [128, 128])
        iota = sb("iota", [128, N_EXPERTS])
        m_in = sb("m_in", [128, 2, D])
        x = sb("x", [128, 2, D])
        mT = sb("mT", [128, 2, KD, 128])
        x1 = sb("x1", [128, 2, D])
        h2 = sb("h2", [128, 2, D])
        h2T = sb("h2T", [128, KD, 128])
        stat = sb("stat", [128, 4])
        lg = sb("lg", [128, NR])
        g8 = sb("g8", [128, 8])
        top = sb("top", [128, 2, 8])
        idx = sb("idx", [128, 2, 8], U32)
        idf = sb("idf", [128, 4])
        sel = sb("sel", [128, N_GROUPS])
        pick = sb("pick", [128, N_GROUPS, PER_GROUP])
        es = sb("es", [128, PER_GROUP])
        ex = sb("ex", [128, 8])
        PT0 = ctx.enter_context(nc.psum_tensor("merge_PT0", [128, KD, 128], F32))
        PT1 = ctx.enter_context(nc.psum_tensor("merge_PT1", [128, KD, 128], F32))
        PO = ctx.enter_context(nc.psum_tensor("merge_PO", [128, 2, 512], F32))
        PR = ctx.enter_context(nc.psum_tensor("merge_PR", [128, 512], F32))

        block = ctx.enter_context(nc.Block())
        LOOP = (NT - 5) // 2

        def tiles(eng, body):
            body(None, 0)
            with eng.Fori(0, LOOP) as i:
                body(i, 1)
                body(i, 2)
            for n in range(2 * LOOP + 1, NT):
                body(None, n)

        @block.sync
        def _(eng):
            eng.dma_start(ident[:, :], t["const"][:, 0:128]).then_inc(ev("w_in"), 16)
            eng.dma_start(w[:, :, :], t["w_out"][0].rearrange("(k p) n -> p k n", p=128)).then_inc(ev("w_in"), 16)
            eng.dma_start(wr[:, :, 0:N_GROUPS], t["router_g_w"][0].rearrange("(k p) n -> p k n", p=128)).then_inc(ev("w_in"), 16)
            for g in range(N_GROUPS):
                c = N_GROUPS + PER_GROUP * g
                eng.dma_start(wr[:, :, c:c + PER_GROUP], t["router_e_w"][0, g].rearrange("(k p) n -> p k n", p=128)).then_inc(ev("w_in"), 16)
            eng.dma_start(wr_bias[:, 0:N_GROUPS], t["router_g_b"].to_broadcast([128, N_GROUPS])).then_inc(ev("w_in"), 16)
            eng.dma_start(wr_bias[:, N_GROUPS:NR], t["router_e_b"].rearrange("a g e -> a (g e)").to_broadcast([128, N_EXPERTS])).then_inc(ev("w_in"), 16)
            eng.dma_start(iota[:, :], t["iota"][:, 0:N_EXPERTS]).then_inc(ev("w_in"), 16)
            for n, row in enumerate((GATE1, SCALE2, SHIFT2)):
                eng.dma_start(maps[:, 0, n, :], t["mods"][0:1, row * D:row * D + D].to_broadcast([128, D])).then_inc(ev("w_in"), 16)
                for s in range(NSEQ):
                    eng.dma_start(maps[DEC * s:DEC * s + DEC, 1, n, :],
                                  t["mods"][1 + s:2 + s, row * D:row * D + D].to_broadcast([DEC, D])).then_inc(ev("w_in"), 16)

            def at_tile(i, n):
                return n * 128 if i is None else i * 256 + n * 128

            def load_m(i, n):
                if n >= 2:
                    eng.wait_ge(ev("m_turned"), at(i, 2, n - 1))
                eng.dma_start(m_in[:, n % 2, :], t["mix"][ds(at_tile(i, n), 128), :]).then_inc(ev(f"m_in{n % 2}"), 16)

            def load_x(i, n):
                if i is None and n == NT - 1:
                    src = t["x_sample"].rearrange("b t d -> (b t) d")
                else:
                    src = t["x_prompt"][0, ds(at_tile(i, n), 128), :]
                eng.dma_start(x[:, n % 2, :], src).then_inc(ev(f"x_in{n % 2}"), 16)

            def body(i, n):
                p = n % 2
                ahead = not (i is None and n + 2 > NT - 1)
                if ahead:
                    load_m(i, n + 2)
                eng.wait_ge(ev("x1_ready"), at(i, 2, n + 1))
                eng.dma_start(t["x1"][ds(at_tile(i, n), 128), :], x1[:, p, :]).then_inc(ev(f"x1_out{p}"), 16)
                if ahead:
                    load_x(i, n + 2)
                eng.wait_ge(ev("h2_ready"), at(i, 2, n + 1))
                eng.dma_start(t["h2"][ds(at_tile(i, n), 128), :], h2[:, p, :]).then_inc(ev(f"h2_out{p}"), 16)

            for n in range(2):
                load_m(None, n)
                load_x(None, n)
            load_expert(eng, t, 0, slot0[0], slot0[1], slot0_loaded)
            tiles(eng, body)
            for p in range(2):
                eng.wait_ge(ev(f"x1_out{p}"), 16 * ((NT + 1 - p) // 2))
                eng.wait_ge(ev(f"h2_out{p}"), 16 * ((NT + 1 - p) // 2))

        @block.tensor
        def _(eng):
            eng.wait_ge(ev("w_in"), 16 * (10 + 3 * (1 + NSEQ)))

            def turn_m(i, n):
                eng.wait_ge(ev(f"m_in{n % 2}"), at(i, 16, 16 * (n // 2 + 1)))
                if n:
                    eng.wait_ge(ev("mT_kept"), at(i, 4, 2 * n))
                for k in range(KD):
                    ins = eng.transpose(PT0[:, k, :], m_in[:, n % 2, 128 * k:128 * k + 128], ident[:, :])
                ins.then_inc(ev("m_turned"), 1)

            def out(i, n):
                eng.wait_ge(ev("mT_kept"), at(i, 4, 2 * n + 2))
                if n:
                    eng.wait_ge(ev("out_read"), at(i, 2, n))
                for half in range(2):
                    for k in range(KD):
                        ins = eng.matmul(PO[:, half, :], mT[:, n % 2, k, :], w[:, k, 512 * half:512 * half + 512],
                                         start=(k == 0), stop=(k == KD - 1))
                ins.then_inc(ev("out_made"), 1)

            def turn_h(i, n):
                eng.wait_ge(ev("h2_ready"), at(i, 2, n + 1))
                if n:
                    eng.wait_ge(ev("h2T_kept"), at(i, 2, n))
                for k in range(KD):
                    ins = eng.transpose(PT1[:, k, :], h2[:, n % 2, 128 * k:128 * k + 128], ident[:, :])
                ins.then_inc(ev("h2_turned"), 1)

            def logits(i, n):
                eng.wait_ge(ev("h2T_kept"), at(i, 2, n + 1))
                if n:
                    eng.wait_ge(ev("logits_read"), at(i, 2, n))
                for k in range(KD):
                    ins = eng.matmul(PR[:, 0:NR], h2T[:, k, :], wr[:, k, :], start=(k == 0), stop=(k == KD - 1))
                ins.then_inc(ev("logits_made"), 1)

            def body(i, n):
                out(i, n)
                if n:
                    turn_h(i, n - 1)
                if not (i is None and n + 2 > NT - 1):
                    turn_m(i, n + 2)
                if n:
                    logits(i, n - 1)

            turn_m(None, 0)
            turn_m(None, 1)
            tiles(eng, body)
            turn_h(None, NT - 1)
            logits(None, NT - 1)

        @block.scalar
        def _(eng):
            def keep_m(i, n):
                eng.wait_ge(ev("m_turned"), at(i, 2, n + 1))
                if n >= 2:
                    eng.wait_ge(ev("out_made"), at(i, 2, n - 1))
                for half in range(2):
                    eng.copy(mT[:, n % 2, 4 * half:4 * half + 4, :], PT0[:, 4 * half:4 * half + 4, :]).then_inc(ev("mT_kept"), 1)

            def keep_h(i, n):
                eng.wait_ge(ev("h2_turned"), at(i, 2, n + 1))
                if n:
                    eng.wait_ge(ev("logits_made"), at(i, 2, n))
                for half in range(2):
                    ins = eng.copy(h2T[:, 4 * half:4 * half + 4, :], PT1[:, 4 * half:4 * half + 4, :])
                ins.then_inc(ev("h2T_kept"), 1)

            def exponentials(i, n):
                eng.wait_ge(ev("ex_ready"), at(i, 2, n + 1))
                eng.activation(ex[:, 0:5], ex[:, 0:5], ACT.Exp).then_inc(ev("ex_made"), 1)

            def body(i, n):
                if n:
                    keep_h(i, n - 1)
                if not (i is None and n + 2 > NT - 1):
                    keep_m(i, n + 2)
                eng.wait_ge(ev("x1_ready"), at(i, 2, n + 1))
                if n >= 2:
                    eng.wait_ge(ev(f"h2_out{n % 2}"), at(i, 16, 16 * (n // 2)))
                    eng.wait_ge(ev("h2_turned"), at(i, 2, n - 1))
                eng.activation(h2[:, n % 2, :], x1[:, n % 2, :], ACT.Square, accum_out=stat[:, 0:1]).then_inc(ev("squared"), 1)
                eng.wait_ge(ev("var_ready"), at(i, 2, n + 1))
                eng.activation(stat[:, 2:3], stat[:, 1:2], ACT.Ln).then_inc(ev("var_log"), 1)
                eng.wait_ge(ev("var_log"), at(i, 2, n + 1))
                eng.activation(stat[:, 3:4], stat[:, 2:3], ACT.Exp, scale=-0.5).then_inc(ev("root_ready"), 1)
                if n:
                    exponentials(i, n - 1)

            eng.preload_act_table_set("natural_log_exp_and_others")
            keep_m(None, 0)
            keep_m(None, 1)
            tiles(eng, body)
            keep_h(None, NT - 1)
            exponentials(None, NT - 1)

        @block.vector
        def _(eng):
            count = 0
            vstep = ev("vector_step")

            def step(ins):
                nonlocal count
                count += 1
                ins.then_inc(vstep, 1)

            def settle():
                eng.wait_ge(vstep, count)

            def restart():
                nonlocal count
                settle()
                eng.sem_clear(vstep)
                count = 0

            def norm(i, n):
                p = n % 2
                m = maps[:, 1 if i is None and n == NT - 1 else 0, :, :]
                eng.wait_ge(ev("out_made"), at(i, 2, n + 1))
                if n >= 2:
                    eng.wait_ge(ev(f"x1_out{p}"), at(i, 16, 16 * (n // 2)))
                eng.tensor_tensor(x1[:, p, :], PO[:, :, :].rearrange("p a b -> p (a b)"), m[:, 0, :], ALU.mult).then_inc(ev("out_read"), 1)
                eng.wait_ge(ev("out_read"), at(i, 2, n + 1))
                eng.wait_ge(ev(f"x_in{p}"), at(i, 16, 16 * (n // 2 + 1)))
                eng.tensor_tensor(x1[:, p, :], x1[:, p, :], x[:, p, :], ALU.add).then_inc(ev("x1_ready"), 1)
                eng.wait_ge(ev("squared"), at(i, 2, n + 1))
                eng.tensor_scalar(stat[:, 1:2], stat[:, 0:1], 1.0 / D, NORM_EPS, ALU.mult, ALU.add).then_inc(ev("var_ready"), 1)
                eng.wait_ge(ev("root_ready"), at(i, 2, n + 1))
                step(eng.scalar_tensor_tensor(h2[:, p, :], x1[:, p, :], stat[:, 3:4], m[:, 1, :], ALU.mult, ALU.mult))
                settle()
                eng.tensor_tensor(h2[:, p, :], h2[:, p, :], m[:, 2, :], ALU.add).then_inc(ev("h2_ready"), 1)

            def route(i, n):
                tile = n if i is None else i * 2 + n
                eng.wait_ge(ev("logits_made"), at(i, 2, n + 1))
                eng.tensor_tensor(lg[:, :], PR[:, 0:NR], wr_bias[:, :], ALU.add).then_inc(ev("logits_read"), 1)
                eng.wait_ge(ev("logits_read"), at(i, 2, n + 1))
                step(eng.tensor_copy(g8[:, 0:N_GROUPS], lg[:, 0:N_GROUPS]))
                settle()
                step(eng.max(top[:, 0, :], g8[:, :]))
                settle()
                step(eng.max_index(idx[:, 0, :], top[:, 0, :], g8[:, :]))
                settle()
                step(eng.tensor_copy(idf[:, 0:1], idx[:, 0, 0:1]))
                settle()
                step(eng.tensor_scalar(sel[:, :], iota[:, 0:N_GROUPS], idf[:, 0:1], None, ALU.is_equal))
                settle()
                step(eng.tensor_tensor(pick[:, :, :], lg[:, N_GROUPS:NR].rearrange("p (g e) -> p g e", g=N_GROUPS),
                                       sel[:, :].unsqueeze(2).to_broadcast([128, N_GROUPS, PER_GROUP]), ALU.mult))
                settle()
                step(eng.tensor_reduce(es[:, :], pick[:, :, :].rearrange("p g e -> p e g"), AX.X, ALU.add))
                settle()
                step(eng.max(top[:, 1, :], es[:, :]))
                settle()
                step(eng.max_index(idx[:, 1, :], top[:, 1, :], es[:, :]))
                step(eng.tensor_scalar(ex[:, 0:4], lg[:, 0:N_GROUPS], top[:, 0, 0:1], None, ALU.subtract))
                settle()
                eng.tensor_tensor(ex[:, 4:5], top[:, 1, 1:2], top[:, 1, 0:1], ALU.subtract).then_inc(ev("ex_ready"), 1)
                step(eng.tensor_copy(idf[:, 2:4], idx[:, 1, 0:2]))
                settle()
                step(eng.scalar_tensor_tensor(expert[:, ds(tile, 1), :].rearrange("p a b -> p (a b)"), idf[:, 0:1].to_broadcast([128, 2]),
                                              float(PER_GROUP), idf[:, 2:4], ALU.mult, ALU.add))
                eng.wait_ge(ev("ex_made"), at(i, 2, n + 1))
                step(eng.tensor_reduce(ex[:, 5:6], ex[:, 0:4], AX.X, ALU.add))
                step(eng.tensor_scalar(ex[:, 6:7], ex[:, 4:5], 1.0, None, ALU.add))
                settle()
                step(eng.tensor_tensor(ex[:, 5:6], ex[:, 5:6], ex[:, 6:7], ALU.mult))
                settle()
                step(eng.reciprocal(ex[:, 7:8], ex[:, 5:6]))
                settle()
                g = gates[:, ds(tile, 1), :].rearrange("p a b -> p (a b)")
                step(eng.tensor_copy(g[:, 0:1], ex[:, 7:8]))
                step(eng.tensor_tensor(g[:, 1:2], ex[:, 7:8], ex[:, 4:5], ALU.mult))
                restart()

            def body(i, n):
                norm(i, n)
                if n:
                    route(i, n - 1)
                else:
                    restart()

            step(eng.memset(g8[:, :], LOWEST))
            eng.wait_ge(ev("w_in"), 16 * (10 + 3 * (1 + NSEQ)))
            tiles(eng, body)
            route(None, NT - 1)
    finish(nc, names)


def experts(nc, t, expert, gates, slot0, slot0_loaded):
    names = []
    with ExitStack() as ctx:
        def sb(name, shape, dt=F32):
            return ctx.enter_context(nc.sbuf_tensor("moe_" + name, shape, dt))

        sems = {}

        def ev(name):
            if name not in sems:
                sems[name] = sem_of(nc, names, "moe_" + name)
            return sems[name]

        NA = NT * TOP_K
        names += slot0_loaded
        loaded = [slot0_loaded, [ev(f"{name}_in1") for name in ("w_gate", "w_up", "w_down")]]
        KE = D_EXPERT // 128
        wgu = [slot0[0], sb("wgu1", [128, 2, KD, D_EXPERT])]
        wd = [slot0[1], sb("wd1", [128, KE, D])]
        const = sb("const", [128, 3, 128])
        iota = sb("iota", [128, 128])
        tokens = sb("tokens", [128, NT, TOP_K])
        onehot = sb("onehot", [128, NT, TOP_K, N_EXPERTS])
        member = sb("member", [128, NT, N_EXPERTS])
        carry = sb("carry", [128, NT + 1, N_EXPERTS])
        blocks_i = sb("blocks_i", [128, N_EXPERTS], I32)
        blocks_f = sb("blocks_f", [128, 2, N_EXPERTS])
        first_f = sb("first_f", [128, N_EXPERTS])
        table = sb("table", [128, N_EXPERTS // 2 + 1], I32)
        dest_f = sb("dest_f", [128, NT, TOP_K])
        dest = sb("dest", [128, NT, TOP_K], I32)
        block_i = sb("block_i", [128, NA], I32)
        block_f = sb("block_f", [128, NA])
        place = sb("place", [128, NA])
        is_place = sb("is_place", [128, NA, BLOCK])
        is_block = sb("is_block", [128, NA, MAX_BLOCKS + 1])
        rows = sb("rows", [128, MAX_BLOCKS + 1], I32)
        row = sb("row", [128, 2], I32)
        xg = sb("xg", [128, D])
        xT = sb("xT", [128, KD, 128])
        sg = sb("sg", [128, D_EXPERT])
        hid = sb("hid", [128, D_EXPERT])
        hT = sb("hT", [128, KE, 128])
        y = sb("y", [128, D])
        zeros = sb("zeros", [128, D])
        PT = ctx.enter_context(nc.psum_tensor("moe_PT", [128, KD, 128], F32))
        PG = ctx.enter_context(nc.psum_tensor("moe_PG", [128, 2, 512], F32))
        PH = ctx.enter_context(nc.psum_tensor("moe_PH", [128, KE, 128], F32))
        PY = ctx.enter_context(nc.psum_tensor("moe_PY", [128, 2, 512], F32))
        ident = const[:, 0, :]

        def total(eng):
            return eng.value_load(table[0:1, N_EXPERTS // 2:N_EXPERTS // 2 + 1], min_val=N_EXPERTS, max_val=MAX_BLOCKS)

        with nc.Block() as block:
            @block.sync
            def _(eng):
                for n, c in enumerate((C_ID, C_CUM, C_ONES)):
                    eng.dma_start(const[:, n, :], t["const"][:, 128 * c:128 * c + 128]).then_inc(ev("const_in"), 16)
                eng.dma_start(iota[:, :], t["iota"]).then_inc(ev("const_in"), 16)
                eng.dma_start(tokens[:, :, :].rearrange("p a b -> p (a b)"), t["token_ids"]).then_inc(ev("const_in"), 16)
                def load(i, p):
                    eng.wait_ge(ev("slot_free"), at(i, 2, p + 1))
                    load_expert(eng, t, p if i is None else i * 2 + p, wgu[p], wd[p], loaded[p])

                load(None, 1)
                with eng.Fori(1, N_EXPERTS // 2) as i:
                    for p in range(2):
                        load(i, p)

            @block.vector
            def _(eng):
                count = 0
                vstep = ev("vector_step")

                def step(ins):
                    nonlocal count
                    count += 1
                    ins.then_inc(vstep, 1)
                    eng.wait_ge(vstep, count)

                step(eng.memset(zeros[:, :], 0.0))
                step(eng.memset(carry[:, 0, :], 0.0))
                eng.wait_ge(ev("const_in"), 80)
                step(eng.tensor_tensor(onehot[:, :, :, :].rearrange("p a b e -> p (a b) e"), iota[:, 0:N_EXPERTS].unsqueeze(1).to_broadcast([128, NA, N_EXPERTS]),
                                       expert[:, :, :].rearrange("p a b -> p (a b)").unsqueeze(2).to_broadcast([128, NA, N_EXPERTS]), ALU.is_equal))
                step(eng.tensor_tensor(member[:, :, :], onehot[:, :, 0, :], onehot[:, :, 1, :], ALU.add))
                eng.sem_inc(ev("member_ready"), 1)
                eng.wait_ge(ev("counted"), 1)
                for n in range(NT):
                    src = PT[:, :, :].rearrange("p a b -> p (a b)")[:, 32 * n:32 * n + 32] if n < NT - 1 else PY[:, 0, 0:32]
                    step(eng.tensor_tensor(carry[:, n + 1, :], carry[:, n, :], src, ALU.add))
                step(eng.tensor_scalar(blocks_f[:, 0, :], carry[:, NT, :], float(BLOCK - 1), None, ALU.add))
                step(eng.tensor_copy(blocks_i[:, :], blocks_f[:, 0, :]))
                step(eng.tensor_scalar(blocks_i[:, :], blocks_i[:, :], 7, None, ALU.logical_shift_right))
                step(eng.tensor_copy(blocks_f[:, 0, :], blocks_i[:, :]))
                step(eng.tensor_scalar(blocks_f[:, 0, :], blocks_f[:, 0, :], 1.0, None, ALU.max))
                step(eng.memset(blocks_f[:, 1, :], 1.0))
                step(eng.tensor_tensor_scan(first_f[:, :], blocks_f[:, 1, :], blocks_f[:, 0, :], 0.0, ALU.mult, ALU.add))
                step(eng.tensor_copy(table[:, N_EXPERTS // 2:], first_f[:, N_EXPERTS - 1:N_EXPERTS]))
                step(eng.tensor_tensor(first_f[:, :], first_f[:, :], blocks_f[:, 0, :], ALU.subtract))
                pairs_f = blocks_f[:, 1, 0:N_EXPERTS // 2]
                step(eng.scalar_tensor_tensor(pairs_f, first_f[:, 0:N_EXPERTS:2], float(PACK), blocks_f[:, 0, 0:N_EXPERTS:2], ALU.mult, ALU.add))
                step(eng.scalar_tensor_tensor(pairs_f, pairs_f, float(PACK), blocks_f[:, 0, 1:N_EXPERTS:2], ALU.mult, ALU.add))
                step(eng.tensor_copy(table[:, 0:N_EXPERTS // 2], pairs_f))
                eng.sem_inc(ev("table_ready"), 1)
                step(eng.tensor_scalar(first_f[:, :], first_f[:, :], float(BLOCK), -1.0, ALU.mult, ALU.add))
                step(eng.tensor_tensor(member[:, 0:NT - 1, :], carry[:, 0:NT - 1, :], PG[:, 0, :].rearrange("p (a e) -> p a e", e=N_EXPERTS), ALU.add))
                step(eng.tensor_tensor(member[:, NT - 1, :], carry[:, NT - 1, :], PG[:, 1, 0:N_EXPERTS], ALU.add))
                step(eng.tensor_tensor(member[:, :, :], member[:, :, :], first_f[:, :].unsqueeze(1).to_broadcast([128, NT, N_EXPERTS]), ALU.add))
                for j in range(TOP_K):
                    step(eng.tensor_tensor(onehot[:, :, j, :], onehot[:, :, j, :], member[:, :, :], ALU.mult))
                step(eng.tensor_reduce(dest_f[:, :, :].rearrange("p a b -> p (a b)"), onehot[:, :, :, :].rearrange("p a b e -> p (a b) e"), AX.X, ALU.add))
                step(eng.tensor_copy(dest[:, :, :], dest_f[:, :, :]))
                flat = dest[:, :, :].rearrange("p a b -> p (a b)")
                step(eng.tensor_scalar(block_i[:, :], flat, 7, None, ALU.logical_shift_right))
                step(eng.tensor_copy(block_f[:, :], block_i[:, :]))
                step(eng.scalar_tensor_tensor(place[:, :], block_f[:, :], -float(BLOCK), dest_f[:, :, :].rearrange("p a b -> p (a b)"),
                                              ALU.mult, ALU.add))
                for g in range(TOP_K):
                    a = slice(g * NT, g * NT + NT)
                    nb = MAX_BLOCKS + 1
                    step(eng.tensor_tensor(is_block[:, a, :], iota[:, 0:nb].unsqueeze(1).to_broadcast([128, NT, nb]),
                                           block_f[:, a].unsqueeze(2).to_broadcast([128, NT, nb]), ALU.is_equal))
                    step(eng.tensor_tensor(is_block[:, a, :], is_block[:, a, :],
                                           tokens[:, :, :].rearrange("p a b -> p (a b)")[:, a].unsqueeze(2).to_broadcast([128, NT, nb]), ALU.mult))
                    step(eng.tensor_tensor(is_place[:, a, :], iota[:, :].unsqueeze(1).to_broadcast([128, NT, BLOCK]),
                                           place[:, a].unsqueeze(2).to_broadcast([128, NT, BLOCK]), ALU.is_equal))
                    eng.sem_inc(ev("places_ready"), 1)
                eng.wait_ge(ev("rows_made"), 1)
                step(eng.tensor_copy(rows[:, :], PH[:, 0, 0:MAX_BLOCKS + 1]))
                eng.sem_inc(ev("rows_ready"), 1)

                with eng.Fori(0, total(eng)) as g:
                    eng.wait_ge(ev("sigmoid_made"), g + 1)
                    eng.tensor_tensor(sg[:, :], sg[:, :], PG[:, 0, :], ALU.mult).then_inc(ev("silu_made"), 1)
                    eng.wait_ge(ev("gu_made"), g + 1 + 1)
                    eng.wait_ge(ev("silu_made"), g + 1)
                    eng.tensor_tensor(hid[:, :], sg[:, :], PG[:, 1, :], ALU.mult).then_inc(ev("hid_ready"), 1)
                    eng.wait_ge(ev("h_turned"), g + 1)
                    eng.tensor_copy(hT[:, :, :], PH[:, :, :]).then_inc(ev("hT_dve"), 1)
                    eng.wait_ge(ev("y_made"), g + 1)
                    eng.wait_ge(ev("y_out"), g * 16 + 16)
                    eng.tensor_copy(y[:, 0:512], PY[:, 0, :]).then_inc(ev("y_dve"), 1)

            @block.scalar
            def _(eng):
                eng.wait_ge(ev("table_ready"), 1)
                with eng.Fori(total(eng), MAX_BLOCKS + 1) as g:
                    eng.dma_start(t["y_rows"][ds(g * BLOCK, BLOCK), :], zeros[:, :]).then_inc(ev("row_blocks"), 16)
                eng.wait_ge(ev("x_turned"), 1 + 1)
                for half in range(2):
                    eng.copy(xT[:, 4 * half:4 * half + 4, :], PT[:, 4 * half:4 * half + 4, :]).then_inc(ev("xT_kept"), 1)
                with eng.Fori(0, total(eng)) as g:
                    eng.wait_ge(ev("g_made"), g + 1)
                    eng.wait_ge(ev("hid_ready"), g + 1)
                    eng.activation(sg[:, :], PG[:, 0, :], ACT.Sigmoid).then_inc(ev("sigmoid_made"), 1)
                    eng.wait_ge(ev("x_turned"), g + 1 + 2)
                    eng.wait_ge(ev("gu_made"), g + 1 + 1)
                    for half in range(2):
                        eng.copy(xT[:, 4 * half:4 * half + 4, :], PT[:, 4 * half:4 * half + 4, :]).then_inc(ev("xT_kept"), 1)
                    eng.wait_ge(ev("y_made"), g + 1)
                    eng.wait_ge(ev("y_out"), g * 16 + 16)
                    eng.copy(y[:, 512:D], PY[:, 1, :]).then_inc(ev("y_act"), 1)
                    eng.wait_ge(ev("y_act"), g + 1 + 1)
                    eng.wait_ge(ev("y_dve"), g + 1 + 1)
                    eng.dma_start(t["y_rows"][ds(g * BLOCK, BLOCK), :], y[:, :]).then_inc(ev("y_out"), 16)
                    eng.sem_inc(ev("row_blocks"), 16)
                eng.wait_ge(ev("y_out"), total(eng) * 16 + 16)
                eng.sem_inc(ev("all_stored"), 1)
                eng.wait_ge(ev("row_blocks"), 16 * (MAX_BLOCKS + 1))

            @block.gpsimd
            def _(eng):
                eng.wait_ge(ev("rows_ready"), 1)
                n_blocks = total(eng)
                with eng.Fori(0, n_blocks + 1) as g:
                    eng.wait_ge(ev("x_turned"), g + 1)
                    eng.tensor_copy(row[:, 0:1], rows[:, ds(g, 1)]).then_inc(ev("row_ready"), 1)
                    eng.wait_ge(ev("row_ready"), g + 1)
                    eng.sem_inc(ev("gather_begun"), 1)
                    eng.indirect_dma_start(xg[:, :], None, t["h2"][:, :], bass.IndirectOffsetOnAxis(ap=row[:, 0:1], axis=0)).then_inc(ev("gathered"), 16)
                eng.wait_ge(ev("gathered"), n_blocks * 16 + 16)

            @block.tensor
            def _(eng):
                eng.wait_ge(ev("const_in"), 80)
                eng.wait_ge(ev("member_ready"), 1)
                eng.sem_inc(ev("slot_free"), 2)
                for name in ("gu_made", "hid_ready", "x_turned", "y_dve", "y_act"):
                    eng.sem_inc(ev(name), 1)
                eng.sem_inc(ev("y_out"), 16)
                flat = member[:, :, :].rearrange("p a e -> p (a e)")
                eng.matmul(PG[:, 0, :], const[:, 1, :], flat[:, 0:512], start=True, stop=True)
                eng.matmul(PG[:, 1, 0:32], const[:, 1, :], flat[:, 512:544], start=True, stop=True)
                eng.matmul(PT[:, 0:4, :].rearrange("p a b -> p (a b)"), const[:, 2, :], flat[:, 0:512], start=True, stop=True)
                eng.matmul(PY[:, 0, 0:32], const[:, 2, :], flat[:, 512:544], start=True, stop=True).then_inc(ev("counted"), 1)
                for n in range(NA):
                    if n % NT == 0:
                        eng.wait_ge(ev("places_ready"), n // NT + 1)
                    ins = eng.matmul(PH[:, 0, 0:MAX_BLOCKS + 1], is_place[:, n, :], is_block[:, n, :], start=(n == 0), stop=(n == NA - 1))
                ins.then_inc(ev("rows_made"), 1)
                eng.wait_ge(ev("rows_ready"), 1)

                def turn(g, half):
                    if half == 0:
                        eng.wait_ge(ev("gathered"), g * 16 + 16)
                    for k in range(4 * half, 4 * half + 4):
                        ins = eng.transpose(PT[:, k, :], xg[:, 128 * k:128 * k + 128], ident)
                    if half:
                        ins.then_inc(ev("x_turned"), 1)

                turn(0, 0)
                turn(0, 1)
                with eng.Fori(0, N_EXPERTS // 2) as i:
                    packed = eng.value_load(table[0:1, ds(i, 1)], min_val=0, max_val=PACK * PACK * (MAX_BLOCKS + 1) - 1)
                    first, second = packed // PACK % PACK, packed % PACK
                    for p in range(2):
                        before = packed // (PACK * PACK) + first * p
                        blocks = (first, second)[p]
                        for matrix_in in loaded[p]:
                            eng.wait_ge(matrix_in, i * 16 + 16)
                        eng.sem_inc(ev("expert_begun"), 1)
                        with eng.Fori(0, blocks) as b:
                            g = before + b
                            eng.wait_ge(ev("xT_kept"), g * 2 + 2)
                            eng.wait_ge(ev("hid_ready"), g + 1)
                            for n in range(2):
                                for k in range(KD):
                                    ins = eng.matmul(PG[:, n, :], xT[:, k, :], wgu[p][:, n, k, :], start=(k == 0), stop=(k == KD - 1))
                                ins.then_inc(ev("g_made" if n == 0 else "gu_made"), 1)
                            turn(g + 1, 0)
                            eng.wait_ge(ev("hid_ready"), g + 1 + 1)
                            for k in range(KE):
                                ins = eng.transpose(PH[:, k, :], hid[:, 128 * k:128 * k + 128], ident)
                            ins.then_inc(ev("h_turned"), 1)
                            turn(g + 1, 1)
                            eng.wait_ge(ev("hT_dve"), g + 1)
                            eng.wait_ge(ev("y_dve"), g + 1)
                            eng.wait_ge(ev("y_act"), g + 1)
                            for n in range(2):
                                for k in range(KE):
                                    ins = eng.matmul(PY[:, n, :], hT[:, k, :], wd[p][:, k, 512 * n:512 * n + 512], start=(k == 0), stop=(k == KE - 1))
                            ins.then_inc(ev("y_made"), 1)
                            eng.nop()
                        eng.wait_ge(ev("y_made"), before + blocks)
                        eng.sem_inc(ev("slot_free"), 1)

        maps = wgu[0][:, 0, 0:4, :].rearrange("p k n -> p (k n)").rearrange("p (a n) -> p a n", a=2)
        final = wgu[0][:, 1, 0:2, :].rearrange("p k n -> p (k n)")
        pick = [[wgu[1][:, n, 2 * j:2 * j + 2, :].rearrange("p k n -> p (k n)") for j in range(2)] for n in range(2)]
        xr = [wgu[1][:, n, 4:6, :].rearrange("p k n -> p (k n)") for n in range(2)]
        out = [wgu[1][:, n, 6:8, :].rearrange("p k n -> p (k n)") for n in range(2)]
        stat = dest_f

        with nc.Block() as block:
            def tiles(eng, body):
                with eng.Fori(0, NT // 2) as i:
                    body(i, 0)
                    body(i, 1)
                body(None, NT - 1)

            @block.sync
            def _(eng):
                eng.dma_start(maps[:, 0, :], t["mods"][0:1, GATE2 * D:GATE2 * D + D].to_broadcast([128, D])).then_inc(ev("maps_in"), 16)
                for s in range(NSEQ):
                    eng.dma_start(maps[DEC * s:DEC * s + DEC, 1, :], t["mods"][1 + s:2 + s, GATE2 * D:GATE2 * D + D].to_broadcast([DEC, D])).then_inc(ev("maps_in"), 16)
                eng.dma_start(final, t["final_norm_w"].rearrange("(o n) -> o n", o=1).to_broadcast([128, D])).then_inc(ev("maps_in"), 16)
                eng.sem_inc(ev("xr_free"), 2)

                def body(i, n):
                    p = n % 2
                    k = n * 128 if i is None else i * 256 + n * 128
                    eng.wait_ge(ev("xr_free"), at(i, 2, n + 1))
                    eng.dma_start(xr[p], t["x1"][ds(k, 128), :]).then_inc(ev(f"xr_in{p}"), 16)

                tiles(eng, body)

            @block.gpsimd
            def _(eng):
                eng.sem_inc(ev("pick_free"), 2)

                def body(i, n):
                    p = n % 2
                    tile = n if i is None else i * 2 + n
                    eng.wait_ge(ev("pick_free"), at(i, 2, n + 1))
                    eng.tensor_copy(row[:, 0:2], dest[:, ds(tile, 1), :].rearrange("p a b -> p (a b)")).then_inc(ev("pick_ready"), 1)
                    eng.wait_ge(ev("pick_ready"), at(i, 2, n + 1))
                    eng.sem_inc(ev("pick_begun"), 1)
                    for j in range(TOP_K):
                        eng.indirect_dma_start(pick[p][j], None, t["y_rows"][:, :], bass.IndirectOffsetOnAxis(ap=row[:, j:j + 1], axis=0)).then_inc(ev(f"picked{p}"), 16)
                    eng.wait_ge(ev(f"picked{p}"), at(i, 32, 32 * (n // 2 + 1)))

                tiles(eng, body)

            @block.scalar
            def _(eng):
                def body(i, n):
                    p = n % 2
                    k = n * 128 if i is None else i * 256 + n * 128
                    eng.wait_ge(ev("sum_ready"), at(i, 2, n + 1))
                    eng.wait_ge(ev(f"out{p}"), at(i, 16, 16 * (n // 2 + 1)))
                    eng.activation(out[p], xr[p], ACT.Square, accum_out=stat[:, 0, 0:1]).then_inc(ev("final_squared"), 1)
                    eng.wait_ge(ev("final_var"), at(i, 2, n + 1))
                    eng.activation(stat[:, 1, 0:1], stat[:, 0, 1:2], ACT.Sqrt).then_inc(ev("final_root"), 1)
                    eng.wait_ge(ev("final_ready"), at(i, 2, n + 1))
                    if i is None and n == NT - 1:
                        dst = t["y_sample"].rearrange("b t d -> (b t) d")
                    else:
                        dst = t["y_prompt"][0, ds(k, 128), :]
                    eng.dma_start(dst, out[p]).then_inc(ev(f"out{p}"), 16)

                for p in range(2):
                    eng.sem_inc(ev(f"out{p}"), 16)
                tiles(eng, body)
                for p in range(2):
                    eng.wait_ge(ev(f"out{p}"), 16 * ((NT + 1 - p) // 2 + 1))

            @block.vector
            def _(eng):
                fstep = ev("final_step")
                eng.wait_ge(ev("maps_in"), 16 * (2 + NSEQ))

                def body(i, n):
                    p = n % 2
                    tile = n if i is None else i * 2 + n
                    count = 0

                    def step(ins):
                        nonlocal count
                        count += 1
                        ins.then_inc(fstep, 1)
                        eng.wait_ge(fstep, count)

                    eng.wait_ge(ev(f"picked{p}"), at(i, 32, 32 * (n // 2 + 1)))
                    g = gates[:, ds(tile, 1), :].rearrange("p a b -> p (a b)")
                    a, b = pick[p]
                    step(eng.tensor_copy(stat[:, 2, :], g))
                    step(eng.tensor_scalar(a, a, stat[:, 2, 0:1], None, ALU.mult))
                    step(eng.scalar_tensor_tensor(a, b, stat[:, 2, 1:2], a, ALU.mult, ALU.add))
                    step(eng.tensor_tensor(a, a, maps[:, 1 if i is None and n == NT - 1 else 0, :], ALU.mult))
                    eng.wait_ge(ev(f"xr_in{p}"), at(i, 16, 16 * (n // 2 + 1)))
                    eng.tensor_tensor(xr[p], xr[p], a, ALU.add).then_inc(ev("sum_ready"), 1)
                    eng.wait_ge(ev("sum_ready"), at(i, 2, n + 1))
                    eng.sem_inc(ev("pick_free"), 1)
                    eng.wait_ge(ev("final_squared"), at(i, 2, n + 1))
                    eng.tensor_scalar(stat[:, 0, 1:2], stat[:, 0, 0:1], 1.0 / D, NORM_EPS, ALU.mult, ALU.add).then_inc(ev("final_var"), 1)
                    eng.wait_ge(ev("final_root"), at(i, 2, n + 1))
                    step(eng.reciprocal(stat[:, 1, 1:2], stat[:, 1, 0:1]))
                    eng.scalar_tensor_tensor(out[p], xr[p], stat[:, 1, 1:2], final, ALU.mult, ALU.mult).then_inc(ev("final_ready"), 1)
                    eng.wait_ge(ev("final_ready"), at(i, 2, n + 1))
                    eng.sem_inc(ev("xr_free"), 1)
                    eng.sem_clear(fstep)

                tiles(eng, body)
    finish(nc, names)


def program(nc, t):
    project(nc, t)
    recur(nc, t, False)
    recur(nc, t, True)
    with nc.sbuf_tensor("expert", [128, NT, TOP_K], F32) as expert, nc.sbuf_tensor("gates", [128, NT, TOP_K], F32) as gates:
        with nc.sbuf_tensor("wgu0", [128, 2, KD, D_EXPERT], F32) as wgu0, nc.sbuf_tensor("wd0", [128, D_EXPERT // 128, D], F32) as wd0:
            slot0_loaded = [nc.alloc_semaphore(f"{name}_in0") for name in ("w_gate", "w_up", "w_down")]
            merge(nc, t, expert, gates, (wgu0, wd0), slot0_loaded)
            experts(nc, t, expert, gates, (wgu0, wd0), slot0_loaded)


SCRATCH = {
    "mods": ((1 + NSEQ, ADA), F32),
    "cm_p": ((NCM * 128, SEQ + 1), F32),
    "cm_s": ((NCM * 128, DEC_W), F32),
    "tm": ((T, 1024), F32),
    "h_last": ((PT + 4, D), F32),
    "mix": ((T, D), F32),
    "x1": ((T, D), F32),
    "h2": ((T, D), F32),
    "y_rows": (((MAX_BLOCKS + 1) * BLOCK, D), F32),
}
OUTPUTS = [
    ("y_prompt", (1, SEQ, D)), ("y_sample", (NSEQ, DEC, D)),
    ("new_hgrn_p", (1, 1, HG_HEADS, 128, 128)), ("new_rwkv_p", (1, 1, RW_HEADS, RW_N, RW_N)), ("shift_p", (1, 1, D)),
    ("new_hgrn_s", (1, NSEQ, HG_HEADS, 128, 128)), ("new_rwkv_s", (1, NSEQ, RW_HEADS, RW_N, RW_N)), ("shift_s", (1, NSEQ, D)),
]
INPUTS = [
    "x_prompt", "x_sample", "state_hgrn", "state_rwkv", "state_shift", "c_prompt", "c_sample", "w_ada", "b_ada",
    "norm_mix_w", "norm_ffn_w", "w_in", "w_out", "hg_norm_w", "rw_mu_proj", "rw_mu_lora", "rw_w0", "rw_w1", "rw_w2",
    "rw_a0", "rw_a1", "rw_a2", "rw_g1", "rw_g2", "rw_kk", "rw_ka", "rw_rk", "rw_ln_w", "rw_ln_b", "router_g_w",
    "router_g_b", "router_e_w", "router_e_b", "w_gate", "w_up", "w_down", "final_norm_w",
]


def shape_constants():
    tok = np.arange(128)[:, None] + 128 * np.arange(NT)[None, :]
    return {
        "const": constants(),
        "reset": resets(),
        "iota": np.broadcast_to(np.arange(128, dtype=np.float32), (128, 128)).copy(),
        "token_ids": np.repeat(tok, TOP_K, axis=1).astype(np.float32),
    }


def kernel(**inputs):
    import concourse.bacc as bacc
    from concourse.bass_utils import run_bass_kernel_spmd

    nc = bacc.Bacc("TRN2", target_bir_lowering=False, num_devices=1)
    arrays, t = {}, {}
    given = {name: np.ascontiguousarray(inputs[name]) for name in INPUTS}
    given.update(shape_constants())
    for name, a in given.items():
        arrays[f"in_{name}"] = a
        t[name] = nc.dram_tensor(f"in_{name}", a.shape, mybir.dt.from_np(a.dtype), kind="ExternalInput").ap()
    for name, (shape, dt) in SCRATCH.items():
        t[name] = nc.dram_tensor(f"scratch_{name}", shape, dt, kind="Internal").ap()
    for name, shape in OUTPUTS:
        t[name] = nc.dram_tensor(f"out_{name}", shape, F32, kind="ExternalOutput").ap()
    program(nc, t)
    r = run_bass_kernel_spmd(nc, [arrays], core_ids=[0])
    return tuple(r.results[0][f"out_{name}"] for name, _ in OUTPUTS)
```
